# Optimizing a Trainium2 kernel written in Bass

```python
import math
import jax, jax.numpy as jnp
from jax import lax
import numpy as np

D_MODEL = 1024
BATCH = 1
SEQ = 256
DEPTH = 1

NSA_HEADS = 8
NSA_KV_GROUPS = 2
NSA_REP = NSA_HEADS // NSA_KV_GROUPS
NSA_DH = 64
CMP_LEN = 32
CMP_STRIDE = 16
CMP_HIDDEN = 256
SLC_BLOCK = 64
SLC_TOP_N = 16
WINDOW = 512
NSA_Q_CHUNK = 64

MLA_HEADS = 8
MLA_Q_RANK = 256
MLA_KV_RANK = 128
MLA_NOPE = 64
MLA_ROPE = 32
MLA_V = 64
MLA_Q_BLOCK = 128
ROPE_THETA = 10000.0

T5_BUCKETS = 32
T5_MAX_DIST = 128

PEER_HEADS = 8
PEER_N_KEYS = 128
PEER_N_EXPERTS = PEER_N_KEYS * PEER_N_KEYS
PEER_KEY_DIM = 128
PEER_TOPK = 16
PEER_TOKEN_CHUNK = 128

NORM_EPS = 1e-6
MASK_VALUE = -1e30
FORCE_BONUS = 1e4

NSA_Q_COLS = NSA_HEADS * NSA_DH
NSA_KV_COLS = 6 * NSA_KV_GROUPS * NSA_DH
NSA_GATE_COLS = 3 * NSA_HEADS
MERGE_GATE_COLS = 2 * D_MODEL
IN_SPLITS = (NSA_Q_COLS, NSA_KV_COLS, NSA_GATE_COLS, MLA_Q_RANK, MLA_KV_RANK, MLA_ROPE, MERGE_GATE_COLS)
IN_COLS = sum(IN_SPLITS)

kernel_name = "hybrid_nsa_mla_peer_layer"

def rmsnorm(x, g):
    xf = x.astype(jnp.float32)
    y = xf * lax.rsqrt(jnp.mean(xf * xf, axis=-1, keepdims=True) + NORM_EPS)
    return y.astype(x.dtype) * g

def masked_softmax(logits, mask, axis):
    logits = jnp.where(mask, logits.astype(jnp.float32), MASK_VALUE)
    m = jnp.max(logits, axis=axis, keepdims=True)
    e = jnp.exp(logits - m) * mask
    return e / jnp.maximum(jnp.sum(e, axis=axis, keepdims=True), 1e-30)

def t5_bucket(n):
    n = jnp.maximum(n, 0)
    max_exact = T5_BUCKETS // 2
    ratio = jnp.maximum(n, max_exact).astype(jnp.float32) / max_exact
    large = max_exact + (jnp.log(ratio) / math.log(T5_MAX_DIST / max_exact)
                         * (T5_BUCKETS - max_exact)).astype(jnp.int32)
    large = jnp.minimum(large, T5_BUCKETS - 1)
    return jnp.where(n < max_exact, n, large)

def split_cols(a, sizes):
    offsets = np.cumsum(np.array(sizes))[:-1].tolist()
    return jnp.split(a, offsets, axis=-1)

def apply_rope(x, cos, sin):
    half = x.shape[-1] // 2
    x1, x2 = x[..., :half], x[..., half:]
    return jnp.concatenate([x1 * cos - x2 * sin, x2 * cos + x1 * sin], axis=-1)

def nsa_mixer(q, kv, gate_logits, t5_bias, cmp_pos_k, cmp_pos_v,
              cmp_k_w1, cmp_k_w2, cmp_v_w1, cmp_v_w2):
    B, S, _ = q.shape
    G, R, Dh = NSA_KV_GROUPS, NSA_REP, NSA_DH
    scale = Dh ** -0.5
    q = q.reshape(B, S, G, R, Dh)
    kv = kv.reshape(B, S, 6, G, Dh)
    k_cr, v_cr, k_slc, v_slc, k_win, v_win = [kv[:, :, i] for i in range(6)]
    t5_gr = t5_bias.reshape(T5_BUCKETS, G, R)
    pos = jnp.arange(S, dtype=jnp.int32)

    NC = (S - CMP_LEN) // CMP_STRIDE + 1
    cmp_start = jnp.arange(NC, dtype=jnp.int32) * CMP_STRIDE
    cmp_tok = cmp_start[:, None] + jnp.arange(CMP_LEN, dtype=jnp.int32)[None, :]

    def compress(src, pos_emb, w1, w2):
        blk = src[:, cmp_tok] + pos_emb[None, None, :, None, :]
        blk = blk.transpose(0, 1, 3, 2, 4).reshape(B, NC, G, CMP_LEN * Dh)
        return jax.nn.gelu(blk @ w1, approximate=False) @ w2

    k_c = compress(k_cr, cmp_pos_k, cmp_k_w1, cmp_k_w2)
    v_c = compress(v_cr, cmp_pos_v, cmp_v_w1, cmp_v_w2)
    cmp_end = cmp_start + CMP_LEN - 1
    dist_c = pos[:, None] - cmp_end[None, :]
    mask_c = dist_c >= 0
    bias_c = t5_gr[t5_bucket(dist_c)].transpose(2, 3, 0, 1)
    logit_c = jnp.einsum('bsgrd,bcgd->bgrsc', q, k_c).astype(jnp.float32) * scale + bias_c
    p_c = masked_softmax(logit_c, mask_c, -1)
    o_cmp = jnp.einsum('bgrsc,bcgd->bsgrd', p_c.astype(v_c.dtype), v_c)

    NB = S // SLC_BLOCK
    blk_start = jnp.arange(NB, dtype=jnp.int32) * SLC_BLOCK
    overlap = ((cmp_start[:, None] < blk_start[None, :] + SLC_BLOCK)
               & (cmp_start[:, None] + CMP_LEN > blk_start[None, :])).astype(jnp.float32)
    imp = jnp.einsum('bgrsc,cn->bgsn', p_c, overlap)
    cur = pos // SLC_BLOCK
    j = jnp.arange(NB, dtype=jnp.int32)
    forced = (j[None, :] == 0) | (j[None, :] == cur[:, None]) | (j[None, :] == cur[:, None] - 1)
    future = blk_start[None, :] > pos[:, None]
    score = jnp.where(future, -1.0, jnp.where(forced, FORCE_BONUS, imp))
    top_n = min(SLC_TOP_N, NB)
    _, sel_idx = lax.top_k(score, top_n)

    k_sb = k_slc.reshape(B, NB, SLC_BLOCK, G, Dh).transpose(0, 3, 1, 2, 4)
    v_sb = v_slc.reshape(B, NB, SLC_BLOCK, G, Dh).transpose(0, 3, 1, 2, 4)
    k_wp = jnp.pad(k_win, ((0, 0), (WINDOW, 0), (0, 0), (0, 0)))
    v_wp = jnp.pad(v_win, ((0, 0), (WINDOW, 0), (0, 0), (0, 0)))

    C = NSA_Q_CHUNK
    NQ = S // C
    q_ch = q.reshape(B, NQ, C, G, R, Dh).transpose(1, 0, 2, 3, 4, 5)
    idx_ch = sel_idx.reshape(B, G, NQ, C, top_n).transpose(2, 0, 1, 3, 4)
    b_ix = jnp.arange(B)[:, None, None, None]
    g_ix = jnp.arange(G)[None, :, None, None]
    g_ix5 = jnp.arange(G)[None, :, None, None, None]

    def chunk_fn(args):
        c, qc, idx = args
        t = c * C + jnp.arange(C, dtype=jnp.int32)
        ks = k_sb[b_ix, g_ix, idx]
        vs = v_sb[b_ix, g_ix, idx]
        kpos = idx[..., None] * SLC_BLOCK + jnp.arange(SLC_BLOCK, dtype=jnp.int32)
        d_s = t[None, None, :, None, None] - kpos
        bias_s = jnp.moveaxis(t5_gr[t5_bucket(d_s), g_ix5], -1, 2)
        logit_s = jnp.einsum('bcgrd,bgcnkd->bgrcnk', qc, ks).astype(jnp.float32) * scale + bias_s
        p_s = masked_softmax(logit_s, (d_s >= 0)[:, :, None], (-2, -1))
        o_s = jnp.einsum('bgrcnk,bgcnkd->bcgrd', p_s.astype(vs.dtype), vs)
        kw = lax.dynamic_slice_in_dim(k_wp, c * C, WINDOW + C, axis=1)
        vw = lax.dynamic_slice_in_dim(v_wp, c * C, WINDOW + C, axis=1)
        wpos = c * C - WINDOW + jnp.arange(WINDOW + C, dtype=jnp.int32)
        d_w = t[:, None] - wpos[None, :]
        mask_w = (d_w >= 0) & (d_w < WINDOW) & (wpos[None, :] >= 0)
        bias_w = t5_gr[t5_bucket(d_w)].transpose(2, 3, 0, 1)
        logit_w = jnp.einsum('bcgrd,bkgd->bgrck', qc, kw).astype(jnp.float32) * scale + bias_w
        p_w = masked_softmax(logit_w, mask_w, -1)
        o_w = jnp.einsum('bgrck,bkgd->bcgrd', p_w.astype(vw.dtype), vw)
        return o_s, o_w

    o_slc, o_win = lax.map(chunk_fn, (jnp.arange(NQ, dtype=jnp.int32), q_ch, idx_ch))
    o_slc = o_slc.transpose(1, 0, 2, 3, 4, 5).reshape(B, S, G, R, Dh)
    o_win = o_win.transpose(1, 0, 2, 3, 4, 5).reshape(B, S, G, R, Dh)

    gate = jax.nn.sigmoid(gate_logits.astype(jnp.float32)).astype(q.dtype).reshape(B, S, G, R, 3)
    o = gate[..., 0:1] * o_cmp + gate[..., 1:2] * o_slc + gate[..., 2:3] * o_win
    return o.reshape(B, S, NSA_HEADS * Dh)

def mla_mixer(c_q_raw, c_kv_raw, k_rope_raw, q_norm_g, kv_norm_g, w_uq, w_ukv):
    B, S, _ = c_q_raw.shape
    H = MLA_HEADS
    q = (rmsnorm(c_q_raw, q_norm_g) @ w_uq).reshape(B, S, H, MLA_NOPE + MLA_ROPE)
    q_nope, q_rope = q[..., :MLA_NOPE], q[..., MLA_NOPE:]
    kv = (rmsnorm(c_kv_raw, kv_norm_g) @ w_ukv).reshape(B, S, H, MLA_NOPE + MLA_V)
    k_nope, v = kv[..., :MLA_NOPE], kv[..., MLA_NOPE:]

    inv_freq = ROPE_THETA ** (-jnp.arange(0, MLA_ROPE, 2, dtype=jnp.float32) / MLA_ROPE)
    ang = jnp.arange(S, dtype=jnp.float32)[:, None] * inv_freq[None, :]
    cos, sin = jnp.cos(ang).astype(q.dtype), jnp.sin(ang).astype(q.dtype)
    q_rope = apply_rope(q_rope, cos[None, :, None, :], sin[None, :, None, :])
    k_rope = apply_rope(k_rope_raw, cos[None], sin[None])

    scale = (MLA_NOPE + MLA_ROPE) ** -0.5
    QB = MLA_Q_BLOCK
    NQ = S // QB
    qn_b = q_nope.reshape(B, NQ, QB, H, MLA_NOPE).transpose(1, 0, 2, 3, 4)
    qr_b = q_rope.reshape(B, NQ, QB, H, MLA_ROPE).transpose(1, 0, 2, 3, 4)
    kpos = jnp.arange(S, dtype=jnp.int32)

    def block_fn(args):
        c, qn, qr = args
        t = c * QB + jnp.arange(QB, dtype=jnp.int32)
        logits = (jnp.einsum('bqhd,bkhd->bhqk', qn, k_nope)
                  + jnp.einsum('bqhd,bkd->bhqk', qr, k_rope)).astype(jnp.float32) * scale
        p = masked_softmax(logits, kpos[None, :] <= t[:, None], -1)
        return jnp.einsum('bhqk,bkhd->bqhd', p.astype(v.dtype), v)

    o = lax.map(block_fn, (jnp.arange(NQ, dtype=jnp.int32), qn_b, qr_b))
    return o.transpose(1, 0, 2, 3, 4).reshape(B, S, H * MLA_V)

def peer_ffn(xn, w_query, sub_keys, u, v):
    B, S, D = xn.shape
    T = B * S
    H, K = PEER_HEADS, PEER_TOPK
    xt = xn.reshape(T, D)
    q = (xt @ w_query).reshape(T, H, 2, PEER_KEY_DIM // 2)
    s = jnp.einsum('thpd,hpkd->thpk', q, sub_keys).astype(jnp.float32)
    s_top, i_top = lax.top_k(s, K)
    cand = s_top[:, :, 0, :, None] + s_top[:, :, 1, None, :]
    cand_idx = i_top[:, :, 0, :, None] * PEER_N_KEYS + i_top[:, :, 1, None, :]
    best, pick = lax.top_k(cand.reshape(T, H, K * K), K)
    expert = jnp.take_along_axis(cand_idx.reshape(T, H, K * K), pick, axis=-1)
    g = jax.nn.softmax(best, axis=-1)

    C = PEER_TOKEN_CHUNK
    NT = T // C

    def chunk_fn(args):
        xc, ec, gc = args
        ue = u[ec]
        ve = v[ec]
        a = jax.nn.gelu(jnp.einsum('chkd,cd->chk', ue, xc).astype(jnp.float32), approximate=False)
        return jnp.einsum('chk,chkd->cd', (gc * a).astype(ve.dtype), ve)

    y = lax.map(chunk_fn, (xt.reshape(NT, C, D), expert.reshape(NT, C, H, K), g.reshape(NT, C, H, K)))
    return y.reshape(B, S, D)

def setup_inputs(seed: int = 0) -> dict:
    key = jax.random.key(seed)
    ks = jax.random.split(key, 23)
    L = DEPTH

    def nrm(k, shape, scale):
        return jax.random.normal(k, shape, jnp.float32) * scale

    def gain(k, shape):
        return 1.0 + 0.01 * jax.random.normal(k, shape, jnp.float32)

    return {
        "x": nrm(ks[0], (BATCH, SEQ, D_MODEL), 1.0),
        "ln_mix_g": gain(ks[1], (L, D_MODEL)),
        "w_in": nrm(ks[2], (L, D_MODEL, IN_COLS), D_MODEL ** -0.5),
        "nsa_cmp_pos_k": nrm(ks[3], (L, CMP_LEN, NSA_DH), 0.1),
        "nsa_cmp_pos_v": nrm(ks[4], (L, CMP_LEN, NSA_DH), 0.1),
        "nsa_cmp_k_w1": nrm(ks[5], (L, CMP_LEN * NSA_DH, CMP_HIDDEN), (CMP_LEN * NSA_DH) ** -0.5),
        "nsa_cmp_k_w2": nrm(ks[6], (L, CMP_HIDDEN, NSA_DH), CMP_HIDDEN ** -0.5),
        "nsa_cmp_v_w1": nrm(ks[7], (L, CMP_LEN * NSA_DH, CMP_HIDDEN), (CMP_LEN * NSA_DH) ** -0.5),
        "nsa_cmp_v_w2": nrm(ks[8], (L, CMP_HIDDEN, NSA_DH), CMP_HIDDEN ** -0.5),
        "mla_q_norm_g": gain(ks[9], (L, MLA_Q_RANK)),
        "mla_kv_norm_g": gain(ks[10], (L, MLA_KV_RANK)),
        "mla_w_uq": nrm(ks[11], (L, MLA_Q_RANK, MLA_HEADS * (MLA_NOPE + MLA_ROPE)), MLA_Q_RANK ** -0.5),
        "mla_w_ukv": nrm(ks[12], (L, MLA_KV_RANK, MLA_HEADS * (MLA_NOPE + MLA_V)), MLA_KV_RANK ** -0.5),
        "w_branch_nsa": nrm(ks[13], (L, NSA_HEADS * NSA_DH, D_MODEL), (NSA_HEADS * NSA_DH) ** -0.5),
        "w_branch_mla": nrm(ks[14], (L, MLA_HEADS * MLA_V, D_MODEL), (MLA_HEADS * MLA_V) ** -0.5),
        "w_out": nrm(ks[15], (L, D_MODEL, D_MODEL), D_MODEL ** -0.5),
        "ln_ffn_g": gain(ks[16], (L, D_MODEL)),
        "peer_w_query": nrm(ks[17], (L, D_MODEL, PEER_HEADS * PEER_KEY_DIM), D_MODEL ** -0.5),
        "peer_sub_keys": nrm(ks[18], (L, PEER_HEADS, 2, PEER_N_KEYS, PEER_KEY_DIM // 2), (PEER_KEY_DIM // 2) ** -0.5),
        "peer_u": nrm(ks[19], (L, PEER_N_EXPERTS, D_MODEL), D_MODEL ** -0.5),
        "peer_v": nrm(ks[20], (L, PEER_N_EXPERTS, D_MODEL), 0.5),
        "t5_bias": nrm(ks[21], (T5_BUCKETS, NSA_HEADS), 0.2),
        "ln_final_g": gain(ks[22], (D_MODEL,)),
    }

def reference(x, ln_mix_g, w_in, nsa_cmp_pos_k, nsa_cmp_pos_v, nsa_cmp_k_w1, nsa_cmp_k_w2,
              nsa_cmp_v_w1, nsa_cmp_v_w2, mla_q_norm_g, mla_kv_norm_g, mla_w_uq, mla_w_ukv,
              w_branch_nsa, w_branch_mla, w_out, ln_ffn_g, peer_w_query, peer_sub_keys,
              peer_u, peer_v, t5_bias, ln_final_g):
    B, S, D = x.shape
    h = x
    for l in range(DEPTH):
        xn = rmsnorm(h, ln_mix_g[l])
        proj = xn @ w_in[l]
        nsa_q, nsa_kv, nsa_gate, c_q, c_kv, k_rope, merge_gate = split_cols(proj, IN_SPLITS)
        o_nsa = nsa_mixer(nsa_q, nsa_kv, nsa_gate, t5_bias, nsa_cmp_pos_k[l], nsa_cmp_pos_v[l],
                          nsa_cmp_k_w1[l], nsa_cmp_k_w2[l], nsa_cmp_v_w1[l], nsa_cmp_v_w2[l])
        o_mla = mla_mixer(c_q, c_kv, k_rope, mla_q_norm_g[l], mla_kv_norm_g[l],
                          mla_w_uq[l], mla_w_ukv[l])
        gates = jax.nn.sigmoid(merge_gate.astype(jnp.float32)).astype(x.dtype).reshape(B, S, 2, D)
        merged = gates[:, :, 0] * (o_nsa @ w_branch_nsa[l]) + gates[:, :, 1] * (o_mla @ w_branch_mla[l])
        h = h + merged @ w_out[l]
        hn = rmsnorm(h, ln_ffn_g[l])
        h = h + peer_ffn(hn, peer_w_query[l], peer_sub_keys[l], peer_u[l], peer_v[l])
    return rmsnorm(h, ln_final_g)


_drawn_inputs = setup_inputs


def setup_inputs(seed=0):
    import zlib

    import numpy as np

    out = dict(_drawn_inputs(seed))
    spreads = {}
    factors = {'ln_mix_g': 3.683,
     'nsa_cmp_pos_k': 4.527,
     'mla_q_norm_g': 8.0,
     'mla_kv_norm_g': 4.889,
     'ln_final_g': 31.934,
     'nsa_cmp_pos_v': 6.392,
     'ln_ffn_g': 7.728}
    for name, (base, spread) in spreads.items():
        noise = np.random.default_rng([zlib.crc32(name.encode()), seed]).standard_normal(out[name].shape)
        drawn = base * np.exp(spread * noise) if base else spread * noise
        out[name] = __import__('jax').numpy.asarray(drawn.astype(out[name].dtype))
    for name, factor in factors.items():
        out[name] = (out[name] * factor).astype(out[name].dtype)
    return out
```

```python
import math
from contextlib import ExitStack

import numpy as np
import concourse.bass as bass
from concourse import mybir

P = 128
T = 256
NT = T // P
D = 1024
KT = D // P
H = 8
G = 2
R = H // G
DH = 64
CMP_LEN, CMP_STRIDE, CMP_HID = 32, 16, 256
NC = (T - CMP_LEN) // CMP_STRIDE + 1
NC0 = (P - CMP_LEN) // CMP_STRIDE + 1
LP = CMP_LEN // 2
Q_RANK, KV_RANK, NOPE, ROPE = 256, 128, 64, 32
QK = NOPE + ROPE
BUCKETS, MAX_DIST = 32, 128
NK = 128
TOPK = 16
EPS = 1e-6
MASKED = -1e30
Q_COLS = H * DH
REST = 3 * H + Q_RANK + KV_RANK + ROPE
K0 = Q_COLS
V0 = K0 + 2 * P
REST0 = V0 + 2 * P
CK0 = REST0 + REST
CV0 = CK0 + 2 * P
MERGE0 = CV0 + 2 * P
PART_A = CV0
CQ0, CKV0, KR0 = 3 * H, 3 * H + Q_RANK, 3 * H + Q_RANK + KV_RANK
DIST = T + P - 1
RING = 4
TB = 8
STEPS = NK // 2 // 2


def build(nc, x, g_mix, g_ffn, g_fin, w_in, pos, w1k, w1v, w2k, w2v, q_gain, kv_gain, w_uq, w_ukv,
          w_bn, w_bm, w_out, w_query, keys_t, u_t, v_t, t5, ident, one_hot, masked_row, cos, sin,
          causal, cmp_mask, head_mask, iota, iota16, out):
    fp32, u32 = mybir.dt.float32, mybir.dt.uint32
    ACT, ALU, AX = mybir.ActivationFunctionType, mybir.AluOpType, mybir.AxisListType
    ds = bass.ds

    ctx = ExitStack()
    with ctx:
        def sb(name, shape, dt=fp32):
            return ctx.enter_context(nc.sbuf_tensor(name, shape, dt))

        def sem(name):
            return ctx.enter_context(nc.semaphore(name))

        def strided(base, dims):
            return bass.AP(base.tensor, base.offset, [base.ap[0], *dims])

        def bcast(ap, n):
            return ap.unsqueeze(len(ap.shape)).to_broadcast([*ap.shape, n])

        def spread(ap, n):
            return ap.unsqueeze(1).to_broadcast([ap.shape[0], n, *ap.shape[1:]])

        big = sb("big", [P, NK * T])
        ring = sb("ring", [P, RING * 2 * D])
        xnT = sb("xnT", [P, KT * T])
        h = sb("h", [P, NT * D])
        work = sb("work", [P, 6100])
        at = [0]

        def part(base, offset, *dims):
            n = int(np.prod(dims))
            v_ = base[:, offset:offset + n]
            if len(dims) == 2:
                return v_.rearrange("p (a b) -> p a b", b=dims[1])
            if len(dims) == 3:
                return v_.rearrange("p (a b c) -> p a b c", b=dims[1], c=dims[2])
            return v_

        def w_(*dims):
            at[0] += int(np.prod(dims))
            return part(work, at[0] - int(np.prod(dims)), *dims)

        win = part(big, 0, KT, PART_A)
        wb = part(big, 0, 2, 4, D)
        mgT = part(big, 8192, 2 * KT, T)
        qn = part(big, 12288, NT, H * QK)
        MG = 13824
        mslot = [part(big, MG + s * 2048, KT, 256) for s in range(2)]
        biasM = part(big, 17920, H, T)
        onat = [part(big, 19968 + s * 1024, NT, H * DH) for s in range(2)]
        wuq = part(big, 22016, 2, H * QK)
        wukv = part(big, 22016 + 1536, H * 2 * DH)
        mqT = part(big, 24576, H, T)
        xs = part(big, 24576, NT, D)
        mergedT = part(big, 24576, KT, T)
        mkT = part(big, 26624, H, T)
        Vm = part(big, 28672, NT, H * DH)
        oT = part(big, 29696, 2 * 4, T)
        wcv = part(big, 29696, KT, 2 * P)
        blkT = part(big, 31744, 2, LP, G * NC)
        tmp = part(big, 31744, H * DH)
        w1 = part(ring[:, :], 0, 2, LP, CMP_HID)
        wo = part(ring[:, :], 0, KT, D)
        wq = part(big, MG, KT, D)
        keysT = part(big, 12288, H, NK)
        qpT = part(big, 8192, H, T)
        S = part(big, 24576, NT, 2 * H, NK)
        cand = part(big, 28672, H, TOPK * TOPK)
        eq = part(big, 30720, H * TOPK, TOPK)
        topv = part(big, 22016, 2 * H, TOPK)
        topi_f = part(big, 22272, 2 * H, TOPK)
        topi = part(big, 22528, 2 * H, TOPK).bitcast(u32)
        best = part(big, 22784, H, TOPK)
        pick = part(big, 22912, H, TOPK).bitcast(u32)
        pick_a = part(big, 23040, H * TOPK).bitcast(u32)
        pick_b = part(big, 23168, H * TOPK).bitcast(u32)
        pa_f = part(big, 23296, H * TOPK)
        pb_f = part(big, 23424, H * TOPK)
        gsum = part(big, 23552, H)
        yT = part(big, 0, KT, T)
        ynat = part(big, 2048, NT, D)
        sq_fin = part(big, 4096, D)
        gfin = part(big, 8192, D)
        xnT3 = part(xnT, 0, KT, T)
        h3 = part(h, 0, NT, D)

        identS = w_(P)
        iotaS = w_(NK)
        iota16S = w_(TOPK)
        gmix, gffn = w_(KT), w_(KT)
        epsS = w_(4)
        ssq, rstd = w_(8), w_(8)
        scratch_at = at[0]
        qT = w_(R, T)
        kT = w_(2, T)
        Vn = w_(NT, 2 * P)
        rest = w_(NT, REST)
        E = w_(2, 2, T)
        cT = part(work, at[0] - 2 * 2 * T, 3, T)
        hTk, hTv = w_(2, G * NC), w_(2, H * NC)
        kcT = w_(NC)
        vcs = w_(DH)
        Ec = w_(2, H * NC)
        posS = w_(2, LP)
        qgS, kvgS = w_(2), w_(1)
        w2kS, w2vS = w_(2, P), w_(2, DH)
        cosS, sinS = w_(NT, ROPE // 2), w_(NT, ROPE // 2)
        cmaskS = w_(NT, NC)
        hmaskS = w_(H)
        nmx = w_(24, 2)
        csum = w_(NT, H)
        sums = w_(6, H)
        sc = w_(8, H)
        ebuf = sb("ebuf", [P, 1024])
        eT = [part(ebuf, s * 512, 512) for s in range(2)]
        kpad = part(ebuf, 0, NT, QK)
        sq = sb("sq", [P, 512])
        VB = part(sq, 0, H * DH)
        rot = [part(sq, n * P, H, ROPE // 2) for n in range(4)]
        causalS = sb("causalS", [P, T])
        t5S = sb("t5S", [BUCKETS + 1, H])
        ohS = part(xnT, 0, DIST)[0:BUCKETS + 1, :]
        revS = part(xnT, 512, DIST)[0:H, :]
        assert at[0] <= 6100, at[0]
        A = [part(work, scratch_at + s * TB * NK, TB, NK) for s in range(2)]
        B = [part(work, scratch_at + 2 * TB * NK + s * TB * 64, TB, 64) for s in range(2)]
        picks = [part(work, scratch_at + 3072 + s * T, NT, P) for s in range(3)]
        i1T, i2T, gT = (part(work, scratch_at + 3840 + s * T, T) for s in range(3))

        rev_dram = nc.dram_tensor("bias_by_distance", [H, P, DIST], fp32, kind="Internal")

        ps = [ctx.enter_context(nc.psum_tensor(f"ps{n}", [P, 512], fp32)) for n in range(8)]

        x_in, const_in, t5_in, bias_in, rev_out = (sem(n) for n in ("x_in", "const_in", "t5_in", "bias_in", "rev_out"))
        win_in = [sem(f"win_in{n}") for n in range(4)]
        merge_in = [sem(f"merge_in{n}") for n in range(2)]
        w1_in, w2_in, wu_in, wb_in, wo_in, wq_in, keys_in = (
            sem(n) for n in ("w1_in", "w2_in", "wu_in", "wb_in", "wo_in", "wq_in", "keys_in"))
        ring_in = [sem(f"ring_in{n}") for n in range(RING)]
        out_done, gfin_in = sem("out_done"), sem("gfin_in")
        dve_chain, act_chain = sem("dve_chain"), sem("act_chain")
        rev_ps, rev_sb = sem("rev_ps"), sem("rev_sb")
        ssq_ready, ms_ready, root_ready, xs_ready = (sem(n) for n in ("ssq_ready", "ms_ready", "root_ready", "xs_ready"))
        xT_ps, xnT_act, xnT_dve = sem("xT_ps"), sem("xnT_act"), sem("xnT_dve")
        job_done, job_act, job_dve = sem("job_done"), sem("job_act"), sem("job_dve")
        c_ssq, c_ms, c_root, cn_ready, kr_ready, rope_ready = (
            sem(n) for n in ("c_ssq", "c_ms", "c_root", "cn_ready", "kr_ready", "rope_ready"))
        hid_ps, hid_ready, kc_ps, kc_ready, vb_ready = (sem(n) for n in ("hid_ps", "hid_ready", "kc_ps", "kc_ready", "vb_ready"))
        L_done, L_free, max_ready, E_ready = (sem(n) for n in ("L_done", "L_free", "max_ready", "E_ready"))
        cmp_sub, cmp_exp, cmp_ready = sem("cmp_sub"), sem("cmp_exp"), sem("cmp_ready")
        T_done, eT_ready, V_done, O_done, O_free = (sem(n) for n in ("T_done", "eT_ready", "V_done", "O_done", "O_free"))
        b_marked = sem("b_marked")
        half_logits = sem("half_logits")
        gate_ready = sem("gate_ready")
        oT_ps, oT_ready = sem("oT_ps"), sem("oT_ready")
        br_done, br_free, merged_ready = sem("br_done"), sem("br_free"), sem("merged_ready")
        h_ps, h_ready = sem("h_ps"), sem("h_ready")
        qp_done, qp_ready, s_done, s_ready = (sem(n) for n in ("qp_done", "qp_ready", "s_done", "s_ready"))
        best_sub, best_exp, picks_ready, pT_done, pT_ready = (
            sem(n) for n in ("best_sub", "best_exp", "picks_ready", "pT_done", "pT_ready"))
        u_done, gelu_done, ab_ready, g_done, w_done, v_done = (
            sem(n) for n in ("u_done", "gelu_done", "ab_ready", "g_done", "w_done", "v_done"))
        y_act, y_dve, yn_done, f_ssq, f_ms, f_root, out_ready = (
            sem(n) for n in ("y_act", "y_dve", "yn_done", "f_ssq", "f_ms", "f_root", "out_ready"))

        CONSTS = 15
        (J_Q0, J_Q1, J_K, J_R0, J_R1, J_CK, J_CV, J_V, J_C, J_CR, J_KN) = range(11)
        J_VM = J_KN + 4
        J_QN = J_VM + 2
        J_QT = J_QN + 4
        J_MG = J_QT + 4
        JOBS = J_MG + 8
        DVE_JOBS = (J_CK, J_CV)
        UNITS = 2 + 3 * NT * H // 2

        def unit(n):
            m = n - 2
            return m // 8, m // 4 % 2, m % 4

        def group(n):
            return n if n < 2 else 2 + (n - 2) // 4

        def act_jobs_before(n):
            return sum(j not in DVE_JOBS for j in range(n))

        def dve_jobs_before(n):
            return sum(j in DVE_JOBS for j in range(n))

        def wait_job_evacuated(eng, n):
            if n in DVE_JOBS:
                eng.wait_ge(job_dve, dve_jobs_before(n) + 1)
            else:
                eng.wait_ge(job_act, act_jobs_before(n) + 1)

        def fill_jobs(n):
            if n < 4:
                return [J_QT + n]
            return [J_MG + n - 4] if n < 12 else []

        block = ctx.enter_context(nc.Block())

        @block.sync
        def _(sp):
            w_in_t = w_in.rearrange("(k p) c -> p k c", p=P)
            sp.dma_start(h3, x.rearrange("(i p) d -> p i d", p=P)).then_inc(x_in, 16)
            for n, (a, b) in enumerate(((0, K0), (K0, REST0), (REST0, PART_A))):
                sp.dma_start(win[:, :, a:b], w_in_t[:, :, a:b]).then_inc(win_in[n], 16)
            sp.dma_start(wcv, w_in_t[:, :, CV0:MERGE0]).then_inc(win_in[3], 16)
            sp.dma_start(w1[:, 0], w1k.rearrange("(k p) c -> p k c", p=P)).then_inc(w1_in, 16)
            sp.dma_start(w1[:, 1], w1v.rearrange("(k p) c -> p k c", p=P)).then_inc(w1_in, 16)
            sp.dma_start(wuq, w_uq.rearrange("(k p) c -> p k c", p=P)).then_inc(wu_in, 16)
            sp.dma_start(wukv, w_ukv).then_inc(wu_in, 16)

            def merge_chunk(c):
                if c >= 2:
                    sp.wait_ge(job_done, J_MG + c - 2 + 1)
                lo = MERGE0 + c * 256
                sp.dma_start(mslot[c % 2], w_in_t[:, :, lo:lo + 256]).then_inc(merge_in[c % 2], 16)

            merge_chunk(0)
            merge_chunk(1)
            sp.wait_ge(job_done, J_V + 1)
            sp.dma_start(wb[:, 0], w_bn.rearrange("(k p) c -> p k c", p=P)).then_inc(wb_in, 16)
            sp.dma_start(wb[:, 1], w_bm.rearrange("(k p) c -> p k c", p=P)).then_inc(wb_in, 16)
            sp.wait_ge(hid_ps, 1)
            sp.dma_start(wo, w_out.rearrange("(k p) c -> p k c", p=P)).then_inc(wo_in, 16)
            for c in range(2, 8):
                merge_chunk(c)
            sp.wait_ge(job_done, JOBS)
            sp.dma_start(keysT, keys_t).then_inc(keys_in, 16)
            sp.wait_ge(oT_ps, 4)
            sp.dma_start(wq, w_query.rearrange("(k p) c -> p k c", p=P)).then_inc(wq_in, 16)
            sp.wait_ge(h_ps, 4)

            def load_u(s, n):
                sp.dma_start(part(ring[:, :], s * 2 * D, 2, D),
                             u_t[ds(n * 2, 2)].rearrange("n p c -> p n c")).then_inc(ring_in[s], 16)

            def load_v(s, n):
                sp.dma_start(part(ring[:, :], s * 2 * D, 2, D),
                             v_t[ds(n * 2, 2)].rearrange("n p c -> p n c")).then_inc(ring_in[s], 16)

            for s in range(RING):
                load_u(s, s)
            with sp.Fori(1, 2 * STEPS // RING) as it:
                for s in range(RING):
                    sp.wait_ge(u_done, (it * RING + s - RING + 1) * 2)
                    load_u(s, it * RING + s)
            for s in range(RING):
                sp.wait_ge(u_done, (2 * STEPS - RING + s + 1) * 2)
                load_v(s, s)
            with sp.Fori(1, 2 * STEPS // RING) as it:
                for s in range(RING):
                    sp.wait_ge(v_done, it * RING + s - RING + 1)
                    load_v(s, it * RING + s)
            for i in range(NT):
                sp.wait_ge(out_ready, i + 1)
                sp.dma_start(out[i * P:(i + 1) * P, :], ynat[:, i]).then_inc(out_done, 16)
            sp.wait_ge(out_done, NT * 16)

        @block.gpsimd
        def _(pool):
            pool.dma_start(t5S[0:BUCKETS, :], t5).then_inc(t5_in, 16)
            pool.dma_start(t5S[BUCKETS:BUCKETS + 1, :], masked_row).then_inc(t5_in, 16)
            pool.dma_start(ohS, one_hot).then_inc(t5_in, 16)
            pool.wait_ge(rev_sb, 1)
            pool.dma_start(rev_dram.ap(), spread(revS, P)).then_inc(rev_out, 16)
            pool.wait_ge(rev_out, 16)
            pool.dma_start(biasM, bass.AP(rev_dram, P - 1, [[DIST - 1, P], [P * DIST, H], [1, T]])).then_inc(bias_in, 16)
            pool.wait_ge(v_done, 2 * STEPS)
            pool.dma_start(gfin, g_fin.partition_broadcast(P)).then_inc(gfin_in, 16)

        @block.scalar
        def _(act):
            for dst, src in ((identS, ident), (gmix, g_mix), (posS, pos), (qgS, q_gain), (kvgS, kv_gain),
                             (cosS, cos), (sinS, sin), (causalS[:, :], causal), (cmaskS, cmp_mask),
                             (hmaskS[0:H * NC, :], head_mask), (iotaS, iota), (iota16S, iota16), (gffn, g_ffn),
                             (w2kS, w2k.rearrange("(k p) c -> p k c", p=P)),
                             (w2vS, w2v.rearrange("(k p) c -> p k c", p=P))):
                act.dma_start(dst, src).then_inc(const_in, 16)
            chain = [0]

            def link(ins):
                chain[0] += 1
                ins.then_inc(act_chain, 1)
                act.wait_ge(act_chain, chain[0])

            act.wait_ge(x_in, 16)
            for i in range(NT):
                link(nc.scalar.activation(xs[:, i], h3[:, i], ACT.Square, accum_out=ssq[:, i:i + 1]))
            nc.scalar.copy(rstd[:, 0:NT], ssq[:, 0:NT]).then_inc(ssq_ready, 1)
            act.wait_ge(ms_ready, 1)
            nc.scalar.activation(rstd[:, 0:NT], ssq[:, 0:NT], ACT.Sqrt).then_inc(root_ready, 1)

            def gained_transposes(first, gain, done):
                act.wait_ge(const_in, CONSTS * 16)
                for q in (0, 2):
                    act.wait_ge(xT_ps, first + q + 1)
                    for m in range(4):
                        k = q % 2 * 4 + m
                        last = nc.scalar.activation(xnT3[:, k, (q // 2) * P:(q // 2 + 1) * P],
                                                    ps[2 + q][:, m * P:(m + 1) * P], ACT.Copy,
                                                    scale=gain[:, k:k + 1])
                    last.then_inc(xnT_act, 1)

            act.wait_ge(rev_ps, 1)
            nc.scalar.copy(revS, ps[6][0:H, 0:DIST]).then_inc(rev_sb, 1)
            act.wait_ge(rev_out, 16)
            gained_transposes(0, gmix, 0)

            def evacuate(n):
                b = ps[n % 2]
                act.wait_ge(job_done, n + 1)
                if n in (J_Q0, J_Q1):
                    last = nc.scalar.copy(qT[:, 2 * n:2 * n + 2], b[:, :].rearrange("p (a t) -> p a t", t=T))
                elif n == J_K:
                    last = nc.scalar.copy(kT, b[:, :].rearrange("p (a t) -> p a t", t=T))
                elif n in (J_R0, J_R1):
                    last = nc.scalar.copy(rest[:, n - J_R0], b[:, 0:REST])
                elif n == J_V:
                    last = nc.scalar.copy(Vn, b[:, :].rearrange("p (i c) -> p i c", i=NT))
                elif n == J_C:
                    for k in range(2):
                        last = nc.scalar.activation(cT[:, k], b[:, k * T:(k + 1) * T], ACT.Copy, scale=qgS[:, k:k + 1])
                elif n == J_CR:
                    nc.scalar.activation(cT[:, 2], b[:, 0:T], ACT.Copy, scale=kvgS[:, 0:1])
                    last = nc.scalar.copy(mkT[NOPE:QK], spread(b[NOPE:QK, T:2 * T], H))
                elif n < J_VM:
                    k = 2 * (n - J_KN)
                    last = nc.scalar.copy(mkT[0:NOPE, k:k + 2], b[0:NOPE, :].rearrange("p (a t) -> p a t", t=T))
                elif n < J_QN:
                    last = nc.scalar.copy(Vm[:, n - J_VM], b[:, :])
                elif n < J_QT:
                    i, half = divmod(n - J_QN, 2)
                    last = nc.scalar.copy(qn[:, i, half * 384:(half + 1) * 384], b[:, 0:384])
                elif n < J_MG:
                    i, quad = divmod(n - J_QT, 2)
                    last = nc.scalar.copy(mqT[0:QK, quad * 4:quad * 4 + 4, i * P:(i + 1) * P],
                                          b[0:QK, :].rearrange("p (a t) -> p a t", t=P))
                else:
                    c = n - J_MG
                    last = nc.scalar.activation(mgT[:, 2 * c:2 * c + 2], b[:, :].rearrange("p (a t) -> p a t", t=T),
                                                ACT.Sigmoid)
                last.then_inc(job_act, 1)
                if n == J_R1:
                    act.wait_ge(job_act, act_jobs_before(J_R1) + 1)
                    for i in range(NT):
                        nc.scalar.activation(sq[:, 0:Q_RANK], rest[:, i, CQ0:CKV0], ACT.Square,
                                             accum_out=ssq[:, 2 + i:3 + i])
                        link(nc.scalar.activation(sq[:, Q_RANK:Q_RANK + KV_RANK], rest[:, i, CKV0:KR0], ACT.Square,
                                                  accum_out=ssq[:, 4 + i:5 + i]))
                    nc.scalar.copy(rstd[:, 2:6], ssq[:, 2:6]).then_inc(c_ssq, 1)
                if n == J_V:
                    act.wait_ge(c_ms, 1)
                    nc.scalar.activation(rstd[:, 2:6], ssq[:, 2:6], ACT.Sqrt).then_inc(c_root, 1)

            for n in range(J_KN):
                if n not in DVE_JOBS:
                    evacuate(n)
            act.wait_ge(hid_ps, 1)
            for hid in range(2):
                nc.scalar.activation(hTk[:, hid], ps[6][:, hid * 32:hid * 32 + G * NC], ACT.Gelu)
                src = ps[6][:, (2 + hid) * 32:(2 + hid) * 32 + G * NC].rearrange("p (g c) -> p g c", g=G)
                last = nc.scalar.activation(hTv[:, hid].rearrange("p (g r c) -> p g r c", g=G, r=R),
                                            src.unsqueeze(2).to_broadcast([P, G, R, NC]), ACT.Gelu)
            last.then_inc(hid_ready, 1)
            for n in range(J_KN, J_QT):
                evacuate(n)
            act.wait_ge(kc_ps, 1)
            for g in range(G):
                nc.scalar.copy(kcT[g * DH:(g + 1) * DH, :], ps[7][g * DH:(g + 1) * DH, g * NC:(g + 1) * NC])
            nc.scalar.copy(vcs[0:H * NC, :], ps[7][0:H * NC, 64:64 + DH]).then_inc(kc_ready, 1)
            for i in range(NT):
                last = nc.scalar.activation(rest[:, i, 0:3 * H], rest[:, i, 0:3 * H], ACT.Sigmoid)
            last.then_inc(gate_ready, 1)

            for n in range(UNITS):
                if n < 2:
                    act.wait_ge(cmp_sub, n + 1)
                    ncv = NC0 if n == 0 else NC
                    e = Ec[:, n].rearrange("p (h c) -> p h c", c=NC)[:, :, 0:ncv]
                    nc.scalar.activation(e, e, ACT.Exp).then_inc(cmp_exp, 1)
                else:
                    br, i, pr = unit(n)
                    act.wait_ge(max_ready, n - 1)
                    for j in range(2):
                        e = E[:, n % 2, j, 0:(i + 1) * P]
                        last = nc.scalar.activation(e, e, ACT.Exp, bias=nmx[:, n - 2, j:j + 1],
                                                    accum_out=sums[:, br * 2 + i, 2 * pr + j:2 * pr + j + 1])
                    last.then_inc(E_ready, 1)
                act.wait_ge(T_done, n + 1)
                if n >= 2:
                    act.wait_ge(V_done, n - 1)
                if n < 2:
                    nc.scalar.copy(eT[n % 2][0:H * NC, 0:P], ps[4 + n % 2][0:H * NC, 0:P]).then_inc(eT_ready, 1)
                else:
                    w = 2 * (i + 1) * P
                    nc.scalar.copy(eT[n % 2][:, 0:w], ps[4 + n % 2][:, 0:w]).then_inc(eT_ready, 1)
                for j in fill_jobs(n):
                    evacuate(j)

            for q in range(4):
                act.wait_ge(oT_ps, q + 1)
                nc.scalar.copy(oT[:, (q // 2) * 4:(q // 2) * 4 + 4, (q % 2) * P:(q % 2 + 1) * P],
                               ps[q][:, :].rearrange("p (a t) -> p a t", t=P)).then_inc(oT_ready, 1)
            act.wait_ge(h_ready, 4)
            for i in range(NT):
                link(nc.scalar.activation(S[:, i].rearrange("p a b -> p (a b)")[:, 0:D], h3[:, i], ACT.Square, accum_out=ssq[:, i:i + 1]))
            nc.scalar.copy(rstd[:, 0:NT], ssq[:, 0:NT]).then_inc(ssq_ready, 1)
            act.wait_ge(ms_ready, 2)
            nc.scalar.activation(rstd[:, 0:NT], ssq[:, 0:NT], ACT.Sqrt).then_inc(root_ready, 1)
            gained_transposes(4, gffn, 2)
            for j in range(4):
                act.wait_ge(qp_done, j + 1)
                nc.scalar.copy(qpT[:, 2 * j:2 * j + 2], ps[j][:, :].rearrange("p (a t) -> p a t", t=T)).then_inc(qp_ready, 1)
            for q in range(2 * 4):
                i, f = divmod(q, 4)
                act.wait_ge(s_done, q + 1)
                nc.scalar.copy(S[:, i, 4 * f:4 * f + 4],
                               ps[(q + 4) % 8][:, :].rearrange("p (a t) -> p a t", t=NK)).then_inc(s_ready, 1)

            def gelus(it, half):
                for s in range(RING):
                    for j in range(2):
                        m = it * (2 * RING) + 2 * s + j + half * 2 * STEPS
                        act.wait_ge(u_done, m + 1)
                        nc.scalar.activation(big[:, ds(m * T, T)], ps[j][:, 0:T], ACT.Gelu).then_inc(gelu_done, 1)

            gelus(0, 0)
            for i in range(NT):
                act.wait_ge(best_sub, i + 1)
                nc.scalar.activation(best, best, ACT.Exp).then_inc(best_exp, 1)
            with act.Fori(1, STEPS // RING) as it:
                gelus(it, 0)
            act.wait_ge(pT_done, 1)
            for s, dst in enumerate((i1T, i2T, gT)):
                last = nc.scalar.copy(dst, ps[2 + s // 2][:, (s % 2) * T:(s % 2 + 1) * T])
            last.then_inc(pT_ready, 1)
            with act.Fori(0, STEPS // RING) as it:
                gelus(it, 1)

            act.wait_ge(v_done, 2 * STEPS)
            for q in (0, 2):
                last = nc.scalar.copy(yT[:, 2 * q:2 * q + 2], ps[4 + q][:, :].rearrange("p (a t) -> p a t", t=T))
            last.then_inc(y_act, 1)
            for i in range(NT):
                for f in range(2):
                    act.wait_ge(yn_done, 2 * i + f + 1)
                    link(nc.scalar.activation(sq_fin[:, f * 512:(f + 1) * 512], ps[2 * i + f][:, :], ACT.Square,
                                              accum_out=ssq[:, 2 * i + f:2 * i + f + 1]))
            nc.scalar.copy(rstd[:, 0:4], ssq[:, 0:4]).then_inc(f_ssq, 1)
            act.wait_ge(f_ms, 1)
            nc.scalar.activation(rstd[:, 0:NT], ssq[:, 4:4 + NT], ACT.Sqrt).then_inc(f_root, 1)

        @block.vector
        def _(dve):
            chain = [0]
            vec = nc.vector

            def link(ins):
                chain[0] += 1
                ins.then_inc(dve_chain, 1)
                dve.wait_ge(dve_chain, chain[0])

            def self_wait(ins, sem_, count):
                ins.then_inc(sem_, 1)
                dve.wait_ge(sem_, count)

            def norm_scale(turn):
                dve.wait_ge(ssq_ready, turn + 1)
                vec.tensor_scalar(ssq[:, 0:NT], rstd[:, 0:NT], 1.0 / D, EPS, ALU.mult, ALU.add).then_inc(ms_ready, 1)
                dve.wait_ge(root_ready, turn + 1)
                link(vec.reciprocal(ssq[:, 0:NT], rstd[:, 0:NT]))
                for i in range(NT):
                    vec.tensor_scalar(xs[:, i], h3[:, i], ssq[:, i:i + 1], None, ALU.mult).then_inc(xs_ready, 1)

            def gained_transposes(first, gain):
                for q in (1, 3):
                    dve.wait_ge(xT_ps, first + q + 1)
                    for m in range(4):
                        k = q % 2 * 4 + m
                        last = vec.tensor_scalar(xnT3[:, k, (q // 2) * P:(q // 2 + 1) * P],
                                                 ps[2 + q][:, m * P:(m + 1) * P], gain[:, k:k + 1], None, ALU.mult)
                    last.then_inc(xnT_dve, 1)

            dve.wait_ge(x_in, 16)
            norm_scale(0)
            vec.memset(kpad, 0.0)
            vec.memset(Ec, 0.0)
            dve.wait_ge(const_in, CONSTS * 16)
            dve.wait_ge(rev_out, 16)
            gained_transposes(0, gmix)
            dve.wait_ge(c_ssq, 1)
            vec.tensor_scalar(ssq[:, 2:4], rstd[:, 2:4], 1.0 / Q_RANK, EPS, ALU.mult, ALU.add)
            vec.tensor_scalar(ssq[:, 4:6], rstd[:, 4:6], 1.0 / KV_RANK, EPS, ALU.mult, ALU.add).then_inc(c_ms, 1)
            for n, jb in enumerate(DVE_JOBS):
                dve.wait_ge(job_done, jb + 1)
                for par in range(2):
                    rows = slice(par * DH, (par + 1) * DH)
                    for g in range(G):
                        o = g * T + par
                        last = vec.tensor_tensor(
                            blkT[rows, n, :, g * NC:(g + 1) * NC],
                            strided(ps[jb % 2][rows, o:o + 1], [[2, LP], [CMP_STRIDE, NC]]),
                            bcast(posS[rows, n], NC), ALU.add)
                last.then_inc(job_dve, 1)
            dve.wait_ge(c_root, 1)
            link(vec.reciprocal(ssq[:, 2:6], rstd[:, 2:6]))
            for i in range(NT):
                vec.tensor_scalar(rest[:, i, CQ0:CKV0], rest[:, i, CQ0:CKV0], ssq[:, 2 + i:3 + i], None, ALU.mult)
                last = vec.tensor_scalar(rest[:, i, CKV0:KR0], rest[:, i, CKV0:KR0], ssq[:, 4 + i:5 + i], None, ALU.mult)
            last.then_inc(cn_ready, 1)

            def rotate(x1, x2, c, s, heads, y1, y2):
                t = [r[:, 0:heads] for r in rot]
                vec.tensor_tensor(t[0], x1, c, ALU.mult)
                vec.tensor_tensor(t[1], x2, s, ALU.mult)
                vec.tensor_tensor(t[2], x2, c, ALU.mult)
                link(vec.tensor_tensor(t[3], x1, s, ALU.mult))
                vec.tensor_tensor(y1, t[0], t[1], ALU.subtract)
                return vec.tensor_tensor(y2, t[2], t[3], ALU.add)

            HR = ROPE // 2
            last = rotate(rest[:, :, KR0:KR0 + HR], rest[:, :, KR0 + HR:KR0 + ROPE], cosS, sinS, NT,
                          kpad[:, :, NOPE:NOPE + HR], kpad[:, :, NOPE + HR:QK])
            last.then_inc(kr_ready, 1)
            for i in range(NT):
                dve.wait_ge(job_act, act_jobs_before(J_QN + 2 * i + 1) + 1)
                q = qn[:, i].rearrange("p (h c) -> p h c", c=QK)
                last = rotate(q[:, :, NOPE:NOPE + HR], q[:, :, NOPE + HR:QK], spread(cosS[:, i], H), spread(sinS[:, i], H),
                              H, q[:, :, NOPE:NOPE + HR], q[:, :, NOPE + HR:QK])
                self_wait(last, rope_ready, i + 1)
            dve.wait_ge(kc_ready, 1)
            vec.tensor_tensor(VB[0:H * NC, :].rearrange("p (h d) -> p h d", d=DH), spread(vcs[0:H * NC, :], H),
                              bcast(hmaskS[0:H * NC, :], DH), ALU.mult).then_inc(vb_ready, 1)
            dve.wait_ge(bias_in, 16)
            dve.wait_ge(gate_ready, 1)

            def combine(gr):
                i = gr % 2
                gate = rest[:, i, 0:3 * H].rearrange("p (h b) -> p b h", b=3)
                dve.wait_ge(O_done, gr + 1)
                if gr < 2:
                    link(vec.reciprocal(sc[:, gr], csum[:, i]))
                    link(vec.tensor_tensor(sc[:, gr], sc[:, gr], gate[:, 0], ALU.mult))
                else:
                    link(vec.reciprocal(sc[:, gr], sums[:, gr - 2]))
                    if gr < 6:
                        link(vec.tensor_tensor(sc[:, gr], sc[:, gr], gate[:, gr // 2], ALU.mult))
                o = ps[6 + gr % 2][:, :].rearrange("p (h d) -> p h d", d=DH)
                dst = onat[gr // 6][:, i].rearrange("p (h d) -> p h d", d=DH)
                if gr < 2 or gr >= 6:
                    self_wait(vec.tensor_tensor(dst, o, bcast(sc[:, gr], DH), ALU.mult), O_free, gr + 1)
                else:
                    self_wait(vec.tensor_tensor(tmp.rearrange("p (h d) -> p h d", d=DH), o, bcast(sc[:, gr], DH), ALU.mult),
                              O_free, gr + 1)
                    link(vec.tensor_tensor(onat[0][:, i], onat[0][:, i], tmp, ALU.add))

            for n in range(2):
                ncv = NC0 if n == 0 else NC
                e = Ec[:, n].rearrange("p (h c) -> p h c", c=NC)[:, :, 0:ncv]
                k0 = CMP_LEN - 1 + (P if n == 0 else 0)
                dve.wait_ge(L_done, n + 1)
                self_wait(vec.scalar_tensor_tensor(
                    e, ps[2 + n][:, 0:H * 16].rearrange("p (h c) -> p h c", c=16)[:, :, 0:ncv], DH ** -0.5,
                    strided(biasM[:, 0, k0:k0 + 1], [[T, H], [CMP_STRIDE, ncv]]), ALU.mult, ALU.add), L_free, n + 1)
                link(vec.tensor_reduce(csum[:, n], e, AX.X, ALU.max))
                vec.tensor_tensor(e, e, bcast(csum[:, n], ncv), ALU.subtract).then_inc(cmp_sub, 1)
                dve.wait_ge(cmp_exp, n + 1)
                link(vec.tensor_tensor(e, e, spread(cmaskS[:, n, 0:ncv], H), ALU.mult))
                link(vec.tensor_reduce(csum[:, n], e, AX.X, ALU.add))
                self_wait(vec.tensor_scalar(csum[:, n], csum[:, n], 1e-30, None, ALU.max), cmp_ready, n + 1)

            for n in range(2, UNITS):
                br, i, pr = unit(n)
                w = (i + 1) * P
                e = E[:, n % 2, :, 0:w]
                lg = ps[2 + n % 2][:, :].rearrange("p (a k) -> p a k", a=2)[:, :, 0:w]
                bias = biasM[:, 2 * pr:2 * pr + 2, T - w:T] if br < 2 else spread(causalS[:, T - w:T], 2)
                scale = DH ** -0.5 if br < 2 else QK ** -0.5
                dve.wait_ge(L_done, n + 1)
                dve.wait_ge(T_done, n - 1)
                self_wait(vec.scalar_tensor_tensor(e, lg, scale, bias, ALU.mult, ALU.add), L_free, n + 1)
                vec.tensor_reduce(nmx[:, n - 2], e, AX.X, ALU.max, negate=True).then_inc(max_ready, 1)
                if n in (3, 4):
                    combine(n - 3)
                elif n >= 7 and (n - 7) % 4 == 0:
                    combine(2 + (n - 7) // 4)
            combine(7)

            for c in range(KT):
                dve.wait_ge(br_done, c + 1)
                b = ps[c % 2 + 4]
                t2 = strided(tmp[:, 0:1], [[T, 2], [1, T]])
                self_wait(vec.tensor_tensor(t2, b[:, :].rearrange("p (a t) -> p a t", t=T),
                                            strided(mgT[:, c, 0:1], [[KT * T, 2], [1, T]]), ALU.mult), br_free, c + 1)
                self_wait(vec.tensor_tensor(mergedT[:, c], tmp[:, 0:T], tmp[:, T:2 * T], ALU.add), merged_ready, c + 1)
            for q in range(4):
                i, f = divmod(q, 2)
                dve.wait_ge(h_ps, q + 1)
                hh = h3[:, i, f * 512:(f + 1) * 512]
                last = vec.tensor_tensor(hh, hh, ps[q][:, :], ALU.add).then_inc(h_ready, 1)
            dve.wait_ge(h_ready, 4)
            norm_scale(1)
            gained_transposes(4, gffn)

            for i in range(NT):
                dve.wait_ge(s_ready, 4 * (i + 1))
                for m in range(2 * H):
                    s = S[:, i, m]
                    link(vec.max(topv[:, m, 0:8], s))
                    vec.max_index(topi[:, m, 0:8], topv[:, m, 0:8], s)
                    link(vec.match_replace(s, topv[:, m, 0:8], s, -3e38))
                    link(vec.max(topv[:, m, 8:16], s))
                    vec.max_index(topi[:, m, 8:16], topv[:, m, 8:16], s)
                link(vec.tensor_tensor(cand.rearrange("p h (a b) -> p h a b", b=TOPK), bcast(topv[:, 0:H], TOPK),
                                       topv[:, H:2 * H].unsqueeze(2).to_broadcast([P, H, TOPK, TOPK]), ALU.add))
                link(vec.tensor_copy(topi_f, topi))
                for m in range(H):
                    c = cand[:, m]
                    link(vec.max(best[:, m, 0:8], c))
                    vec.max_index(pick[:, m, 0:8], best[:, m, 0:8], c)
                    link(vec.match_replace(c, best[:, m, 0:8], c, -3e38))
                    link(vec.max(best[:, m, 8:16], c))
                    link(vec.max_index(pick[:, m, 8:16], best[:, m, 8:16], c))
                link(vec.tensor_copy(gsum, best[:, :, 0]))
                vec.tensor_tensor(best, best, bcast(gsum, TOPK), ALU.subtract).then_inc(best_sub, 1)
                pf = pick.rearrange("p h k -> p (h k)")
                vec.tensor_scalar(pick_a, pf, 4, None, ALU.logical_shift_right)
                link(vec.tensor_scalar(pick_b, pf, TOPK - 1, None, ALU.bitwise_and))
                vec.tensor_copy(pa_f, pick_a)
                link(vec.tensor_copy(pb_f, pick_b))
                for side, pos_f in enumerate((pa_f, pb_f)):
                    link(vec.tensor_tensor(eq, bcast(pos_f, TOPK), spread(iota16S, H * TOPK), ALU.is_equal))
                    eq4 = eq.rearrange("p (h k) a -> p h k a", h=H)
                    link(vec.tensor_tensor(eq4, eq4, topi_f[:, side * H:(side + 1) * H].unsqueeze(2).to_broadcast(
                        [P, H, TOPK, TOPK]), ALU.mult))
                    link(vec.tensor_reduce(picks[side][:, i], eq, AX.X, ALU.add))
                dve.wait_ge(best_exp, i + 1)
                link(vec.tensor_reduce(gsum, best, AX.X, ALU.add))
                link(vec.reciprocal(gsum, gsum))
                self_wait(vec.tensor_tensor(picks[2][:, i].rearrange("p (h k) -> p h k", h=H), best, bcast(gsum, TOPK),
                                            ALU.mult), picks_ready, i + 1)

            bigT = part(big, 0, NK, T).rearrange("p c t -> p t c")
            dve.wait_ge(pT_ready, 1)

            def spread_picks(it, s, half):
                n = it * RING + s
                t0 = n * TB
                a, b = A[s % 2], B[s % 2]
                vec.tensor_tensor(a, spread(iotaS, TB), bcast(i1T[:, ds(t0, TB)], NK), ALU.is_equal)
                vec.tensor_tensor(b, spread(iotaS[:, half * 64:(half + 1) * 64], TB),
                                  bcast(i2T[:, ds(t0, TB)], 64), ALU.is_equal).then_inc(b_marked, 1)
                dve.wait_ge(b_marked, n + (half * STEPS + 1))
                vec.tensor_tensor(b, b, bcast(gT[:, ds(t0, TB)], 64), ALU.mult).then_inc(ab_ready, 1)

            def weigh(it, s, half):
                n = it * RING + s
                w = bigT[:, ds(n * TB, TB), half * 64:(half + 1) * 64]
                dve.wait_ge(g_done, n + (half * STEPS + 1))
                vec.tensor_tensor(w, ps[2 + s % 2][:, :].rearrange("p (t c) -> p t c", t=TB), w, ALU.mult).then_inc(w_done, 1)

            for half in range(2):
                dve.wait_ge(gelu_done, (half + 1) * 2 * STEPS)
                spread_picks(0, 0, half)
                spread_picks(0, 1, half)
                with dve.Fori(0, STEPS // RING - 1) as it:
                    for s in range(RING):
                        weigh(it, s, half)
                        spread_picks(it + (s + 2) // RING, (s + 2) % RING, half)
                for s in range(RING):
                    weigh(STEPS // RING - 1, s, half)
                    if s < 2:
                        spread_picks(STEPS // RING - 1, s + 2, half)

            dve.wait_ge(v_done, 2 * STEPS)
            for q in (1, 3):
                last = vec.tensor_copy(yT[:, 2 * q:2 * q + 2], ps[4 + q][:, :].rearrange("p (a t) -> p a t", t=T))
            last.then_inc(y_dve, 1)
            dve.wait_ge(f_ssq, 1)
            link(vec.tensor_tensor(ssq[:, 4:6], strided(rstd[:, 0:1], [[2, NT]]), strided(rstd[:, 1:2], [[2, NT]]), ALU.add))
            vec.tensor_scalar(ssq[:, 4:6], ssq[:, 4:6], 1.0 / D, EPS, ALU.mult, ALU.add).then_inc(f_ms, 1)
            dve.wait_ge(f_root, 1)
            link(vec.reciprocal(ssq[:, 0:NT], rstd[:, 0:NT]))
            dve.wait_ge(gfin_in, 16)
            for i in range(NT):
                for f in range(2):
                    c = slice(f * 512, (f + 1) * 512)
                    last = vec.scalar_tensor_tensor(ynat[:, i, c], ps[2 * i + f][:, :], ssq[:, i:i + 1], gfin[:, c],
                                                    ALU.mult, ALU.mult)
                last.then_inc(out_ready, 1)

        @block.tensor
        def _(pe):
            def mm(o, lhsT, rhs, start=True, stop=True, **kw):
                return nc.tensor.matmul(o, lhsT, rhs, start=start, stop=stop, **kw)

            def transpose(o, a):
                return nc.tensor.transpose(o, a, identS[0:a.shape[0], 0:a.shape[0]])

            pe.wait_ge(t5_in, 48)
            mm(ps[6][0:H, 0:DIST], t5S[:, :], ohS).then_inc(rev_ps, 1)

            def transpose_xs(turn):
                pe.wait_ge(const_in, CONSTS * 16)
                for q in range(4):
                    i = q // 2
                    pe.wait_ge(xs_ready, turn * NT + i + 1)
                    for m in range(4):
                        k = q % 2 * 4 + m
                        last = transpose(ps[2 + q][:, m * P:(m + 1) * P], xs[:, i, k * P:(k + 1) * P])
                    last.then_inc(xT_ps, 1)

            transpose_xs(0)
            pe.wait_ge(xnT_act, 2)
            pe.wait_ge(xnT_dve, 2)

            def project(o, weight, n=KT, rhs=xnT3):
                for k in range(n):
                    last = mm(o, weight(k), rhs[:, k], start=k == 0, stop=k == n - 1)
                return last

            def job(n):
                if n >= 2:
                    wait_job_evacuated(pe, n - 2)
                b = ps[n % 2]
                if n in (J_Q0, J_Q1):
                    pe.wait_ge(win_in[0], 16)
                    for j in range(2):
                        r = 2 * n + j
                        last = project(b[:, j * T:(j + 1) * T],
                                       lambda k: win[:, k, r * P:(r + 1) * P])
                elif n == J_K:
                    pe.wait_ge(win_in[1], 16)
                    for j in range(2):
                        c = K0 + j * P
                        last = project(b[:, j * T:(j + 1) * T], lambda k: win[:, k, c:c + P])
                elif n in (J_CK, J_CV):
                    pe.wait_ge(win_in[2 + n - J_CK], 16)
                    src, lo = (win, CK0) if n == J_CK else (wcv, 0)
                    for g in range(G):
                        c = lo + g * P
                        last = project(b[:, g * T:(g + 1) * T], lambda k: src[:, k, c:c + P])
                elif n == J_V:
                    for i in range(NT):
                        for k in range(KT):
                            last = mm(b[:, i * T:(i + 1) * T], xnT3[:, k, i * P:(i + 1) * P], win[:, k, V0:REST0],
                                      start=k == 0, stop=k == KT - 1)
                elif n in (J_R0, J_R1):
                    pe.wait_ge(win_in[2], 16)
                    i = n - J_R0
                    for k in range(KT):
                        last = mm(b[:, 0:REST], xnT3[:, k, i * P:(i + 1) * P], win[:, k, REST0:CK0],
                                  start=k == 0, stop=k == KT - 1)
                elif n == J_C:
                    pe.wait_ge(cn_ready, 1)
                    for k in range(2):
                        for i in range(NT):
                            last = transpose(b[:, k * T + i * P:k * T + (i + 1) * P],
                                             rest[:, i, CQ0 + k * P:CQ0 + (k + 1) * P])
                elif n == J_CR:
                    pe.wait_ge(kr_ready, 1)
                    for i in range(NT):
                        transpose(b[:, i * P:(i + 1) * P], rest[:, i, CKV0:KR0])
                        last = transpose(b[0:QK, T + i * P:T + (i + 1) * P], kpad[:, i])
                elif n < J_VM:
                    pe.wait_ge(wu_in, 32)
                    wait_job_evacuated(pe, J_CR)
                    for j in range(2):
                        hd = 2 * (n - J_KN) + j
                        last = mm(b[0:NOPE, j * T:(j + 1) * T], wukv[:, hd * 2 * DH:hd * 2 * DH + NOPE], cT[:, 2])
                elif n < J_QN:
                    i = n - J_VM
                    last = mm(b[:, :].rearrange("p (h d) -> p h d", d=DH), cT[:, 2, i * P:(i + 1) * P],
                              wukv.rearrange("p (h c) -> p h c", c=2 * DH)[:, :, NOPE:2 * DH])
                elif n < J_QT:
                    i, half = divmod(n - J_QN, 2)
                    for k in range(2):
                        last = mm(b[:, 0:384], cT[:, k, i * P:(i + 1) * P], wuq[:, k, half * 384:(half + 1) * 384],
                                  start=k == 0, stop=k == 1)
                elif n < J_MG:
                    pe.wait_ge(rope_ready, NT)
                    i, quad = divmod(n - J_QT, 2)
                    for j in range(4):
                        hd = quad * 4 + j
                        last = transpose(b[0:QK, j * P:(j + 1) * P], qn[:, i, hd * QK:(hd + 1) * QK])
                else:
                    c = n - J_MG
                    pe.wait_ge(merge_in[c % 2], 16 * (c // 2 + 1))
                    for j in range(2):
                        last = project(b[:, j * T:(j + 1) * T], lambda k: mslot[c % 2][:, k, j * P:(j + 1) * P])
                last.then_inc(job_done, 1)

            for n in range(J_KN):
                job(n)
            pe.wait_ge(w1_in, 32)
            pe.wait_ge(job_dve, 2)
            for kv in range(2):
                for hid in range(2):
                    c = (kv * 2 + hid) * 32
                    for l in range(LP):
                        last = mm(ps[6][:, c:c + G * NC], w1[:, kv, l, hid * P:(hid + 1) * P], blkT[:, kv, l],
                                  start=l == 0, stop=l == LP - 1)
            last.then_inc(hid_ps, 1)
            for n in range(J_KN, J_QT):
                job(n)
            pe.wait_ge(hid_ready, 1)
            for hid in range(2):
                mm(ps[7][:, 0:G * NC], w2kS[:, hid], hTk[:, hid],
                   start=hid == 0, stop=hid == 1)
            for hid in range(2):
                last = mm(ps[7][0:H * NC, 64:64 + DH], hTv[:, hid], w2vS[:, hid], start=hid == 0, stop=hid == 1)
            last.then_inc(kc_ps, 1)
            pe.wait_ge(kc_ready, 1)

            def logits(n):
                if n >= 2:
                    pe.wait_ge(L_free, n - 1)
                b = ps[2 + n % 2]
                if n < 2:
                    for hd in range(H):
                        g, r = divmod(hd, R)
                        rows = slice(g * DH, (g + 1) * DH)
                        last = mm(b[:, hd * 16:hd * 16 + NC], qT[rows, r, n * P:(n + 1) * P], kcT[rows, :])
                        if hd == R - 1:
                            last.then_inc(half_logits, 1)
                            pe.wait_ge(half_logits, n + 1)
                else:
                    br, i, pr = unit(n)
                    w = (i + 1) * P
                    for j in range(2):
                        hd = 2 * pr + j
                        o = b[:, j * T:j * T + w]
                        if br < 2:
                            g, r = divmod(hd, R)
                            rows = slice(g * DH, (g + 1) * DH)
                            last = mm(o, qT[rows, r, i * P:(i + 1) * P], kT[rows, br, 0:w])
                        else:
                            last = mm(o, mqT[0:QK, hd, i * P:(i + 1) * P], mkT[0:QK, hd, 0:w])
                last.then_inc(L_done, 1)

            logits(0)
            logits(1)
            for n in range(UNITS):
                if n < 2:
                    pe.wait_ge(cmp_ready, n + 1)
                    last = transpose(ps[4 + n][0:H * NC, 0:P], Ec[:, n])
                else:
                    br, i, pr = unit(n)
                    pe.wait_ge(E_ready, n - 1)
                    pe.wait_ge(eT_ready, n - 1)
                    for j in range(2):
                        for k in range(i + 1):
                            c = (j * (i + 1) + k) * P
                            last = transpose(ps[4 + n % 2][:, c:c + P], E[:, n % 2, j, k * P:(k + 1) * P])
                last.then_inc(T_done, 1)
                if n + 2 < UNITS:
                    if unit(n + 2)[0] == 2:
                        wait_job_evacuated(pe, J_QT + 3)
                    logits(n + 2)
                for j in fill_jobs(n):
                    job(j)
                gr = group(n)
                first = n < 2 or (n - 2) % 4 == 0
                if first and gr >= 2:
                    pe.wait_ge(O_free, gr - 1)
                pe.wait_ge(eT_ready, n + 1)
                b = ps[6 + gr % 2]
                if n < 2:
                    pe.wait_ge(vb_ready, 1)
                    last = mm(b[:, :], eT[n % 2][0:H * NC, 0:P], VB[0:H * NC, :])
                else:
                    for j in range(2):
                        hd = 2 * pr + j
                        for k in range(i + 1):
                            c = (j * (i + 1) + k) * P
                            if br < 2:
                                lo = br * P + hd // R * DH
                                val = Vn[:, k, lo:lo + DH]
                            else:
                                val = Vm[:, k, hd * DH:(hd + 1) * DH]
                            last = mm(b[:, hd * DH:(hd + 1) * DH], eT[n % 2][:, c:c + P], val, start=k == 0, stop=k == i)
                last.then_inc(V_done, 1)
                if n < 2 or (n - 2) % 4 == 3:
                    pe.wait_ge(V_done, n + 1)
                    pe.sem_inc(O_done, 1)

            pe.wait_ge(O_free, 8)
            wait_job_evacuated(pe, JOBS - 1)
            for q in range(4):
                for m in range(4):
                    last = transpose(ps[q][:, m * P:(m + 1) * P], onat[q // 2][:, q % 2, m * P:(m + 1) * P])
                last.then_inc(oT_ps, 1)
            pe.wait_ge(oT_ready, 4)
            pe.wait_ge(wb_in, 32)
            for c in range(KT):
                if c >= 2:
                    pe.wait_ge(br_free, c - 1)
                for m in range(2):
                    last = project(ps[c % 2 + 4][:, m * T:(m + 1) * T], lambda k: wb[:, m, k, c * P:(c + 1) * P], 4,
                                   oT[:, 4 * m:4 * m + 4])
                last.then_inc(br_done, 1)
            pe.wait_ge(wo_in, 16)
            pe.wait_ge(merged_ready, KT)
            for q in range(4):
                i, f = divmod(q, 2)
                for k in range(KT):
                    last = mm(ps[q][:, :], mergedT[:, k, i * P:(i + 1) * P], wo[:, k, f * 512:(f + 1) * 512],
                              start=k == 0, stop=k == KT - 1)
                last.then_inc(h_ps, 1)

            transpose_xs(1)
            pe.wait_ge(xnT_act, 4)
            pe.wait_ge(xnT_dve, 4)
            pe.wait_ge(wq_in, 16)
            pe.wait_ge(h_ready, 4)
            for j in range(4):
                for m in range(2):
                    hd = 2 * j + m
                    last = project(ps[j][:, m * T:(m + 1) * T], lambda k: wq[:, k, hd * P:(hd + 1) * P])
                last.then_inc(qp_done, 1)
            pe.wait_ge(keys_in, 16)
            for q in range(2 * 4):
                i, f = divmod(q, 4)
                if q == 0:
                    pe.wait_ge(qp_ready, 4)
                for m in range(4):
                    side, hd = divmod(4 * f + m, H)
                    rows = slice(side * DH, (side + 1) * DH)
                    last = mm(ps[(q + 4) % 8][:, m * NK:(m + 1) * NK], qpT[rows, hd, i * P:(i + 1) * P], keysT[rows, hd])
                last.then_inc(s_done, 1)

            pe.wait_ge(s_ready, 8)
            for k in range(KT):
                for i in range(NT):
                    mm(ps[4 + k // 2][:, (k % 2) * T + i * P:(k % 2) * T + (i + 1) * P], h3[:, i, k * P:(k + 1) * P],
                       identS, start=k % 2 == 0 and i == 0, stop=False, skip_group_check=True)

            def expert_inputs(it, s, half):
                n = it * RING + s + half * STEPS
                pe.wait_ge(ring_in[s], (it + (half * STEPS // RING + 1)) * 16)
                for j in range(2):
                    yield_bank = ps[j]
                    if half == 0 and isinstance(it, int) and it == 0 and s == 0:
                        pass
                    else:
                        pe.wait_ge(gelu_done, n * 2 + j - 1)
                    for k in range(KT):
                        c = (2 * s + j) * D + k * P
                        last = mm(yield_bank[:, 0:T], ring[:, c:c + P], xnT3[:, k], start=k == 0, stop=k == KT - 1)
                    last.then_inc(u_done, 1)

            def pick_weights(it, s, half):
                n = it * RING + s
                pe.wait_ge(ab_ready, n + (half * STEPS + 1))
                if not (half == 0 and isinstance(it, int) and it == 0 and s < 2):
                    pe.wait_ge(w_done, n + (half * STEPS - 1))
                for t in range(TB):
                    last = mm(ps[2 + s % 2][:, t * 64:(t + 1) * 64], A[s % 2][:, t], B[s % 2][:, t])
                last.then_inc(g_done, 1)

            def expert_outputs(it, s, half):
                n = it * RING + s + half * STEPS
                pe.wait_ge(ring_in[s], (it + ((half + 2) * STEPS // RING + 1)) * 16)
                for j in range(2):
                    for k in range(KT):
                        c = (2 * s + j) * D + k * P
                        last = mm(ps[4 + k // 2][:, (k % 2) * T:(k % 2 + 1) * T], ring[:, c:c + P],
                                  big[:, ds((n * 2 + j) * T, T)], start=False, stop=False, skip_group_check=True)
                last.then_inc(v_done, 1)

            for s in range(RING):
                expert_inputs(0, s, 0)
            with pe.Fori(1, STEPS // RING) as it:
                for s in range(RING):
                    expert_inputs(it, s, 0)
            pe.wait_ge(picks_ready, NT)
            for s in range(3):
                for i in range(NT):
                    c = (s % 2) * T + i * P
                    last = transpose(ps[2 + s // 2][:, c:c + P], picks[s][:, i])
            last.then_inc(pT_done, 1)
            pe.wait_ge(pT_ready, 1)
            for s in range(RING):
                expert_inputs(0, s, 1)
                pick_weights(0, s, 0)
            with pe.Fori(1, STEPS // RING) as it:
                for s in range(RING):
                    expert_inputs(it, s, 1)
                    pick_weights(it, s, 0)
            pe.wait_ge(w_done, STEPS)
            with pe.Fori(0, STEPS // RING) as it:
                for s in range(RING):
                    expert_outputs(it, s, 0)
                    pick_weights(it, s, 1)
            pe.wait_ge(w_done, 2 * STEPS)
            with pe.Fori(0, STEPS // RING) as it:
                for s in range(RING):
                    expert_outputs(it, s, 1)
            pe.wait_ge(y_act, 1)
            pe.wait_ge(y_dve, 1)
            for i in range(NT):
                for f in range(2):
                    for m in range(4):
                        last = transpose(ps[2 * i + f][:, m * P:(m + 1) * P], yT[:, 4 * f + m, i * P:(i + 1) * P])
                    last.then_inc(yn_done, 1)


def constants():
    f = np.float32
    dist = (T - 1) - np.arange(DIST)
    n = np.maximum(dist, 0)
    half = BUCKETS // 2
    ratio = np.maximum(n, half).astype(f) / f(half)
    large = half + (np.log(ratio) / f(math.log(MAX_DIST / half)) * f(BUCKETS - half)).astype(np.int32)
    bucket = np.where(n < half, n, np.minimum(large, BUCKETS - 1))
    bucket = np.where(dist < 0, BUCKETS, bucket)
    one_hot = (np.arange(BUCKETS + 1)[:, None] == bucket[None, :]).astype(f)
    inv = f(10000.0) ** (-np.arange(0, ROPE, 2, dtype=f) / f(ROPE))
    ang = (np.arange(T, dtype=f)[:, None] * inv[None, :]).astype(f)
    tiles = lambda a: np.ascontiguousarray(a.reshape(NT, P, -1).transpose(1, 0, 2)).astype(f)
    keys, p = np.arange(T), np.arange(P)[:, None]
    causal = np.where(P + p - keys[None, :] >= 0, f(0), f(MASKED)).astype(f)
    ends = np.arange(NC) * CMP_STRIDE + CMP_LEN - 1
    return {
        "ident": np.eye(P, dtype=f),
        "one_hot": one_hot,
        "masked_row": np.full((1, H), MASKED, f),
        "cos": tiles(np.cos(ang)), "sin": tiles(np.sin(ang)),
        "causal": causal,
        "cmp_mask": tiles((np.arange(T)[:, None] >= ends[None, :]).astype(f)),
        "head_mask": np.repeat(np.eye(H, dtype=f), NC, axis=0),
        "iota": np.tile(np.arange(NK, dtype=f), (P, 1)),
        "iota16": np.tile(np.arange(TOPK, dtype=f), (P, 1)),
    }


def kernel(**inputs):
    import concourse.bacc as bacc
    from concourse.bass_utils import run_bass_kernel_spmd

    a = {k: np.asarray(val) for k, val in inputs.items()}
    cols = lambda g: g.reshape(-1, P).T
    pos = lambda g: g.reshape(LP, 2 * DH).T
    w = a["w_in"][0]
    kv = w[:, Q_COLS:Q_COLS + 6 * P].reshape(D, 6, G, DH)
    twice = lambda z: np.stack([z, z], axis=2).reshape(D, 2 * P)
    end = Q_COLS + 6 * P
    w_in = np.concatenate([
        w[:, :Q_COLS].reshape(D, G, R, DH).transpose(0, 2, 1, 3).reshape(D, Q_COLS),
        kv[:, 2].reshape(D, P), kv[:, 4].reshape(D, P), kv[:, 3].reshape(D, P), kv[:, 5].reshape(D, P),
        w[:, end:end + REST], twice(kv[:, 0]), twice(kv[:, 1]), w[:, end + REST:]], axis=1)
    w2k = a["nsa_cmp_k_w2"][0]
    arrays = {
        "x": a["x"].reshape(T, D),
        "g_mix": cols(a["ln_mix_g"][0]), "g_ffn": cols(a["ln_ffn_g"][0]), "g_fin": a["ln_final_g"],
        "w_in": w_in,
        "pos": np.stack([pos(a["nsa_cmp_pos_k"][0]), pos(a["nsa_cmp_pos_v"][0])], axis=1),
        "w1k": a["nsa_cmp_k_w1"][0], "w1v": a["nsa_cmp_v_w1"][0],
        "w2k": np.concatenate([w2k, w2k], axis=1), "w2v": a["nsa_cmp_v_w2"][0],
        "q_gain": cols(a["mla_q_norm_g"][0]), "kv_gain": cols(a["mla_kv_norm_g"][0]),
        "w_uq": a["mla_w_uq"][0], "w_ukv": a["mla_w_ukv"][0],
        "w_bn": a["w_branch_nsa"][0], "w_bm": a["w_branch_mla"][0], "w_out": a["w_out"][0],
        "w_query": a["peer_w_query"][0],
        "keys_t": a["peer_sub_keys"][0].transpose(1, 3, 0, 2).reshape(P, H, NK),
        "u_t": a["peer_u"][0].reshape(NK, NK, KT, P).transpose(1, 3, 2, 0).reshape(NK, P, KT * NK),
        "v_t": a["peer_v"][0].reshape(NK, NK, D).transpose(1, 0, 2),
        "t5": a["t5_bias"],
        **constants(),
    }
    arrays = {k: np.ascontiguousarray(val) for k, val in arrays.items()}
    nc = bacc.Bacc("TRN2", target_bir_lowering=False, num_devices=1)
    aps = {k: nc.dram_tensor(k, val.shape, mybir.dt.from_np(val.dtype), kind="ExternalInput").ap()
           for k, val in arrays.items()}
    out = nc.dram_tensor("out", (T, D), mybir.dt.float32, kind="ExternalOutput").ap()
    build(nc, out=out, **aps)
    r = run_bass_kernel_spmd(nc, [arrays], core_ids=[0])
    return r.results[0]["out"].reshape(1, T, D)
```

```python
import math
from contextlib import ExitStack

import numpy as np
import concourse.bass as bass
from concourse import mybir

P = 128
T = 256
NT = T // P
D = 1024
KT = D // P
H = 8
G = 2
R = H // G
DH = 64
CMP_LEN, CMP_STRIDE, CMP_HID = 32, 16, 256
NC = (T - CMP_LEN) // CMP_STRIDE + 1
NC0 = (P - CMP_LEN) // CMP_STRIDE + 1
LP = CMP_LEN // 2
Q_RANK, KV_RANK, NOPE, ROPE = 256, 128, 64, 32
QK = NOPE + ROPE
BUCKETS, MAX_DIST = 32, 128
NK = 128
TOPK = 16
EPS = 1e-6
MASKED = -1e30
Q_COLS = H * DH
REST = 3 * H + Q_RANK + KV_RANK + ROPE
K0 = Q_COLS
V0 = K0 + 2 * P
REST0 = V0 + 2 * P
CK0 = REST0 + REST
CV0 = CK0 + 2 * P
MERGE0 = CV0 + 2 * P
PART_A = CV0
CQ0, CKV0, KR0 = 3 * H, 3 * H + Q_RANK, 3 * H + Q_RANK + KV_RANK
DIST = T + P - 1
RING = 4
TB = 8
HALF = NK // 2
KEEP = P + NK + TOPK + 2 * KT
EARLY = 2 * LP + 3 + NT * ROPE + NT * NC + H + 2 * P + 2 * DH + T
STEPS = HALF // 2
UNROLL = RING // 2
LOOPS = STEPS // UNROLL
KH = KT // 2


def build(nc, x, g_fin, w_in, w1k, w1v, w_uq, w_ukv,
          w_bn, w_bm, w_out, w_query, keys_t, u_t, v_t, t5, one_hot, keep_pack, early_pack, out):
    fp32, u32 = mybir.dt.float32, mybir.dt.uint32
    ACT, ALU, AX = mybir.ActivationFunctionType, mybir.AluOpType, mybir.AxisListType
    ds = bass.ds

    ctx = ExitStack()
    with ctx:
        def sb(name, shape, dt=fp32):
            return ctx.enter_context(nc.sbuf_tensor(name, shape, dt))

        def sem(name):
            return ctx.enter_context(nc.semaphore(name))

        def strided(base, dims):
            return bass.AP(base.tensor, base.offset, [base.ap[0], *dims])

        def bcast(ap, n):
            return ap.unsqueeze(len(ap.shape)).to_broadcast([*ap.shape, n])

        def spread(ap, n):
            return ap.unsqueeze(1).to_broadcast([ap.shape[0], n, *ap.shape[1:]])

        big = sb("big", [P, NK * T])
        keep = sb("keep", [P, KEEP + 16])
        before = ctx.enter_context(ExitStack())

        def early(name, shape, dt=fp32):
            return before.enter_context(nc.sbuf_tensor(name, shape, dt))

        area = early("area", [P, 8192])
        xnT = early("xnT", [P, KT * T])
        h = early("h", [P, NT * D])
        ebuf = early("ebuf", [P, 1024])
        sq = early("sq", [P, 512])
        t5S = early("t5S", [BUCKETS + 1, H])
        work = early("work", [P, 5280])
        early_in = early("early_in", [P, EARLY])
        at = [0]

        def part(base, offset, *dims):
            n = int(np.prod(dims))
            v_ = base[:, offset:offset + n]
            if len(dims) == 2:
                return v_.rearrange("p (a b) -> p a b", b=dims[1])
            if len(dims) == 3:
                return v_.rearrange("p (a b c) -> p a b c", b=dims[1], c=dims[2])
            return v_

        ep = [0]

        def e_(*dims):
            ep[0] += int(np.prod(dims))
            return part(early_in, ep[0] - int(np.prod(dims)), *dims)

        def w_(*dims):
            at[0] += int(np.prod(dims))
            return part(work, at[0] - int(np.prod(dims)), *dims)

        def keep_(n):
            at[0] += n
            return part(keep, at[0] - n, n)

        win = part(big, 0, KT, PART_A)
        wb = part(big, 0, 2, 4, D)
        mgT = part(big, 8192, 2 * KT, T)
        qn = part(big, 12288, NT, H * QK)
        MG = 13824
        mslot = [part(big, MG + s * 2048, KT, 256) for s in range(2)]
        biasM = part(big, 17920, H, T)
        onat = [part(big, 19968 + s * 1024, NT, H * DH) for s in range(2)]
        wuq = part(big, 22016, 2, H * QK)
        wukv = part(big, 22016 + 1536, H * 2 * DH)
        mqT = part(big, 24576, H, T)
        xs = part(big, 24576, NT, D)
        mergedT = part(big, 24576, KT, T)
        mkT = part(big, 26624, H, T)
        Vm = part(big, 28672, NT, H * DH)
        oT = part(big, 29696, 2 * 4, T)
        wcv = part(big, 29696, KT, 2 * P)
        blkT = part(big, 31744, 2, LP, G * NC)
        tmp = part(big, 31744, H * DH)
        w1 = part(area, 0, 2, LP, CMP_HID)
        wo = part(area, 0, KT, D)
        wq = part(big, MG, KT, D)
        keysT = part(big, 12288, H, NK)
        qpT = part(big, 8192, H, T)
        S = part(big, 24576, NT, 2 * H, NK)
        cand = part(big, 28672, H, TOPK * TOPK)
        eq = part(big, 30720, H * TOPK, TOPK)
        topv = part(big, 22016, 2 * H, TOPK)
        topi_f = part(big, 22272, 2 * H, TOPK)
        topi = part(big, 22528, 2 * H, TOPK).bitcast(u32)
        best = [part(big, n, H, TOPK) for n in (22784, 23560)]
        picks = [part(big, 23688 + s * T, NT, P) for s in range(3)]
        pick = part(big, 22912, H, TOPK).bitcast(u32)
        pick_a = part(big, 23040, H * TOPK).bitcast(u32)
        pick_b = part(big, 23168, H * TOPK).bitcast(u32)
        pa_f = part(big, 23296, H * TOPK)
        pb_f = part(big, 23424, H * TOPK)
        gsum = part(big, 23552, H)
        yT = part(big, 0, KT, T)
        ynat = part(big, 2048, NT, D)
        sq_fin = part(big, 4096, D)
        gfin = part(big, 8192, D)
        xnT3 = part(xnT, 0, KT, T)
        h3 = part(h, 0, NT, D)

        identS, iotaS, iota16S = keep_(P), keep_(NK), keep_(TOPK)
        gmix, gffn = keep_(KT), keep_(KT)
        assert at[0] == KEEP
        ssq, rstd = keep_(8), keep_(8)
        posS, qgS, kvgS, cosS, sinS = e_(2, LP), e_(2), e_(1), e_(NT, ROPE // 2), e_(NT, ROPE // 2)
        cmaskS, hmaskS, w2kS, w2vS, causalS = e_(NT, NC), e_(H), e_(2, P), e_(2, DH), e_(T)
        assert ep[0] == EARLY
        at[0] = 0
        qT = w_(R, T)
        kT = w_(2, T)
        Vn = w_(NT, 2 * P)
        rest = w_(NT, REST)
        E = w_(2, 2, T)
        cT = part(work, at[0] - 2 * 2 * T, 3, T)
        hTk, hTv = w_(2, G * NC), w_(2, H * NC)
        kcT = w_(NC)
        vcs = w_(DH)
        Ec = w_(2, H * NC)
        nmx = w_(24, 2)
        csum = w_(NT, H)
        sums = w_(6, H)
        sc = w_(14, H)
        eT = [part(ebuf, s * 512, 512) for s in range(2)]
        kpad = part(ebuf, 0, NT, QK)
        VB = part(sq, 0, H * DH)
        rot = [part(sq, n * P, H, ROPE // 2) for n in range(4)]
        ohS = part(sq, 0, DIST)[0:BUCKETS + 1, :]
        revS = part(ebuf, 512, DIST)[0:H, :]
        hidS = part(ebuf, 512, 2 * CMP_HID)[0:G * NC, :]
        assert at[0] <= 5280, at[0]
        before.close()
        f32r = mybir.dt.float32r
        raw = sb("raw", [P, RING * D])
        hi, lo = sb("hi", [P, 2 * D], f32r), sb("lo", [P, 2 * D], f32r)
        bf16 = mybir.dt.bfloat16
        A_ = sb("A", [P, 2 * TB * NK], bf16)
        B_ = [sb(f"B{n}", [P, 2 * TB * HALF], bf16) for n in range(3)]
        wh, wl = sb("wh", [P, 2 * T], f32r), sb("wl", [P, 2 * T], f32r)
        marks = sb("marks", [P, TB * HALF], bf16)
        gT, g_rest, g_rest2 = (sb(n, [P, T]) for n in ("gT", "g_rest", "g_rest2"))
        i1T, i2T = sb("i1T", [P, T], bf16), sb("i2T", [P, T], bf16)
        gp = [sb(f"g_part{n}", [P, T], bf16) for n in range(3)]
        iotaB = sb("iotaB", [P, NK], bf16)
        xh, xl = sb("xh", [P, KT * T], f32r), sb("xl", [P, KT * T], f32r)
        A = [part(A_, s * TB * NK, TB, NK) for s in range(2)]
        B = [[part(b, s * TB * HALF, TB, HALF) for b in B_] for s in range(2)]
        as_f32 = lambda ap: ap.bitcast(fp32)

        rev_dram = nc.dram_tensor("bias_by_distance", [H, P, DIST], fp32, kind="Internal")

        ps = [ctx.enter_context(nc.psum_tensor(f"ps{n}", [P, 512], fp32)) for n in range(8)]

        x_in, const_in, t5_in, bias_in, rev_out = (sem(n) for n in ("x_in", "const_in", "t5_in", "bias_in", "rev_out"))
        win_in = [sem(f"win_in{n}") for n in range(4)]
        merge_in = [sem(f"merge_in{n}") for n in range(2)]
        w1_in, w2_in, wu_in, wb_in, wo_in, wq_in, keys_in = (
            sem(n) for n in ("w1_in", "w2_in", "wu_in", "wb_in", "wo_in", "wq_in", "keys_in"))
        raw_in = [sem(f"raw_in{n}") for n in range(RING)]
        xh_ready, xl_ready = sem("xh_ready"), sem("xl_ready")
        hi_ready, lo_ready, half_used = sem("hi_ready"), sem("lo_ready"), sem("half_used")
        wh_ready, wl_ready = sem("wh_ready"), sem("wl_ready")
        out_done, gfin_in = sem("out_done"), sem("gfin_in")
        dve_chain, act_chain = sem("dve_chain"), sem("act_chain")
        rev_ps, rev_sb = sem("rev_ps"), sem("rev_sb")
        ssq_ready, ms_ready, root_ready, xs_ready = (sem(n) for n in ("ssq_ready", "ms_ready", "root_ready", "xs_ready"))
        xT_ps, xnT_act, xnT_dve = sem("xT_ps"), sem("xnT_act"), sem("xnT_dve")
        job_done, job_act, job_dve = sem("job_done"), sem("job_act"), sem("job_dve")
        c_ssq, c_ms, c_root, cn_ready, kr_ready, rope_ready = (
            sem(n) for n in ("c_ssq", "c_ms", "c_root", "cn_ready", "kr_ready", "rope_ready"))
        hid_ps, hid_ready, kc_ps, kc_ready, vb_ready = (sem(n) for n in ("hid_ps", "hid_ready", "kc_ps", "kc_ready", "vb_ready"))
        L_done, L_free, max_ready, E_ready = (sem(n) for n in ("L_done", "L_free", "max_ready", "E_ready"))
        cmp_sub, cmp_exp, cmp_ready = sem("cmp_sub"), sem("cmp_exp"), sem("cmp_ready")
        T_done, eT_ready, V_done, O_done, O_free = (sem(n) for n in ("T_done", "eT_ready", "V_done", "O_done", "O_free"))
        b_marked = sem("b_marked")
        hid_act, hT_ps = sem("hid_act"), sem("hT_ps")
        sig_ready = sem("sig_ready")
        half_logits = sem("half_logits")
        gate_ready = sem("gate_ready")
        oT_ps, oT_ready = sem("oT_ps"), sem("oT_ready")
        br_done, br_free, merged_ready = sem("br_done"), sem("br_free"), sem("merged_ready")
        h_ps, h_ready = sem("h_ps"), sem("h_ready")
        qp_done, qp_ready, s_done, s_ready = (sem(n) for n in ("qp_done", "qp_ready", "s_done", "s_ready"))
        best_sub, best_exp, picks_ready, pT_done, pT_ready = (
            sem(n) for n in ("best_sub", "best_exp", "picks_ready", "pT_done", "pT_ready"))
        gelu_done, ab_ready, g_done, w_done = (sem(n) for n in ("gelu_done", "ab_ready", "g_done", "w_done"))
        y_act, y_dve, yn_done, f_ssq, f_ms, f_root, out_ready = (
            sem(n) for n in ("y_act", "y_dve", "yn_done", "f_ssq", "f_ms", "f_root", "out_ready"))

        CONSTS = 2
        (J_Q0, J_Q1, J_K, J_R0, J_R1, J_CK, J_CV, J_V, J_C, J_CR, J_KN) = range(11)
        J_VM = J_KN + 4
        J_QN = J_VM + 2
        J_QT = J_QN + 4
        J_MG = J_QT + 4
        JOBS = J_MG + 8
        DVE_JOBS = (J_CK, J_CV)
        UNITS = 2 + 3 * NT * H // 2

        def unit(n):
            m = n - 2
            return m // 8, m // 4 % 2, m % 4

        def group(n):
            return n if n < 2 else 2 + (n - 2) // 2

        def act_jobs_before(n):
            return sum(j not in DVE_JOBS for j in range(n))

        def dve_jobs_before(n):
            return sum(j in DVE_JOBS for j in range(n))

        def wait_job_evacuated(eng, n):
            if n in DVE_JOBS:
                eng.wait_ge(job_dve, dve_jobs_before(n) + 1)
            else:
                eng.wait_ge(job_act, act_jobs_before(n) + 1)

        def fill_jobs(n):
            if n < 4:
                return [J_QT + n]
            return [J_MG + n - 4] if n < 12 else []

        block = ctx.enter_context(nc.Block())

        @block.sync
        def _(sp):
            w_in_t = w_in.rearrange("(k p) c -> p k c", p=P)
            sp.dma_start(h3, x.rearrange("(i p) d -> p i d", p=P)).then_inc(x_in, 16)
            for n, (a, b) in enumerate(((0, K0), (K0, REST0), (REST0, PART_A))):
                sp.dma_start(win[:, :, a:b], w_in_t[:, :, a:b]).then_inc(win_in[n], 16)
            sp.dma_start(wcv, w_in_t[:, :, CV0:MERGE0]).then_inc(win_in[3], 16)
            sp.dma_start(w1[:, 0], w1k.rearrange("(k p) c -> p k c", p=P)).then_inc(w1_in, 16)
            sp.dma_start(w1[:, 1], w1v.rearrange("(k p) c -> p k c", p=P)).then_inc(w1_in, 16)
            sp.dma_start(wuq, w_uq.rearrange("(k p) c -> p k c", p=P)).then_inc(wu_in, 16)
            sp.dma_start(wukv, w_ukv).then_inc(wu_in, 16)

            def merge_chunk(c):
                if c >= 2:
                    sp.wait_ge(job_done, J_MG + c - 2 + 1)
                lo = MERGE0 + c * 256
                sp.dma_start(mslot[c % 2], w_in_t[:, :, lo:lo + 256]).then_inc(merge_in[c % 2], 16)

            merge_chunk(0)
            merge_chunk(1)
            sp.wait_ge(job_done, J_V + 1)
            sp.dma_start(wb[:, 0], w_bn.rearrange("(k p) c -> p k c", p=P)).then_inc(wb_in, 16)
            sp.dma_start(wb[:, 1], w_bm.rearrange("(k p) c -> p k c", p=P)).then_inc(wb_in, 16)
            sp.wait_ge(hid_ps, 1)
            sp.dma_start(wo, w_out.rearrange("(k p) c -> p k c", p=P)).then_inc(wo_in, 16)
            for c in range(2, 8):
                merge_chunk(c)
            sp.wait_ge(job_done, JOBS)
            sp.dma_start(keysT, keys_t).then_inc(keys_in, 16)
            sp.wait_ge(oT_ps, 4)
            sp.dma_start(wq, w_query.rearrange("(k p) c -> p k c", p=P)).then_inc(wq_in, 16)
            sp.wait_ge(h_ps, 4)

            def load(src, slot, n):
                sp.dma_start(raw[:, slot * D:(slot + 1) * D], src[n]).then_inc(raw_in[slot], 16)

            for s in range(RING):
                load(u_t, s, s)
            with sp.Fori(1, NK // RING) as it:
                for s in range(RING):
                    sp.wait_ge(lo_ready, (it * RING + s - RING + 1) * 2)
                    load(u_t, s, it * RING + s)
            with sp.Fori(0, NK // RING) as it:
                for s in range(RING):
                    sp.wait_ge(lo_ready, (it * RING + s + NK - RING + 1) * 2)
                    load(v_t, s, it * RING + s)
            for i in range(NT):
                sp.wait_ge(out_ready, i + 1)
                sp.dma_start(out[i * P:(i + 1) * P, :], ynat[:, i]).then_inc(out_done, 16)
            sp.wait_ge(out_done, NT * 16)

        @block.gpsimd
        def _(pool):
            pool.dma_start(t5S[:, :], t5).then_inc(t5_in, 16)
            pool.dma_start(ohS, one_hot).then_inc(t5_in, 16)
            pool.wait_ge(rev_sb, 1)
            pool.dma_start(rev_dram.ap(), spread(revS, P)).then_inc(rev_out, 16)
            pool.wait_ge(rev_out, 16)
            pool.dma_start(biasM, bass.AP(rev_dram, P - 1, [[DIST - 1, P], [P * DIST, H], [1, T]])).then_inc(bias_in, 16)
            with pool.Fori(0, 2 * NK // RING) as it:
                for s in range(RING):
                    for f in range(2):
                        pool.wait_ge(hi_ready, (it * RING + s) * 2 + f + 1)
                        a, b = s * D + f * KH * P, s % 2 * D + f * KH * P
                        nc.gpsimd.tensor_tensor(lo[:, b:b + KH * P], raw[:, a:a + KH * P],
                                                as_f32(hi[:, b:b + KH * P]), ALU.subtract).then_inc(lo_ready, 1)
            pool.wait_ge(half_used, 4 * NK)
            pool.dma_start(gfin, g_fin.partition_broadcast(P)).then_inc(gfin_in, 16)

        @block.scalar
        def _(act):
            act.dma_start(keep[:, 0:KEEP], keep_pack).then_inc(const_in, 16)
            act.dma_start(early_in[:, :], early_pack).then_inc(const_in, 16)
            chain = [0]

            def link(ins):
                chain[0] += 1
                ins.then_inc(act_chain, 1)
                act.wait_ge(act_chain, chain[0])

            act.wait_ge(x_in, 16)
            for i in range(NT):
                link(nc.scalar.activation(xs[:, i], h3[:, i], ACT.Square, accum_out=ssq[:, i:i + 1]))
            nc.scalar.copy(rstd[:, 0:NT], ssq[:, 0:NT]).then_inc(ssq_ready, 1)
            act.wait_ge(ms_ready, 1)
            nc.scalar.activation(rstd[:, 0:NT], ssq[:, 0:NT], ACT.Sqrt).then_inc(root_ready, 1)

            def gained_transposes(first, gain, done):
                act.wait_ge(const_in, CONSTS * 16)
                for q in (0, 2):
                    act.wait_ge(xT_ps, first + q + 1)
                    for m in range(4):
                        k = q % 2 * 4 + m
                        last = nc.scalar.activation(xnT3[:, k, (q // 2) * P:(q // 2 + 1) * P],
                                                    ps[2 + q][:, m * P:(m + 1) * P], ACT.Copy,
                                                    scale=gain[:, k:k + 1])
                    last.then_inc(xnT_act, 1)

            act.wait_ge(rev_ps, 1)
            nc.scalar.copy(revS, ps[6][0:H, 0:DIST]).then_inc(rev_sb, 1)
            gained_transposes(0, gmix, 0)

            def evacuate(n):
                b = ps[n % 2]
                act.wait_ge(job_done, n + 1)
                if n in (J_Q0, J_Q1):
                    last = nc.scalar.copy(qT[:, 2 * n:2 * n + 2], b[:, :].rearrange("p (a t) -> p a t", t=T))
                elif n == J_K:
                    last = nc.scalar.copy(kT, b[:, :].rearrange("p (a t) -> p a t", t=T))
                elif n in (J_R0, J_R1):
                    last = nc.scalar.copy(rest[:, n - J_R0], b[:, 0:REST])
                elif n == J_V:
                    last = nc.scalar.copy(Vn, b[:, :].rearrange("p (i c) -> p i c", i=NT))
                elif n == J_C:
                    for k in range(2):
                        last = nc.scalar.activation(cT[:, k], b[:, k * T:(k + 1) * T], ACT.Copy, scale=qgS[:, k:k + 1])
                elif n == J_CR:
                    nc.scalar.activation(cT[:, 2], b[:, 0:T], ACT.Copy, scale=kvgS[:, 0:1])
                    last = nc.scalar.copy(mkT[NOPE:QK], spread(b[NOPE:QK, T:2 * T], H))
                elif n < J_VM:
                    k = 2 * (n - J_KN)
                    last = nc.scalar.copy(mkT[0:NOPE, k:k + 2], b[0:NOPE, :].rearrange("p (a t) -> p a t", t=T))
                elif n < J_QN:
                    last = nc.scalar.copy(Vm[:, n - J_VM], b[:, :])
                elif n < J_QT:
                    i, half = divmod(n - J_QN, 2)
                    last = nc.scalar.copy(qn[:, i, half * 384:(half + 1) * 384], b[:, 0:384])
                elif n < J_MG:
                    i, quad = divmod(n - J_QT, 2)
                    last = nc.scalar.copy(mqT[0:QK, quad * 4:quad * 4 + 4, i * P:(i + 1) * P],
                                          b[0:QK, :].rearrange("p (a t) -> p a t", t=P))
                else:
                    c = n - J_MG
                    last = nc.scalar.copy(mgT[:, 2 * c:2 * c + 2], b[:, :].rearrange("p (a t) -> p a t", t=T))
                last.then_inc(job_act, 1)
                if n == J_R1:
                    act.wait_ge(job_act, act_jobs_before(J_R1) + 1)
                    for i in range(NT):
                        nc.scalar.activation(sq[:, 0:Q_RANK], rest[:, i, CQ0:CKV0], ACT.Square,
                                             accum_out=ssq[:, 2 + i:3 + i])
                        link(nc.scalar.activation(sq[:, Q_RANK:Q_RANK + KV_RANK], rest[:, i, CKV0:KR0], ACT.Square,
                                                  accum_out=ssq[:, 4 + i:5 + i]))
                    nc.scalar.copy(rstd[:, 2:6], ssq[:, 2:6]).then_inc(c_ssq, 1)
                if n == J_V:
                    act.wait_ge(c_ms, 1)
                    nc.scalar.activation(rstd[:, 2:6], ssq[:, 2:6], ACT.Sqrt).then_inc(c_root, 1)

            for n in range(J_KN):
                if n not in DVE_JOBS:
                    evacuate(n)
            act.wait_ge(hid_ps, 1)
            act.wait_ge(rev_out, 16)
            nc.scalar.activation(hidS, ps[6][0:G * NC, :], ACT.Gelu).then_inc(hid_act, 1)
            for n in range(J_KN, J_QT):
                evacuate(n)
            act.wait_ge(hT_ps, 1)
            for hid in range(2):
                nc.scalar.copy(hTk[:, hid], ps[7][:, hid * 32:hid * 32 + G * NC])
                src = ps[7][:, (2 + hid) * 32:(2 + hid) * 32 + G * NC].rearrange("p (g c) -> p g c", g=G)
                last = nc.scalar.copy(hTv[:, hid].rearrange("p (g r c) -> p g r c", g=G, r=R),
                                      src.unsqueeze(2).to_broadcast([P, G, R, NC]))
            last.then_inc(hid_ready, 1)
            act.wait_ge(kc_ps, 1)
            for g in range(G):
                nc.scalar.copy(kcT[g * DH:(g + 1) * DH, :], ps[6][g * DH:(g + 1) * DH, g * NC:(g + 1) * NC])
            nc.scalar.copy(vcs[0:H * NC, :], ps[6][0:H * NC, 64:64 + DH]).then_inc(kc_ready, 1)
            for i in range(NT):
                last = nc.scalar.activation(rest[:, i, 0:3 * H], rest[:, i, 0:3 * H], ACT.Exp, scale=-1.0)
            last.then_inc(gate_ready, 1)

            for n in range(UNITS):
                if n < 2:
                    act.wait_ge(cmp_sub, n + 1)
                    ncv = NC0 if n == 0 else NC
                    e = Ec[:, n].rearrange("p (h c) -> p h c", c=NC)[:, :, 0:ncv]
                    nc.scalar.activation(e, e, ACT.Exp).then_inc(cmp_exp, 1)
                else:
                    br, i, pr = unit(n)
                    act.wait_ge(max_ready, n - 1)
                    for j in range(2):
                        e = E[:, n % 2, j, 0:(i + 1) * P]
                        last = nc.scalar.activation(e, e, ACT.Exp, bias=nmx[:, n - 2, j:j + 1],
                                                    accum_out=sums[:, br * 2 + i, 2 * pr + j:2 * pr + j + 1])
                    last.then_inc(E_ready, 1)
                act.wait_ge(T_done, n + 1)
                if n >= 2:
                    act.wait_ge(V_done, n - 1)
                if n < 2:
                    nc.scalar.copy(eT[n % 2][0:H * NC, 0:P], ps[4 + n % 2][0:H * NC, 0:P]).then_inc(eT_ready, 1)
                else:
                    w = 2 * (i + 1) * P
                    nc.scalar.copy(eT[n % 2][:, 0:w], ps[4 + n % 2][:, 0:w]).then_inc(eT_ready, 1)
                for j in fill_jobs(n):
                    evacuate(j)

            for q in range(4):
                act.wait_ge(oT_ps, q + 1)
                nc.scalar.copy(oT[:, (q // 2) * 4:(q // 2) * 4 + 4, (q % 2) * P:(q % 2 + 1) * P],
                               ps[q][:, :].rearrange("p (a t) -> p a t", t=P)).then_inc(oT_ready, 1)
            for c in range(KT):
                m = strided(mgT[:, c, 0:1], [[KT * T, 2], [1, T]])
                if c == 0:
                    act.wait_ge(job_act, act_jobs_before(JOBS))
                nc.scalar.activation(m, m, ACT.Sigmoid).then_inc(sig_ready, 1)
            act.wait_ge(h_ready, 4)
            for i in range(NT):
                link(nc.scalar.activation(S[:, i].rearrange("p a b -> p (a b)")[:, 0:D], h3[:, i], ACT.Square, accum_out=ssq[:, i:i + 1]))
            nc.scalar.copy(rstd[:, 0:NT], ssq[:, 0:NT]).then_inc(ssq_ready, 1)
            act.wait_ge(ms_ready, 2)
            nc.scalar.activation(rstd[:, 0:NT], ssq[:, 0:NT], ACT.Sqrt).then_inc(root_ready, 1)
            gained_transposes(4, gffn, 2)
            for j in range(4):
                act.wait_ge(qp_done, j + 1)
                nc.scalar.copy(qpT[:, 2 * j:2 * j + 2], ps[j][:, :].rearrange("p (a t) -> p a t", t=T)).then_inc(qp_ready, 1)
            for q in range(2 * 4):
                i, f = divmod(q, 4)
                act.wait_ge(s_done, q + 1)
                nc.scalar.copy(S[:, i, 4 * f:4 * f + 4],
                               ps[(q + 4) % 8][:, :].rearrange("p (a t) -> p a t", t=NK)).then_inc(s_ready, 1)

            nc.scalar.copy(xh[:, :], xnT[:, :]).then_inc(xh_ready, 1)

            def split(c, slot, it, early_=False):
                act.wait_ge(raw_in[slot], (it + 1) * 16)
                for f in range(2):
                    if not early_:
                        act.wait_ge(half_used, c * 2 + (f - 3))
                    a, b = slot * D + f * KH * P, slot % 2 * D + f * KH * P
                    nc.scalar.copy(hi[:, b:b + KH * P], raw[:, a:a + KH * P]).then_inc(hi_ready, 1)

            def u_stage(it):
                for s in range(RING):
                    c = it * RING + s
                    split(c + 2, (s + 2) % RING, it + (s + 2) // RING)
                    act.wait_ge(half_used, c * 2 + 2)
                    nc.scalar.activation(big[:, ds(c * T, T)], ps[s % 2][:, 0:T], ACT.Gelu).then_inc(gelu_done, 1)

            def split_w(c, s):
                nc.scalar.copy(wh[:, s % 2 * T:(s % 2 + 1) * T], big[:, ds(c * T, T)]).then_inc(wh_ready, 1)

            def v_stage(it, last_=False):
                for s in range(RING):
                    c = it * RING + s
                    if last_ and s >= 2:
                        break
                    split(c + (NK + 2), (s + 2) % RING, it + (s + 2) // RING + NK // RING)
                    act.wait_ge(half_used, c * 2 + (2 * NK + 2))
                    split_w(c + 2, s)

            split(0, 0, 0, True)
            split(1, 1, 0, True)
            with act.Fori(0, 13) as it:
                u_stage(it)
            for i in range(NT):
                act.wait_ge(best_sub, i + 1)
                nc.scalar.activation(best[i], best[i], ACT.Exp).then_inc(best_exp, 1)
            with act.Fori(13, LOOPS) as it:
                u_stage(it)
            act.wait_ge(pT_done, 1)
            for s, dst in enumerate((i1T, i2T, gT)):
                last = nc.scalar.copy(dst[:, :], ps[2 + s // 2][:, (s % 2) * T:(s % 2 + 1) * T])
            last.then_inc(pT_ready, 1)
            with act.Fori(LOOPS, 2 * LOOPS) as it:
                u_stage(it)
            act.wait_ge(w_done, STEPS)
            split_w(0, 0)
            split_w(1, 1)
            with act.Fori(0, LOOPS - 1) as it:
                v_stage(it)
            for s in range(RING):
                c = (LOOPS - 1) * RING + s
                split(c + NK + 2, (s + 2) % RING, LOOPS - 1 + (s + 2) // RING + NK // RING)
                act.wait_ge(half_used, c * 2 + 2 * NK + 2)
                if s == 2:
                    act.wait_ge(w_done, 2 * STEPS)
                split_w(c + 2, s)
            with act.Fori(LOOPS, 2 * LOOPS - 1) as it:
                v_stage(it)
            v_stage(2 * LOOPS - 1, True)

            act.wait_ge(half_used, 4 * NK)
            for q in (0, 2):
                last = nc.scalar.copy(yT[:, 2 * q:2 * q + 2], ps[4 + q][:, :].rearrange("p (a t) -> p a t", t=T))
            last.then_inc(y_act, 1)
            for i in range(NT):
                for f in range(2):
                    act.wait_ge(yn_done, 2 * i + f + 1)
                    link(nc.scalar.activation(sq_fin[:, f * 512:(f + 1) * 512], ps[2 * i + f][:, :], ACT.Square,
                                              accum_out=ssq[:, 2 * i + f:2 * i + f + 1]))
            nc.scalar.copy(rstd[:, 0:4], ssq[:, 0:4]).then_inc(f_ssq, 1)
            act.wait_ge(f_ms, 1)
            nc.scalar.activation(rstd[:, 0:NT], ssq[:, 4:4 + NT], ACT.Sqrt).then_inc(f_root, 1)

        @block.vector
        def _(dve):
            chain = [0]
            vec = nc.vector

            def link(ins):
                chain[0] += 1
                ins.then_inc(dve_chain, 1)
                dve.wait_ge(dve_chain, chain[0])

            def self_wait(ins, sem_, count):
                ins.then_inc(sem_, 1)
                dve.wait_ge(sem_, count)

            def norm_scale(turn):
                dve.wait_ge(ssq_ready, turn + 1)
                vec.tensor_scalar(ssq[:, 0:NT], rstd[:, 0:NT], 1.0 / D, EPS, ALU.mult, ALU.add).then_inc(ms_ready, 1)
                dve.wait_ge(root_ready, turn + 1)
                link(vec.reciprocal(ssq[:, 0:NT], rstd[:, 0:NT]))
                for i in range(NT):
                    vec.tensor_scalar(xs[:, i], h3[:, i], ssq[:, i:i + 1], None, ALU.mult).then_inc(xs_ready, 1)

            def gained_transposes(first, gain):
                for q in (1, 3):
                    dve.wait_ge(xT_ps, first + q + 1)
                    for m in range(4):
                        k = q % 2 * 4 + m
                        last = vec.tensor_scalar(xnT3[:, k, (q // 2) * P:(q // 2 + 1) * P],
                                                 ps[2 + q][:, m * P:(m + 1) * P], gain[:, k:k + 1], None, ALU.mult)
                    last.then_inc(xnT_dve, 1)

            dve.wait_ge(x_in, 16)
            norm_scale(0)
            vec.memset(kpad, 0.0)
            vec.memset(Ec, 0.0)
            dve.wait_ge(const_in, CONSTS * 16)
            gained_transposes(0, gmix)
            dve.wait_ge(c_ssq, 1)
            vec.tensor_scalar(ssq[:, 2:4], rstd[:, 2:4], 1.0 / Q_RANK, EPS, ALU.mult, ALU.add)
            vec.tensor_scalar(ssq[:, 4:6], rstd[:, 4:6], 1.0 / KV_RANK, EPS, ALU.mult, ALU.add).then_inc(c_ms, 1)
            for n, jb in enumerate(DVE_JOBS):
                dve.wait_ge(job_done, jb + 1)
                for par in range(2):
                    rows = slice(par * DH, (par + 1) * DH)
                    for g in range(G):
                        o = g * T + par
                        last = vec.tensor_tensor(
                            blkT[rows, n, :, g * NC:(g + 1) * NC],
                            strided(ps[jb % 2][rows, o:o + 1], [[2, LP], [CMP_STRIDE, NC]]),
                            bcast(posS[rows, n], NC), ALU.add)
                last.then_inc(job_dve, 1)
            dve.wait_ge(c_root, 1)
            link(vec.reciprocal(ssq[:, 2:6], rstd[:, 2:6]))
            for i in range(NT):
                vec.tensor_scalar(rest[:, i, CQ0:CKV0], rest[:, i, CQ0:CKV0], ssq[:, 2 + i:3 + i], None, ALU.mult)
                last = vec.tensor_scalar(rest[:, i, CKV0:KR0], rest[:, i, CKV0:KR0], ssq[:, 4 + i:5 + i], None, ALU.mult)
            last.then_inc(cn_ready, 1)

            def rotate(x1, x2, c, s, heads, y1, y2):
                t = [r[:, 0:heads] for r in rot]
                vec.tensor_tensor(t[0], x1, c, ALU.mult)
                vec.tensor_tensor(t[1], x2, s, ALU.mult)
                vec.tensor_tensor(t[2], x2, c, ALU.mult)
                link(vec.tensor_tensor(t[3], x1, s, ALU.mult))
                vec.tensor_tensor(y1, t[0], t[1], ALU.subtract)
                return vec.tensor_tensor(y2, t[2], t[3], ALU.add)

            HR = ROPE // 2
            last = rotate(rest[:, :, KR0:KR0 + HR], rest[:, :, KR0 + HR:KR0 + ROPE], cosS, sinS, NT,
                          kpad[:, :, NOPE:NOPE + HR], kpad[:, :, NOPE + HR:QK])
            last.then_inc(kr_ready, 1)
            for i in range(NT):
                dve.wait_ge(job_act, act_jobs_before(J_QN + 2 * i + 1) + 1)
                q = qn[:, i].rearrange("p (h c) -> p h c", c=QK)
                last = rotate(q[:, :, NOPE:NOPE + HR], q[:, :, NOPE + HR:QK], spread(cosS[:, i], H), spread(sinS[:, i], H),
                              H, q[:, :, NOPE:NOPE + HR], q[:, :, NOPE + HR:QK])
                self_wait(last, rope_ready, i + 1)
            dve.wait_ge(kc_ready, 1)
            vec.tensor_tensor(VB[0:H * NC, :].rearrange("p (h d) -> p h d", d=DH), spread(vcs[0:H * NC, :], H),
                              bcast(hmaskS[0:H * NC, :], DH), ALU.mult).then_inc(vb_ready, 1)
            dve.wait_ge(bias_in, 16)
            dve.wait_ge(gate_ready, 1)
            gates = rest[:, :, 0:3 * H]
            link(vec.tensor_scalar(gates, gates, 1.0, None, ALU.add))
            link(vec.reciprocal(gates, gates))

            def combine(gr):
                dve.wait_ge(O_done, gr + 1)
                bank = ps[6 + gr % 2]
                if gr < 2:
                    i, br, hs, dst = gr, 0, slice(0, H), onat[0]
                    link(vec.reciprocal(sc[:, gr], csum[:, i]))
                    o = bank[:, :].rearrange("p (h d) -> p h d", d=DH)
                else:
                    br, i, quad = (gr - 2) // 4, gr // 2 % 2 ^ 1, gr % 2
                    hs, dst = slice(4 * quad, 4 * quad + 4), onat[br // 2]
                    link(vec.reciprocal(sc[:, gr, hs], sums[:, br * 2 + i, hs]))
                    o = (strided(bank[:, quad * DH:quad * DH + 1], [[P, 4], [1, DH]]) if br < 2 else
                         strided(bank[:, 0:1], [[2 * P, 2], [P + DH, 2], [1, DH]]))
                w = sc[:, gr, hs]
                if br < 2:
                    gate = rest[:, i, 0:3 * H].rearrange("p (h b) -> p b h", b=3)
                    link(vec.tensor_tensor(w, w, gate[:, 0 if gr < 2 else br + 1, hs], ALU.mult))
                d = dst[:, i, hs.start * DH:hs.stop * DH]
                nh = hs.stop - hs.start
                if gr < 2 or br == 2:
                    shape = (lambda z: z.rearrange("p (a b d) -> p a b d", b=2, d=DH)) if br == 2 else (
                        lambda z: z.rearrange("p (h d) -> p h d", d=DH))
                    wb_ = bcast(w.rearrange("p (a b) -> p a b", b=2) if br == 2 else w, DH)
                    self_wait(vec.tensor_tensor(shape(d), o, wb_, ALU.mult), O_free, gr + 1)
                else:
                    t = tmp[:, 0:nh * DH]
                    self_wait(vec.tensor_tensor(t.rearrange("p (h d) -> p h d", d=DH), o, bcast(w, DH), ALU.mult),
                              O_free, gr + 1)
                    link(vec.tensor_tensor(d, d, t, ALU.add))

            for n in range(2):
                ncv = NC0 if n == 0 else NC
                e = Ec[:, n].rearrange("p (h c) -> p h c", c=NC)[:, :, 0:ncv]
                k0 = CMP_LEN - 1 + (P if n == 0 else 0)
                dve.wait_ge(L_done, n + 1)
                self_wait(vec.scalar_tensor_tensor(
                    e, ps[2 + n][:, 0:H * 16].rearrange("p (h c) -> p h c", c=16)[:, :, 0:ncv], DH ** -0.5,
                    strided(biasM[:, 0, k0:k0 + 1], [[T, H], [CMP_STRIDE, ncv]]), ALU.mult, ALU.add), L_free, n + 1)
                link(vec.tensor_reduce(csum[:, n], e, AX.X, ALU.max))
                vec.tensor_tensor(e, e, bcast(csum[:, n], ncv), ALU.subtract).then_inc(cmp_sub, 1)
                dve.wait_ge(cmp_exp, n + 1)
                link(vec.tensor_tensor(e, e, spread(cmaskS[:, n, 0:ncv], H), ALU.mult))
                link(vec.tensor_reduce(csum[:, n], e, AX.X, ALU.add))
                self_wait(vec.tensor_scalar(csum[:, n], csum[:, n], 1e-30, None, ALU.max), cmp_ready, n + 1)

            for n in range(2, UNITS):
                br, i, pr = unit(n)
                w = (i + 1) * P
                e = E[:, n % 2, :, 0:w]
                lg = ps[2 + n % 2][:, :].rearrange("p (a k) -> p a k", a=2)[:, :, 0:w]
                bias = biasM[:, 2 * pr:2 * pr + 2, T - w:T] if br < 2 else spread(causalS[:, T - w:T], 2)
                scale = DH ** -0.5 if br < 2 else QK ** -0.5
                dve.wait_ge(L_done, n + 1)
                dve.wait_ge(T_done, n - 1)
                self_wait(vec.scalar_tensor_tensor(e, lg, scale, bias, ALU.mult, ALU.add), L_free, n + 1)
                vec.tensor_reduce(nmx[:, n - 2], e, AX.X, ALU.max, negate=True).then_inc(max_ready, 1)
                if n in (3, 4):
                    combine(n - 3)
                if n >= 5 and n % 2:
                    combine(2 + (n - 5) // 2)
            combine(13)

            for c in range(KT):
                dve.wait_ge(br_done, c + 1)
                dve.wait_ge(sig_ready, c + 1)
                b = ps[c % 2 + 4]
                t2 = strided(tmp[:, 0:1], [[T, 2], [1, T]])
                self_wait(vec.tensor_tensor(t2, b[:, :].rearrange("p (a t) -> p a t", t=T),
                                            strided(mgT[:, c, 0:1], [[KT * T, 2], [1, T]]), ALU.mult), br_free, c + 1)
                self_wait(vec.tensor_tensor(mergedT[:, c], tmp[:, 0:T], tmp[:, T:2 * T], ALU.add), merged_ready, c + 1)
            for q in range(4):
                i, f = divmod(q, 2)
                dve.wait_ge(h_ps, q + 1)
                hh = h3[:, i, f * 512:(f + 1) * 512]
                last = vec.tensor_tensor(hh, hh, ps[q][:, :], ALU.add).then_inc(h_ready, 1)
            dve.wait_ge(h_ready, 4)
            norm_scale(1)
            gained_transposes(4, gffn)

            dve.wait_ge(xh_ready, 1)
            vec.tensor_tensor(xl[:, :], xnT[:, :], as_f32(xh[:, :]), ALU.subtract).then_inc(xl_ready, 1)

            for i in range(NT):
                dve.wait_ge(s_ready, 4 * (i + 1))
                for m in range(2 * H):
                    s = S[:, i, m]
                    link(vec.max(topv[:, m, 0:8], s))
                    vec.max_index(topi[:, m, 0:8], topv[:, m, 0:8], s)
                    link(vec.match_replace(s, topv[:, m, 0:8], s, -3e38))
                    link(vec.max(topv[:, m, 8:16], s))
                    vec.max_index(topi[:, m, 8:16], topv[:, m, 8:16], s)
                link(vec.tensor_tensor(cand.rearrange("p h (a b) -> p h a b", b=TOPK), bcast(topv[:, 0:H], TOPK),
                                       topv[:, H:2 * H].unsqueeze(2).to_broadcast([P, H, TOPK, TOPK]), ALU.add))
                link(vec.tensor_copy(topi_f, topi))
                for m in range(H):
                    c = cand[:, m]
                    link(vec.max(best[i][:, m, 0:8], c))
                    vec.max_index(pick[:, m, 0:8], best[i][:, m, 0:8], c)
                    link(vec.match_replace(c, best[i][:, m, 0:8], c, -3e38))
                    link(vec.max(best[i][:, m, 8:16], c))
                    link(vec.max_index(pick[:, m, 8:16], best[i][:, m, 8:16], c))
                link(vec.tensor_copy(gsum, best[i][:, :, 0]))
                vec.tensor_tensor(best[i], best[i], bcast(gsum, TOPK), ALU.subtract).then_inc(best_sub, 1)
                pf = pick.rearrange("p h k -> p (h k)")
                vec.tensor_scalar(pick_a, pf, 4, None, ALU.logical_shift_right)
                link(vec.tensor_scalar(pick_b, pf, TOPK - 1, None, ALU.bitwise_and))
                vec.tensor_copy(pa_f, pick_a)
                link(vec.tensor_copy(pb_f, pick_b))
                for side, pos_f in enumerate((pa_f, pb_f)):
                    link(vec.tensor_tensor(eq, bcast(pos_f, TOPK), spread(iota16S, H * TOPK), ALU.is_equal))
                    eq4 = eq.rearrange("p (h k) a -> p h k a", h=H)
                    link(vec.tensor_tensor(eq4, eq4, topi_f[:, side * H:(side + 1) * H].unsqueeze(2).to_broadcast(
                        [P, H, TOPK, TOPK]), ALU.mult))
                    link(vec.tensor_reduce(picks[side][:, i], eq, AX.X, ALU.add))
            for i in range(NT):
                dve.wait_ge(best_exp, i + 1)
                link(vec.tensor_reduce(gsum, best[i], AX.X, ALU.add))
                link(vec.reciprocal(gsum, gsum))
                self_wait(vec.tensor_tensor(picks[2][:, i].rearrange("p (h k) -> p h k", h=H), best[i], bcast(gsum, TOPK),
                                            ALU.mult), picks_ready, i + 1)

            bigT = part(big, 0, NK, T).rearrange("p c t -> p t c")
            dve.wait_ge(pT_ready, 1)
            vec.tensor_copy(iotaB[:, :], iotaS)
            link(vec.tensor_copy(gp[0][:, :], gT[:, :]))
            link(vec.tensor_tensor(g_rest[:, :], gT[:, :], gp[0][:, :], ALU.subtract))
            link(vec.tensor_copy(gp[1][:, :], g_rest[:, :]))
            link(vec.tensor_tensor(g_rest2[:, :], g_rest[:, :], gp[1][:, :], ALU.subtract))
            link(vec.tensor_copy(gp[2][:, :], g_rest2[:, :]))

            def spread_picks(it, s, half):
                n = it * UNROLL + s
                tok = ds(n * TB, TB)
                a, b = A[s % 2], part(marks, 0, TB, HALF)
                if not (half == 0 and isinstance(it, int) and it == 0 and s == 0):
                    dve.wait_ge(ab_ready, n + half * STEPS)
                vec.tensor_tensor(a, spread(iotaB[:, :], TB), bcast(i1T[:, tok], NK), ALU.is_equal)
                vec.tensor_tensor(b, spread(iotaB[:, half * HALF:(half + 1) * HALF], TB),
                                  bcast(i2T[:, tok], HALF), ALU.is_equal).then_inc(b_marked, 1)
                dve.wait_ge(b_marked, n + (half * STEPS + 1))
                for m in range(3):
                    last = vec.tensor_tensor(B[s % 2][m], b, bcast(gp[m][:, tok], HALF), ALU.mult)
                last.then_inc(ab_ready, 1)

            def weigh(it, s, half):
                n = it * UNROLL + s
                w = bigT[:, ds(n * TB, TB), half * HALF:(half + 1) * HALF]
                dve.wait_ge(g_done, n + (half * STEPS + 1))
                vec.tensor_tensor(w, ps[2 + s % 2][:, :].rearrange("p (t c) -> p t c", t=TB), w, ALU.mult).then_inc(w_done, 1)

            def rest_of_w(c, s):
                dve.wait_ge(wh_ready, c + 1)
                b = slice(s % 2 * T, (s % 2 + 1) * T)
                vec.tensor_tensor(wl[:, b], big[:, ds(c * T, T)], as_f32(wh[:, b]), ALU.subtract).then_inc(wl_ready, 1)

            dve.wait_ge(gelu_done, HALF)
            spread_picks(0, 0, 0)
            with dve.Fori(0, LOOPS - 1) as it:
                for s in range(UNROLL):
                    spread_picks(it + (s + 1) // UNROLL, (s + 1) % UNROLL, 0)
                    weigh(it, s, 0)
            for s in range(UNROLL):
                if s + 1 < UNROLL:
                    spread_picks(LOOPS - 1, s + 1, 0)
                weigh(LOOPS - 1, s, 0)
            rest_of_w(0, 0)
            rest_of_w(1, 1)
            dve.wait_ge(gelu_done, 2 * HALF)
            spread_picks(0, 0, 1)
            spread_picks(0, 1, 1)
            rest_of_w(2, 0)
            rest_of_w(3, 1)

            def second_half(it, s):
                c = (it * UNROLL + s) * 2
                weigh(it, s, 1)
                rest_of_w(c + 4, 0)
                spread_picks(it + 1, s, 1)
                rest_of_w(c + 5, 1)

            with dve.Fori(0, LOOPS - 1) as it:
                for s in range(UNROLL):
                    second_half(it, s)
            for s in range(UNROLL):
                weigh(LOOPS - 1, s, 1)
            with dve.Fori(HALF // 2, NK // 2) as it:
                for j in range(2):
                    rest_of_w(it * 2 + j, j)

            dve.wait_ge(half_used, 4 * NK)
            for q in (1, 3):
                last = vec.tensor_copy(yT[:, 2 * q:2 * q + 2], ps[4 + q][:, :].rearrange("p (a t) -> p a t", t=T))
            last.then_inc(y_dve, 1)
            dve.wait_ge(f_ssq, 1)
            link(vec.tensor_tensor(ssq[:, 4:6], strided(rstd[:, 0:1], [[2, NT]]), strided(rstd[:, 1:2], [[2, NT]]), ALU.add))
            vec.tensor_scalar(ssq[:, 4:6], ssq[:, 4:6], 1.0 / D, EPS, ALU.mult, ALU.add).then_inc(f_ms, 1)
            dve.wait_ge(f_root, 1)
            link(vec.reciprocal(ssq[:, 0:NT], rstd[:, 0:NT]))
            dve.wait_ge(gfin_in, 16)
            for i in range(NT):
                for f in range(2):
                    c = slice(f * 512, (f + 1) * 512)
                    last = vec.scalar_tensor_tensor(ynat[:, i, c], ps[2 * i + f][:, :], ssq[:, i:i + 1], gfin[:, c],
                                                    ALU.mult, ALU.mult)
                last.then_inc(out_ready, 1)

        @block.tensor
        def _(pe):
            def mm(o, lhsT, rhs, start=True, stop=True, **kw):
                return nc.tensor.matmul(o, lhsT, rhs, start=start, stop=stop, **kw)

            def transpose(o, a):
                return nc.tensor.transpose(o, a, identS[0:a.shape[0], 0:a.shape[0]])

            pe.wait_ge(t5_in, 32)
            mm(ps[6][0:H, 0:DIST], t5S[:, :], ohS).then_inc(rev_ps, 1)

            def transpose_xs(turn):
                pe.wait_ge(const_in, CONSTS * 16)
                for q in range(4):
                    i = q // 2
                    pe.wait_ge(xs_ready, turn * NT + i + 1)
                    for m in range(4):
                        k = q % 2 * 4 + m
                        last = transpose(ps[2 + q][:, m * P:(m + 1) * P], xs[:, i, k * P:(k + 1) * P])
                    last.then_inc(xT_ps, 1)

            transpose_xs(0)
            pe.wait_ge(xnT_act, 2)
            pe.wait_ge(xnT_dve, 2)

            def project(o, weight, n=KT, rhs=xnT3):
                for k in range(n):
                    last = mm(o, weight(k), rhs[:, k], start=k == 0, stop=k == n - 1)
                return last

            def job(n):
                if n >= 2:
                    wait_job_evacuated(pe, n - 2)
                b = ps[n % 2]
                if n in (J_Q0, J_Q1):
                    pe.wait_ge(win_in[0], 16)
                    for j in range(2):
                        r = 2 * n + j
                        last = project(b[:, j * T:(j + 1) * T],
                                       lambda k: win[:, k, r * P:(r + 1) * P])
                elif n == J_K:
                    pe.wait_ge(win_in[1], 16)
                    for j in range(2):
                        c = K0 + j * P
                        last = project(b[:, j * T:(j + 1) * T], lambda k: win[:, k, c:c + P])
                elif n in (J_CK, J_CV):
                    pe.wait_ge(win_in[2 + n - J_CK], 16)
                    src, lo = (win, CK0) if n == J_CK else (wcv, 0)
                    for g in range(G):
                        c = lo + g * P
                        last = project(b[:, g * T:(g + 1) * T], lambda k: src[:, k, c:c + P])
                elif n == J_V:
                    for i in range(NT):
                        for k in range(KT):
                            last = mm(b[:, i * T:(i + 1) * T], xnT3[:, k, i * P:(i + 1) * P], win[:, k, V0:REST0],
                                      start=k == 0, stop=k == KT - 1)
                elif n in (J_R0, J_R1):
                    pe.wait_ge(win_in[2], 16)
                    i = n - J_R0
                    for k in range(KT):
                        last = mm(b[:, 0:REST], xnT3[:, k, i * P:(i + 1) * P], win[:, k, REST0:CK0],
                                  start=k == 0, stop=k == KT - 1)
                elif n == J_C:
                    pe.wait_ge(cn_ready, 1)
                    for k in range(2):
                        for i in range(NT):
                            last = transpose(b[:, k * T + i * P:k * T + (i + 1) * P],
                                             rest[:, i, CQ0 + k * P:CQ0 + (k + 1) * P])
                elif n == J_CR:
                    pe.wait_ge(kr_ready, 1)
                    for i in range(NT):
                        transpose(b[:, i * P:(i + 1) * P], rest[:, i, CKV0:KR0])
                        last = transpose(b[0:QK, T + i * P:T + (i + 1) * P], kpad[:, i])
                elif n < J_VM:
                    pe.wait_ge(wu_in, 32)
                    wait_job_evacuated(pe, J_CR)
                    for j in range(2):
                        hd = 2 * (n - J_KN) + j
                        last = mm(b[0:NOPE, j * T:(j + 1) * T], wukv[:, hd * 2 * DH:hd * 2 * DH + NOPE], cT[:, 2])
                elif n < J_QN:
                    i = n - J_VM
                    last = mm(b[:, :].rearrange("p (h d) -> p h d", d=DH), cT[:, 2, i * P:(i + 1) * P],
                              wukv.rearrange("p (h c) -> p h c", c=2 * DH)[:, :, NOPE:2 * DH])
                elif n < J_QT:
                    i, half = divmod(n - J_QN, 2)
                    for k in range(2):
                        last = mm(b[:, 0:384], cT[:, k, i * P:(i + 1) * P], wuq[:, k, half * 384:(half + 1) * 384],
                                  start=k == 0, stop=k == 1)
                elif n < J_MG:
                    pe.wait_ge(rope_ready, NT)
                    i, quad = divmod(n - J_QT, 2)
                    for j in range(4):
                        hd = quad * 4 + j
                        last = transpose(b[0:QK, j * P:(j + 1) * P], qn[:, i, hd * QK:(hd + 1) * QK])
                else:
                    c = n - J_MG
                    pe.wait_ge(merge_in[c % 2], 16 * (c // 2 + 1))
                    for j in range(2):
                        last = project(b[:, j * T:(j + 1) * T], lambda k: mslot[c % 2][:, k, j * P:(j + 1) * P])
                last.then_inc(job_done, 1)

            for n in range(J_KN):
                job(n)
            pe.wait_ge(w1_in, 32)
            pe.wait_ge(job_dve, 2)
            for kv in range(2):
                for l in range(LP):
                    last = mm(ps[6][0:G * NC, kv * CMP_HID:(kv + 1) * CMP_HID], blkT[:, kv, l], w1[:, kv, l],
                              start=l == 0, stop=l == LP - 1)
            last.then_inc(hid_ps, 1)
            for n in range(J_KN, J_VM):
                job(n)
            pe.wait_ge(hid_act, 1)
            for m in range(4):
                last = transpose(ps[7][:, m * 32:m * 32 + G * NC], hidS[:, m * P:(m + 1) * P])
            last.then_inc(hT_ps, 1)
            for n in range(J_VM, J_QT):
                job(n)
            pe.wait_ge(hid_ready, 1)
            for hid in range(2):
                mm(ps[6][:, 0:G * NC], w2kS[:, hid], hTk[:, hid],
                   start=hid == 0, stop=hid == 1)
            for hid in range(2):
                last = mm(ps[6][0:H * NC, 64:64 + DH], hTv[:, hid], w2vS[:, hid], start=hid == 0, stop=hid == 1)
            last.then_inc(kc_ps, 1)
            pe.wait_ge(kc_ready, 1)

            def logits(n):
                if n >= 2:
                    pe.wait_ge(L_free, n - 1)
                b = ps[2 + n % 2]
                if n < 2:
                    for hd in range(H):
                        g, r = divmod(hd, R)
                        rows = slice(g * DH, (g + 1) * DH)
                        last = mm(b[:, hd * 16:hd * 16 + NC], qT[rows, r, n * P:(n + 1) * P], kcT[rows, :])
                        if hd == R - 1:
                            last.then_inc(half_logits, 1)
                            pe.wait_ge(half_logits, n + 1)
                else:
                    br, i, pr = unit(n)
                    w = (i + 1) * P
                    for j in range(2):
                        hd = 2 * pr + j
                        o = b[:, j * T:j * T + w]
                        if br < 2:
                            g, r = divmod(hd, R)
                            rows = slice(g * DH, (g + 1) * DH)
                            last = mm(o, qT[rows, r, i * P:(i + 1) * P], kT[rows, br, 0:w])
                        else:
                            last = mm(o, mqT[0:QK, hd, i * P:(i + 1) * P], mkT[0:QK, hd, 0:w])
                last.then_inc(L_done, 1)

            logits(0)
            logits(1)
            for n in range(UNITS):
                if n < 2:
                    pe.wait_ge(cmp_ready, n + 1)
                    last = transpose(ps[4 + n][0:H * NC, 0:P], Ec[:, n])
                else:
                    br, i, pr = unit(n)
                    pe.wait_ge(E_ready, n - 1)
                    pe.wait_ge(eT_ready, n - 1)
                    for j in range(2):
                        for k in range(i + 1):
                            c = (j * (i + 1) + k) * P
                            last = transpose(ps[4 + n % 2][:, c:c + P], E[:, n % 2, j, k * P:(k + 1) * P])
                last.then_inc(T_done, 1)
                if n + 2 < UNITS:
                    if unit(n + 2)[0] == 2:
                        wait_job_evacuated(pe, J_QT + 3)
                    logits(n + 2)
                for j in fill_jobs(n):
                    job(j)
                gr = group(n)
                first = n < 2 or n % 2 == 0
                if first and gr >= 2:
                    pe.wait_ge(O_free, gr - 1)
                pe.wait_ge(eT_ready, n + 1)
                b = ps[6 + gr % 2]
                if n < 2:
                    pe.wait_ge(vb_ready, 1)
                    last = mm(b[:, :], eT[n % 2][0:H * NC, 0:P], VB[0:H * NC, :])
                else:
                    for j in range(2):
                        hd = 2 * pr + j
                        for k in range(i + 1):
                            c = (j * (i + 1) + k) * P
                            val = Vn[:, k, br * P:(br + 1) * P] if br < 2 else Vm[:, k, hd // 2 * P:(hd // 2 + 1) * P]
                            last = mm(b[:, hd % 4 * P:(hd % 4 + 1) * P], eT[n % 2][:, c:c + P], val, start=k == 0, stop=k == i)
                last.then_inc(V_done, 1)
                if n < 2 or n % 2:
                    pe.wait_ge(V_done, n + 1)
                    pe.sem_inc(O_done, 1)

            pe.wait_ge(O_free, 14)
            wait_job_evacuated(pe, JOBS - 1)
            for q in range(4):
                for m in range(4):
                    last = transpose(ps[q][:, m * P:(m + 1) * P], onat[q // 2][:, q % 2, m * P:(m + 1) * P])
                last.then_inc(oT_ps, 1)
            pe.wait_ge(oT_ready, 4)
            pe.wait_ge(wb_in, 32)
            for c in range(KT):
                if c >= 2:
                    pe.wait_ge(br_free, c - 1)
                for m in range(2):
                    last = project(ps[c % 2 + 4][:, m * T:(m + 1) * T], lambda k: wb[:, m, k, c * P:(c + 1) * P], 4,
                                   oT[:, 4 * m:4 * m + 4])
                last.then_inc(br_done, 1)
            pe.wait_ge(wo_in, 16)
            pe.wait_ge(merged_ready, KT)
            for q in range(4):
                i, f = divmod(q, 2)
                for k in range(KT):
                    last = mm(ps[q][:, :], mergedT[:, k, i * P:(i + 1) * P], wo[:, k, f * 512:(f + 1) * 512],
                              start=k == 0, stop=k == KT - 1)
                last.then_inc(h_ps, 1)

            transpose_xs(1)
            pe.wait_ge(xnT_act, 4)
            pe.wait_ge(xnT_dve, 4)
            pe.wait_ge(wq_in, 16)
            pe.wait_ge(h_ready, 4)
            for j in range(4):
                for m in range(2):
                    hd = 2 * j + m
                    last = project(ps[j][:, m * T:(m + 1) * T], lambda k: wq[:, k, hd * P:(hd + 1) * P])
                last.then_inc(qp_done, 1)
            pe.wait_ge(keys_in, 16)
            for q in range(2 * 4):
                i, f = divmod(q, 4)
                if q == 0:
                    pe.wait_ge(qp_ready, 4)
                for m in range(4):
                    side, hd = divmod(4 * f + m, H)
                    rows = slice(side * DH, (side + 1) * DH)
                    last = mm(ps[(q + 4) % 8][:, m * NK:(m + 1) * NK], qpT[rows, hd, i * P:(i + 1) * P], keysT[rows, hd])
                last.then_inc(s_done, 1)

            pe.wait_ge(s_ready, 4)
            for k in range(KT):
                for i in range(NT):
                    mm(ps[4 + k // 2][:, (k % 2) * T + i * P:(k % 2) * T + (i + 1) * P], h3[:, i, k * P:(k + 1) * P],
                       identS, start=k % 2 == 0 and i == 0, stop=False, skip_group_check=True)

            def three_passes(o, part_, moving_h, moving_l, start, stop, **kw):
                mm(o, hi[:, part_], moving_h, start=start, stop=False, **kw)
                mm(o, hi[:, part_], moving_l, start=False, stop=False, **kw)
                return mm(o, lo[:, part_], moving_h, start=False, stop=stop, **kw)

            def expert_inputs(it, s):
                c = it * RING + s
                if not (isinstance(it, int) and it == 0 and s < 2):
                    pe.wait_ge(gelu_done, c - 1)
                for k in range(KT):
                    if k % KH == 0:
                        pe.wait_ge(lo_ready, c * 2 + (k // KH + 1))
                    w, m = s % 2 * D + k * P, slice(k * T, (k + 1) * T)
                    last = three_passes(ps[s % 2][:, 0:T], slice(w, w + P), xh[:, m], xl[:, m], k == 0, k == KT - 1)
                    if k % KH == KH - 1:
                        last.then_inc(half_used, 1)

            def pick_weights(it, s, half):
                n = it * UNROLL + s
                pe.wait_ge(ab_ready, n + (half * STEPS + 1))
                if not (half == 0 and isinstance(it, int) and it == 0):
                    pe.wait_ge(w_done, n + (half * STEPS - 1))
                for t in range(TB):
                    o = ps[2 + s % 2][:, t * HALF:(t + 1) * HALF]
                    for m in range(3):
                        last = mm(o, A[s % 2][:, t], B[s % 2][m][:, t], start=m == 0, stop=m == 2)
                last.then_inc(g_done, 1)

            def expert_outputs(it, s):
                c = it * RING + s
                pe.wait_ge(wl_ready, c + 1)
                for k in range(KT):
                    if k % KH == 0:
                        pe.wait_ge(lo_ready, c * 2 + (2 * NK + k // KH + 1))
                    w, m = s % 2 * D + k * P, slice(s % 2 * T, (s % 2 + 1) * T)
                    last = three_passes(ps[4 + k // 2][:, (k % 2) * T:(k % 2 + 1) * T], slice(w, w + P), wh[:, m], wl[:, m],
                                        False, False, skip_group_check=True)
                    if k % KH == KH - 1:
                        last.then_inc(half_used, 1)

            pe.wait_ge(s_ready, 8)
            pe.wait_ge(xl_ready, 1)
            for s in range(RING):
                expert_inputs(0, s)
            with pe.Fori(1, LOOPS) as it:
                for s in range(RING):
                    expert_inputs(it, s)
            pe.wait_ge(picks_ready, NT)
            for s in range(3):
                for i in range(NT):
                    c = (s % 2) * T + i * P
                    last = transpose(ps[2 + s // 2][:, c:c + P], picks[s][:, i])
            last.then_inc(pT_done, 1)
            for s in range(RING):
                expert_inputs(LOOPS, s)
                if s == 0:
                    pe.wait_ge(pT_ready, 1)
                if s % 2:
                    pick_weights(0, s // 2, 0)
            with pe.Fori(1, LOOPS) as it:
                for s in range(RING):
                    expert_inputs(it + LOOPS, s)
                    if s % 2:
                        pick_weights(it, s // 2, 0)
            with pe.Fori(0, LOOPS) as it:
                for s in range(RING):
                    expert_outputs(it, s)
                    if s % 2:
                        pick_weights(it, s // 2, 1)
            with pe.Fori(LOOPS, 2 * LOOPS) as it:
                for s in range(RING):
                    expert_outputs(it, s)
            pe.wait_ge(y_act, 1)
            pe.wait_ge(y_dve, 1)
            for i in range(NT):
                for f in range(2):
                    for m in range(4):
                        last = transpose(ps[2 * i + f][:, m * P:(m + 1) * P], yT[:, 4 * f + m, i * P:(i + 1) * P])
                    last.then_inc(yn_done, 1)


def constants():
    f = np.float32
    dist = (T - 1) - np.arange(DIST)
    n = np.maximum(dist, 0)
    half = BUCKETS // 2
    ratio = np.maximum(n, half).astype(f) / f(half)
    large = half + (np.log(ratio) / f(math.log(MAX_DIST / half)) * f(BUCKETS - half)).astype(np.int32)
    bucket = np.where(n < half, n, np.minimum(large, BUCKETS - 1))
    bucket = np.where(dist < 0, BUCKETS, bucket)
    one_hot = (np.arange(BUCKETS + 1)[:, None] == bucket[None, :]).astype(f)
    inv = f(10000.0) ** (-np.arange(0, ROPE, 2, dtype=f) / f(ROPE))
    ang = (np.arange(T, dtype=f)[:, None] * inv[None, :]).astype(f)
    tiles = lambda a: np.ascontiguousarray(a.reshape(NT, P, -1).transpose(1, 0, 2)).astype(f)
    keys, p = np.arange(T), np.arange(P)[:, None]
    causal = np.where(P + p - keys[None, :] >= 0, f(0), f(MASKED)).astype(f)
    ends = np.arange(NC) * CMP_STRIDE + CMP_LEN - 1
    return {
        "ident": np.eye(P, dtype=f),
        "one_hot": one_hot,
        "cos": tiles(np.cos(ang)), "sin": tiles(np.sin(ang)),
        "causal": causal,
        "cmp_mask": tiles((np.arange(T)[:, None] >= ends[None, :]).astype(f)),
        "head_mask": np.concatenate([np.repeat(np.eye(H, dtype=f), NC, axis=0), np.zeros((P - H * NC, H), f)]),
        "iota": np.tile(np.arange(NK, dtype=f), (P, 1)),
        "iota16": np.tile(np.arange(TOPK, dtype=f), (P, 1)),
    }


def kernel(**inputs):
    import concourse.bacc as bacc
    from concourse.bass_utils import run_bass_kernel_spmd

    a = {k: np.asarray(val) for k, val in inputs.items()}
    cols = lambda g: g.reshape(-1, P).T
    pos = lambda g: g.reshape(LP, 2 * DH).T
    w = a["w_in"][0]
    kv = w[:, Q_COLS:Q_COLS + 6 * P].reshape(D, 6, G, DH)
    twice = lambda z: np.stack([z, z], axis=2).reshape(D, 2 * P)
    end = Q_COLS + 6 * P
    w_in = np.concatenate([
        w[:, :Q_COLS].reshape(D, G, R, DH).transpose(0, 2, 1, 3).reshape(D, Q_COLS),
        kv[:, 2].reshape(D, P), kv[:, 4].reshape(D, P), kv[:, 3].reshape(D, P), kv[:, 5].reshape(D, P),
        w[:, end:end + REST], twice(kv[:, 0]), twice(kv[:, 1]), w[:, end + REST:]], axis=1)
    w2k = a["nsa_cmp_k_w2"][0]
    c = constants()
    rows = lambda z: z.reshape(2, P, -1).transpose(1, 0, 2)
    pack = lambda *z: np.concatenate([t.reshape(P, -1) for t in z], axis=1)
    arrays = {
        "x": a["x"].reshape(T, D),
        "g_fin": a["ln_final_g"],
        "w_in": w_in,
        "w1k": a["nsa_cmp_k_w1"][0], "w1v": a["nsa_cmp_v_w1"][0],
        "w_uq": a["mla_w_uq"][0], "w_ukv": a["mla_w_ukv"][0],
        "w_bn": a["w_branch_nsa"][0], "w_bm": a["w_branch_mla"][0], "w_out": a["w_out"][0],
        "w_query": a["peer_w_query"][0],
        "keys_t": a["peer_sub_keys"][0].transpose(1, 3, 0, 2).reshape(P, H, NK),
        "u_t": a["peer_u"][0].reshape(NK, NK, KT, P).transpose(1, 3, 2, 0).reshape(NK, P, KT * NK),
        "v_t": a["peer_v"][0].reshape(NK, NK, D).transpose(1, 0, 2),
        "t5": np.concatenate([a["t5_bias"], np.full((1, H), MASKED, np.float32)]),
        "one_hot": c["one_hot"],
        "keep_pack": pack(c["ident"], c["iota"], c["iota16"], cols(a["ln_mix_g"][0]), cols(a["ln_ffn_g"][0])),
        "early_pack": pack(pos(a["nsa_cmp_pos_k"][0]), pos(a["nsa_cmp_pos_v"][0]), cols(a["mla_q_norm_g"][0]),
                           cols(a["mla_kv_norm_g"][0]), c["cos"], c["sin"], c["cmp_mask"], c["head_mask"],
                           rows(np.concatenate([w2k, w2k], axis=1)), rows(a["nsa_cmp_v_w2"][0]), c["causal"]),
    }
    arrays = {k: np.ascontiguousarray(val) for k, val in arrays.items()}
    nc = bacc.Bacc("TRN2", target_bir_lowering=False, num_devices=1)
    aps = {k: nc.dram_tensor(k, val.shape, mybir.dt.from_np(val.dtype), kind="ExternalInput").ap()
           for k, val in arrays.items()}
    out = nc.dram_tensor("out", (T, D), mybir.dt.float32, kind="ExternalOutput").ap()
    build(nc, out=out, **aps)
    r = run_bass_kernel_spmd(nc, [arrays], core_ids=[0])
    return r.results[0]["out"].reshape(1, T, D)
```

```python
import math
from contextlib import ExitStack

import numpy as np
import concourse.bass as bass
from concourse import mybir

P = 128
T = 256
NT = T // P
D = 1024
KT = D // P
H = 8
G = 2
R = H // G
DH = 64
CMP_LEN, CMP_STRIDE, CMP_HID = 32, 16, 256
NC = (T - CMP_LEN) // CMP_STRIDE + 1
NC0 = (P - CMP_LEN) // CMP_STRIDE + 1
LP = CMP_LEN // 2
Q_RANK, KV_RANK, NOPE, ROPE = 256, 128, 64, 32
QK = NOPE + ROPE
BUCKETS, MAX_DIST = 32, 128
NK = 128
TOPK = 16
EPS = 1e-6
MASKED = -1e30
Q_COLS = H * DH
REST = 3 * H + Q_RANK + KV_RANK + ROPE
K0 = Q_COLS
V0 = K0 + 2 * P
REST0 = V0 + 2 * P
CK0 = REST0 + REST
MERGE0 = CK0 + 2 * P
PART_A = MERGE0
CQ0, CKV0, KR0 = 3 * H, 3 * H + Q_RANK, 3 * H + Q_RANK + KV_RANK
DIST = T + P - 1
RING = 4
TB = 8
HALF = NK // 2
KEEP = P + NK + TOPK + 2 * KT
EARLY = 4 * LP + 3 + NT * ROPE + NT * NC + H + 2 * P + 2 * DH + T
STEPS = HALF // 2
UNROLL = RING // 2
LOOPS = STEPS // UNROLL
KH = KT // 2


def build(nc, x, g_fin, w_in, w1k, w1v, w_uq, w_ukv,
          w_bn, w_bm, w_out, w_query, keys_t, u_t, v_t, t5, one_hot, keep_pack, early_pack, out):
    fp32, u32 = mybir.dt.float32, mybir.dt.uint32
    ACT, ALU, AX = mybir.ActivationFunctionType, mybir.AluOpType, mybir.AxisListType
    ds = bass.ds

    ctx = ExitStack()
    with ctx:
        def sb(name, shape, dt=fp32):
            return ctx.enter_context(nc.sbuf_tensor(name, shape, dt))

        def sem(name):
            return ctx.enter_context(nc.semaphore(name))

        def strided(base, dims):
            return bass.AP(base.tensor, base.offset, [base.ap[0], *dims])

        def bcast(ap, n):
            return ap.unsqueeze(len(ap.shape)).to_broadcast([*ap.shape, n])

        def spread(ap, n):
            return ap.unsqueeze(1).to_broadcast([ap.shape[0], n, *ap.shape[1:]])

        big = sb("big", [P, NK * T])
        keep = sb("keep", [P, KEEP + 16])
        before = ctx.enter_context(ExitStack())

        def early(name, shape, dt=fp32):
            return before.enter_context(nc.sbuf_tensor(name, shape, dt))

        area = early("area", [P, 8192])
        xnT = early("xnT", [P, KT * T])
        x_early = early("x_early", [P, NT * D])
        ebuf = early("ebuf", [P, 1024])
        sq = early("sq", [P, 512])
        t5S = early("t5S", [BUCKETS + 1, H])
        work = early("work", [P, 5280])
        early_in = early("early_in", [P, EARLY])
        at = [0]

        def part(base, offset, *dims):
            n = int(np.prod(dims))
            v_ = base[:, offset:offset + n]
            if len(dims) == 2:
                return v_.rearrange("p (a b) -> p a b", b=dims[1])
            if len(dims) == 3:
                return v_.rearrange("p (a b c) -> p a b c", b=dims[1], c=dims[2])
            return v_

        ep = [0]

        def e_(*dims):
            ep[0] += int(np.prod(dims))
            return part(early_in, ep[0] - int(np.prod(dims)), *dims)

        def w_(*dims):
            at[0] += int(np.prod(dims))
            return part(work, at[0] - int(np.prod(dims)), *dims)

        def keep_(n):
            at[0] += n
            return part(keep, at[0] - n, n)

        win = part(big, 0, KT, PART_A)
        wb = part(big, 0, 2, 4, D)
        mgT = part(big, 8192, 2 * KT, T)
        qn = part(big, 12288, NT, H * QK)
        MG = 13824
        mslot = [part(big, MG + s * 2048, KT, 256) for s in range(2)]
        biasM = part(big, 17920, H, T)
        onat = [part(big, 19968 + s * 1024, NT, H * DH) for s in range(2)]
        wuq = part(big, 22016, 2, H * QK)
        wukv = part(big, 22016 + 1536, H * 2 * DH)
        mqT = part(big, 24576, H, T)
        scaled = [part(big, 24576, NT, D), part(big, 26624, NT, D)]
        mergedT = part(big, 24576, KT, T)
        mkT = part(big, 26624, H, T)
        Vm = part(big, 28672, NT, H * DH)
        oT = part(big, 29696, 2 * 4, T)
        blkT = part(big, 31744, 2, LP, G * NC)
        tmp = part(big, 31744, H * DH)
        w1 = part(area, 0, 2, LP, CMP_HID)
        wo = part(area, 0, KT, D)
        wq = part(big, MG, KT, D)
        keysT = part(big, 12288, H, NK)
        qpT = part(big, 8192, H, T)
        S = part(big, 24576, NT, 2 * H, NK)
        cand = part(big, 28672, H, TOPK * TOPK)
        eq = part(big, 30720, H * TOPK, TOPK)
        topv = part(big, 22016, 2 * H, TOPK)
        topi_f = part(big, 22272, 2 * H, TOPK)
        topi = part(big, 22528, 2 * H, TOPK).bitcast(u32)
        best = [part(big, n, H, TOPK) for n in (22784, 23560)]
        picks = [part(big, 23688 + s * T, NT, P) for s in range(3)]
        pick = part(big, 22912, H, TOPK).bitcast(u32)
        pick_a = part(big, 23040, H * TOPK).bitcast(u32)
        pick_b = part(big, 23168, H * TOPK).bitcast(u32)
        pa_f = part(big, 23296, H * TOPK)
        pb_f = part(big, 23424, H * TOPK)
        gsum = part(big, 23552, H)
        ynat = part(big, 2048, NT, D)
        sq_h = part(big, 28672, 4 * 512)
        sq_fin = part(big, 4096, 4 * 512)
        gfin = part(big, 8192, D)
        xnT3 = part(xnT, 0, KT, T)
        x3 = part(x_early, 0, NT, D)

        identS, iotaS, iota16S = keep_(P), keep_(NK), keep_(TOPK)
        gmix, gffn = keep_(KT), keep_(KT)
        assert at[0] == KEEP
        ssq, rstd = keep_(8), keep_(8)
        posS, qgS, kvgS, cosS, sinS = e_(4, LP), e_(2), e_(1), e_(NT, ROPE // 2), e_(NT, ROPE // 2)
        cmaskS, hmaskS, w2kS, w2vS, causalS = e_(NT, NC), e_(H), e_(2, P), e_(2, DH), e_(T)
        assert ep[0] == EARLY
        at[0] = 0
        qT = w_(R, T)
        kT = w_(2, T)
        Vn = w_(NT, 2 * P)
        rest = w_(NT, REST)
        E = w_(2, 2, T)
        cT = part(work, at[0] - 2 * 2 * T, 3, T)
        hTk, hTv = w_(2, G * NC), w_(2, H * NC)
        kcT = w_(NC)
        vcs = w_(DH)
        Ec = w_(2, H * NC)
        nmx = w_(24, 2)
        csum = w_(NT, H)
        sums = w_(6, H)
        sc = w_(14, H)
        eT = [part(ebuf, s * 512, 512) for s in range(2)]
        kpad = part(ebuf, 0, NT, QK)
        VB = part(sq, 0, H * DH)
        rot = [part(sq, n * P, H, ROPE // 2) for n in range(4)]
        ohS = part(sq, 0, DIST)[0:BUCKETS + 1, :]
        revS = part(ebuf, 512, DIST)[0:H, :]
        hidS = part(ebuf, 512, 2 * CMP_HID)[0:G * NC, :]
        assert at[0] <= 5280, at[0]
        before.close()
        f32r = mybir.dt.float32r
        raw = sb("raw", [P, RING * D])
        hi, lo = sb("hi", [P, 2 * D], f32r), sb("lo", [P, 2 * D], f32r)
        bf16 = mybir.dt.bfloat16
        A_ = sb("A", [P, 2 * TB * NK], bf16)
        B_ = [sb(f"B{n}", [P, 2 * TB * HALF], bf16) for n in range(3)]
        wh, wl = sb("wh", [P, 2 * T], f32r), sb("wl", [P, 2 * T], f32r)
        marks = sb("marks", [P, TB * HALF], bf16)
        gT, g_rest, g_rest2 = (sb(n, [P, T]) for n in ("gT", "g_rest", "g_rest2"))
        i1T, i2T = sb("i1T", [P, T], bf16), sb("i2T", [P, T], bf16)
        gp = [sb(f"g_part{n}", [P, T], bf16) for n in range(3)]
        iotaB = sb("iotaB", [P, NK], bf16)
        xh, xl = sb("xh", [P, KT * T], f32r), sb("xl", [P, KT * T], f32r)
        A = [part(A_, s * TB * NK, TB, NK) for s in range(2)]
        B = [[part(b, s * TB * HALF, TB, HALF) for b in B_] for s in range(2)]
        as_f32 = lambda ap: ap.bitcast(fp32)

        rev_dram = nc.dram_tensor("bias_by_distance", [H, P, DIST], fp32, kind="Internal")

        ps = [ctx.enter_context(nc.psum_tensor(f"ps{n}", [P, 512], fp32)) for n in range(8)]
        Y_BANKS = ps[4:8]

        x_in = [sem(f"x_in{n}") for n in range(NT)]
        const_in, t5_in, bias_in, rev_out = (sem(n) for n in ("const_in", "t5_in", "bias_in", "rev_out"))
        win_in = [sem(f"win_in{n}") for n in range(4)]
        merge_in = [sem(f"merge_in{n}") for n in range(2)]
        w1_in, w2_in, wu_in, wb_in, wo_in, wq_in, keys_in = (
            sem(n) for n in ("w1_in", "w2_in", "wu_in", "wb_in", "wo_in", "wq_in", "keys_in"))
        raw_in = [sem(f"raw_in{n}") for n in range(RING)]
        xh_ready, xl_ready = sem("xh_ready"), sem("xl_ready")
        hi_ready, lo_ready, half_used = sem("hi_ready"), sem("lo_ready"), sem("half_used")
        wh_ready, wl_ready = sem("wh_ready"), sem("wl_ready")
        out_done, gfin_in = sem("out_done"), sem("gfin_in")
        dve_chain, act_chain = sem("dve_chain"), sem("act_chain")
        rev_ps, rev_sb = sem("rev_ps"), sem("rev_sb")
        ssq_ready, ms_ready, root_ready, xs_ready = (sem(n) for n in ("ssq_ready", "ms_ready", "root_ready", "xs_ready"))
        xT_ps, xnT_act, xnT_dve = sem("xT_ps"), sem("xnT_act"), sem("xnT_dve")
        job_done, job_act, job_dve = sem("job_done"), sem("job_act"), sem("job_dve")
        c_ssq, c_ms, c_root, cn_ready, kr_ready, rope_ready = (
            sem(n) for n in ("c_ssq", "c_ms", "c_root", "cn_ready", "kr_ready", "rope_ready"))
        hid_ps, hid_ready, kc_ps, kc_ready, vb_ready = (sem(n) for n in ("hid_ps", "hid_ready", "kc_ps", "kc_ready", "vb_ready"))
        L_done, L_free, max_ready, E_ready = (sem(n) for n in ("L_done", "L_free", "max_ready", "E_ready"))
        cmp_sub, cmp_exp, cmp_ready = sem("cmp_sub"), sem("cmp_exp"), sem("cmp_ready")
        T_done, eT_ready, V_done, O_free = (sem(n) for n in ("T_done", "eT_ready", "V_done", "O_free"))
        b_marked = sem("b_marked")
        hid_act, hT_ps = sem("hid_act"), sem("hT_ps")
        onat_ready = sem("onat_ready")
        sig_ready = sem("sig_ready")
        half_logits = sem("half_logits")
        gate_ready = sem("gate_ready")
        oT_ps, oT_ready = sem("oT_ps"), sem("oT_ready")
        br_done, br_free, merged_ready = sem("br_done"), sem("br_free"), sem("merged_ready")
        h_ps = sem("h_ps")
        qp_done, qp_ready, s_done, s_ready = (sem(n) for n in ("qp_done", "qp_ready", "s_done", "s_ready"))
        best_sub, best_exp, picks_ready, pT_done, pT_ready = (
            sem(n) for n in ("best_sub", "best_exp", "picks_ready", "pT_done", "pT_ready"))
        gelu_done, ab_ready, g_done, w_done = (sem(n) for n in ("gelu_done", "ab_ready", "g_done", "w_done"))
        f_ssq, f_ms, f_root, out_ready = (
            sem(n) for n in ("f_ssq", "f_ms", "f_root", "out_ready"))

        CONSTS = 2
        (J_Q0, J_Q1, J_K, J_R0, J_R1, J_CK, J_V, J_C, J_CR, J_KN) = range(10)
        J_VM = J_KN + 4
        J_QN = J_VM + 2
        J_QT = J_QN + 4
        J_MG = J_QT + 4
        JOBS = J_MG + 8
        DVE_JOBS = (J_CK,)
        UNITS = 2 + 3 * NT * H // 2

        def unit(n):
            m = n - 2
            return m // 8, m // 4 % 2, m % 4

        def group(n):
            return n if n < 2 else 2 + (n - 2) // 2

        def act_jobs_before(n):
            return sum(j not in DVE_JOBS for j in range(n))

        def dve_jobs_before(n):
            return sum(j in DVE_JOBS for j in range(n))

        def wait_job_evacuated(eng, n):
            if n in DVE_JOBS:
                eng.wait_ge(job_dve, dve_jobs_before(n) + 1)
            else:
                eng.wait_ge(job_act, act_jobs_before(n) + 1)

        def fill_job(n):
            if n < 4:
                return J_QT + n, None
            return (J_MG + (n - 4) // 2, n % 2) if n < 20 else (None, None)

        block = ctx.enter_context(nc.Block())

        @block.sync
        def _(sp):
            w_in_t = w_in.rearrange("(k p) c -> p k c", p=P)
            for i in range(NT):
                sp.dma_start(x3[:, i], x[i * P:(i + 1) * P]).then_inc(x_in[i], 16)
            sp.dma_start(keep[:, 0:KEEP], keep_pack).then_inc(const_in, 16)
            sp.dma_start(t5S[:, :], t5).then_inc(t5_in, 16)
            sp.dma_start(ohS, one_hot).then_inc(t5_in, 16)
            sp.dma_start(early_in[:, :], early_pack).then_inc(const_in, 16)
            for n, (a, b) in enumerate(((0, K0 // 2), (K0 // 2, K0), (K0, REST0), (REST0, PART_A))):
                sp.dma_start(win[:, :, a:b], w_in_t[:, :, a:b]).then_inc(win_in[n], 16)
            sp.dma_start(w1[:, 0], w1k.rearrange("(k p) c -> p k c", p=P)).then_inc(w1_in, 16)
            sp.dma_start(w1[:, 1], w1v.rearrange("(k p) c -> p k c", p=P)).then_inc(w1_in, 16)
            sp.dma_start(wuq, w_uq.rearrange("(k p) c -> p k c", p=P)).then_inc(wu_in, 16)
            sp.dma_start(wukv, w_ukv).then_inc(wu_in, 16)

            def merge_chunk(c):
                if c >= 2:
                    sp.wait_ge(job_done, J_MG + c - 2 + 1)
                lo = MERGE0 + c * 256
                sp.dma_start(mslot[c % 2], w_in_t[:, :, lo:lo + 256]).then_inc(merge_in[c % 2], 16)

            merge_chunk(0)
            merge_chunk(1)
            sp.wait_ge(job_done, J_V + 1)
            sp.dma_start(wb[:, 0], w_bn.rearrange("(k p) c -> p k c", p=P)).then_inc(wb_in, 16)
            sp.dma_start(wb[:, 1], w_bm.rearrange("(k p) c -> p k c", p=P)).then_inc(wb_in, 16)
            sp.wait_ge(hid_ps, 1)
            sp.dma_start(wo, w_out.rearrange("(k p) c -> p k c", p=P)).then_inc(wo_in, 16)
            for c in range(2, 8):
                merge_chunk(c)
            sp.wait_ge(job_done, JOBS)
            sp.dma_start(keysT, keys_t).then_inc(keys_in, 16)
            sp.wait_ge(oT_ps, 4)
            sp.dma_start(wq, w_query.rearrange("(k p) c -> p k c", p=P)).then_inc(wq_in, 16)
            sp.wait_ge(h_ps, 4)

            def load(src, slot, n):
                sp.dma_start(raw[:, slot * D:(slot + 1) * D], src[n]).then_inc(raw_in[slot], 16)

            for s in range(RING):
                load(u_t, s, s)
            with sp.Fori(1, NK // RING) as it:
                for s in range(RING):
                    sp.wait_ge(lo_ready, (it * RING + s - RING + 1) * 2)
                    load(u_t, s, it * RING + s)
            with sp.Fori(0, NK // RING) as it:
                for s in range(RING):
                    sp.wait_ge(lo_ready, (it * RING + s + NK - RING + 1) * 2)
                    load(v_t, s, it * RING + s)
            for q in range(4):
                i, f = divmod(q, 2)
                c = slice(f * 512, (f + 1) * 512)
                sp.wait_ge(out_ready, q + 1)
                sp.dma_start(out[i * P:(i + 1) * P, c], ynat[:, i, c]).then_inc(out_done, 16)
            sp.wait_ge(out_done, 4 * 16)

        @block.gpsimd
        def _(pool):
            pool.wait_ge(rev_sb, 1)
            pool.dma_start(rev_dram.ap(), spread(revS, P)).then_inc(rev_out, 16)
            pool.wait_ge(rev_out, 16)
            pool.dma_start(biasM, bass.AP(rev_dram, P - 1, [[DIST - 1, P], [P * DIST, H], [1, T]])).then_inc(bias_in, 16)
            with pool.Fori(0, 2 * NK // RING) as it:
                for s in range(RING):
                    for f in range(2):
                        pool.wait_ge(hi_ready, (it * RING + s) * 2 + f + 1)
                        a, b = s * D + f * KH * P, s % 2 * D + f * KH * P
                        nc.gpsimd.tensor_tensor(lo[:, b:b + KH * P], raw[:, a:a + KH * P],
                                                as_f32(hi[:, b:b + KH * P]), ALU.subtract).then_inc(lo_ready, 1)
            pool.wait_ge(half_used, 3 * NK)
            pool.dma_start(gfin, g_fin.partition_broadcast(P)).then_inc(gfin_in, 16)

        @block.scalar
        def _(act):
            chain = [0]

            def link(ins):
                chain[0] += 1
                ins.then_inc(act_chain, 1)
                act.wait_ge(act_chain, chain[0])

            for i in range(NT):
                act.wait_ge(x_in[i], 16)
                nc.scalar.activation(scaled[0][:, i], x3[:, i], ACT.Square, accum_out=ssq[:, i:i + 1]).then_inc(ssq_ready, 1)
                act.wait_ge(ms_ready, i + 1)
                nc.scalar.activation(ssq[:, i:i + 1], rstd[:, i:i + 1], ACT.Sqrt).then_inc(root_ready, 1)

            def gained_transposes(first, bank, gain):
                act.wait_ge(const_in, CONSTS * 16)
                for q in (0, 2):
                    act.wait_ge(xT_ps, first + q + 1)
                    for m in range(4):
                        k = q % 2 * 4 + m
                        last = nc.scalar.activation(xnT3[:, k, (q // 2) * P:(q // 2 + 1) * P],
                                                    ps[bank + q][:, m * P:(m + 1) * P], ACT.Copy,
                                                    scale=gain[:, k:k + 1])
                    last.then_inc(xnT_act, 1)

            gained_transposes(0, 2, gmix)
            act.wait_ge(rev_ps, 1)
            nc.scalar.copy(revS, ps[6][0:H, 0:DIST]).then_inc(rev_sb, 1)

            def evacuate(n):
                b = ps[n % 2]
                act.wait_ge(job_done, n + 1)
                if n in (J_Q0, J_Q1):
                    last = nc.scalar.copy(qT[:, 2 * n:2 * n + 2], b[:, :].rearrange("p (a t) -> p a t", t=T))
                elif n == J_K:
                    last = nc.scalar.copy(kT, b[:, :].rearrange("p (a t) -> p a t", t=T))
                elif n in (J_R0, J_R1):
                    last = nc.scalar.copy(rest[:, n - J_R0], b[:, 0:REST])
                elif n == J_V:
                    last = nc.scalar.copy(Vn, b[:, :].rearrange("p (i c) -> p i c", i=NT))
                elif n == J_C:
                    for k in range(2):
                        last = nc.scalar.activation(cT[:, k], b[:, k * T:(k + 1) * T], ACT.Copy, scale=qgS[:, k:k + 1])
                elif n == J_CR:
                    nc.scalar.activation(cT[:, 2], b[:, 0:T], ACT.Copy, scale=kvgS[:, 0:1])
                    last = nc.scalar.copy(mkT[NOPE:QK], spread(b[NOPE:QK, T:2 * T], H))
                elif n < J_VM:
                    k = 2 * (n - J_KN)
                    last = nc.scalar.copy(mkT[0:NOPE, k:k + 2], b[0:NOPE, :].rearrange("p (a t) -> p a t", t=T))
                elif n < J_QN:
                    last = nc.scalar.copy(Vm[:, n - J_VM], b[:, :])
                elif n < J_QT:
                    i, half = divmod(n - J_QN, 2)
                    last = nc.scalar.copy(qn[:, i, half * 384:(half + 1) * 384], b[:, 0:384])
                elif n < J_MG:
                    i, quad = divmod(n - J_QT, 2)
                    last = nc.scalar.copy(mqT[0:QK, quad * 4:quad * 4 + 4, i * P:(i + 1) * P],
                                          b[0:QK, :].rearrange("p (a t) -> p a t", t=P))
                else:
                    c = n - J_MG
                    last = nc.scalar.copy(mgT[:, 2 * c:2 * c + 2], b[:, :].rearrange("p (a t) -> p a t", t=T))
                last.then_inc(job_act, 1)
                if n == J_R1:
                    act.wait_ge(job_act, act_jobs_before(J_R1) + 1)
                    for i in range(NT):
                        nc.scalar.activation(sq[:, 0:Q_RANK], rest[:, i, CQ0:CKV0], ACT.Square,
                                             accum_out=ssq[:, 2 + i:3 + i])
                        link(nc.scalar.activation(sq[:, Q_RANK:Q_RANK + KV_RANK], rest[:, i, CKV0:KR0], ACT.Square,
                                                  accum_out=ssq[:, 4 + i:5 + i]))
                    nc.scalar.copy(rstd[:, 2:6], ssq[:, 2:6]).then_inc(c_ssq, 1)
                    act.wait_ge(c_ms, 1)
                    nc.scalar.activation(rstd[:, 2:6], ssq[:, 2:6], ACT.Sqrt).then_inc(c_root, 1)

            for n in range(J_KN):
                if n not in DVE_JOBS:
                    evacuate(n)
            act.wait_ge(hid_ps, 1)
            act.wait_ge(rev_out, 16)
            nc.scalar.activation(hidS, ps[6][0:G * NC, :], ACT.Gelu).then_inc(hid_act, 1)
            for n in range(J_KN, J_QT):
                evacuate(n)
            act.wait_ge(hT_ps, 1)
            for hid in range(2):
                nc.scalar.copy(hTk[:, hid], ps[7][:, hid * 32:hid * 32 + G * NC])
                src = ps[7][:, (2 + hid) * 32:(2 + hid) * 32 + G * NC].rearrange("p (g c) -> p g c", g=G)
                last = nc.scalar.copy(hTv[:, hid].rearrange("p (g r c) -> p g r c", g=G, r=R),
                                      src.unsqueeze(2).to_broadcast([P, G, R, NC]))
            last.then_inc(hid_ready, 1)
            act.wait_ge(kc_ps, 1)
            for g in range(G):
                nc.scalar.copy(kcT[g * DH:(g + 1) * DH, :], ps[6][g * DH:(g + 1) * DH, g * NC:(g + 1) * NC])
            nc.scalar.copy(vcs[0:H * NC, :], ps[6][0:H * NC, 64:64 + DH]).then_inc(kc_ready, 1)
            for i in range(NT):
                last = nc.scalar.activation(rest[:, i, 0:3 * H], rest[:, i, 0:3 * H], ACT.Exp, scale=-1.0)
            last.then_inc(gate_ready, 1)

            def exponentials(n):
                if n < 2:
                    act.wait_ge(cmp_sub, n + 1)
                    ncv = NC0 if n == 0 else NC
                    e = Ec[:, n].rearrange("p (h c) -> p h c", c=NC)[:, :, 0:ncv]
                    nc.scalar.activation(e, e, ACT.Exp).then_inc(cmp_exp, 1)
                else:
                    br, i, pr = unit(n)
                    act.wait_ge(max_ready, n - 1)
                    for j in range(2):
                        e = E[:, n % 2, j, 0:(i + 1) * P]
                        last = nc.scalar.activation(e, e, ACT.Exp, bias=nmx[:, n - 2, j:j + 1],
                                                    accum_out=sums[:, br * 2 + i, 2 * pr + j:2 * pr + j + 1])
                    last.then_inc(E_ready, 1)

            def output_transposes(q):
                act.wait_ge(oT_ps, q + 1)
                nc.scalar.copy(oT[:, (q // 2) * 4:(q // 2) * 4 + 4, (q % 2) * P:(q % 2 + 1) * P],
                               ps[q][:, :].rearrange("p (a t) -> p a t", t=P)).then_inc(oT_ready, 1)

            exponentials(0)
            for n in range(UNITS):
                act.wait_ge(T_done, n + 1)
                if n >= 2:
                    act.wait_ge(V_done, n - 1)
                if n < 2:
                    nc.scalar.copy(eT[n % 2][0:H * NC, 0:P], ps[4 + n % 2][0:H * NC, 0:P]).then_inc(eT_ready, 1)
                else:
                    w = 2 * (unit(n)[1] + 1) * P
                    nc.scalar.copy(eT[n % 2][:, 0:w], ps[4 + n % 2][:, 0:w]).then_inc(eT_ready, 1)
                if n + 1 < UNITS:
                    exponentials(n + 1)
                j, half = fill_job(n)
                if half != 0 and j is not None:
                    evacuate(j)
                if n in (22, 23):
                    output_transposes(n - 22)
            output_transposes(2)
            output_transposes(3)
            for c in range(KT):
                m = strided(mgT[:, c, 0:1], [[KT * T, 2], [1, T]])
                if c == 0:
                    act.wait_ge(job_act, act_jobs_before(JOBS))
                nc.scalar.activation(m, m, ACT.Sigmoid).then_inc(sig_ready, 1)
            for i in range(NT):
                for f in range(2):
                    q = 2 * i + f
                    act.wait_ge(h_ps, q + 1)
                    nc.scalar.activation(sq_h[:, q * 512:(q + 1) * 512], Y_BANKS[q][:, :], ACT.Square,
                                         accum_out=ssq[:, q:q + 1]).then_inc(ssq_ready, 1)
                act.wait_ge(ms_ready, NT + i + 1)
                nc.scalar.activation(ssq[:, 4 + i:5 + i], rstd[:, i:i + 1], ACT.Sqrt).then_inc(root_ready, 1)
            gained_transposes(4, 0, gffn)
            def split(c, slot, it, early_=False):
                act.wait_ge(raw_in[slot], (it + 1) * 16)
                for f in range(2):
                    if not early_:
                        act.wait_ge(half_used, c * 2 + (f - 3))
                    a, b = slot * D + f * KH * P, slot % 2 * D + f * KH * P
                    nc.scalar.copy(hi[:, b:b + KH * P], raw[:, a:a + KH * P]).then_inc(hi_ready, 1)

            act.wait_ge(xnT_act, 4)
            act.wait_ge(xnT_dve, 4)
            nc.scalar.copy(xh[:, :], xnT[:, :]).then_inc(xh_ready, 1)
            for j in range(4):
                if j >= 2:
                    split(j - 2, j - 2, 0, True)
                act.wait_ge(qp_done, j + 1)
                nc.scalar.copy(qpT[:, 2 * j:2 * j + 2], ps[j][:, :].rearrange("p (a t) -> p a t", t=T)).then_inc(qp_ready, 1)
            for q in range(2 * 4):
                i, f = divmod(q, 4)
                act.wait_ge(s_done, q + 1)
                nc.scalar.copy(S[:, i, 4 * f:4 * f + 4],
                               ps[q % 4][:, :].rearrange("p (a t) -> p a t", t=NK)).then_inc(s_ready, 1)

            def u_stage(it, last_=False):
                for s in range(RING):
                    c = it * RING + s
                    split(c + 2, (s + 2) % RING, it + (s + 2) // RING)
                    if last_ and s == RING - 1:
                        act.wait_ge(w_done, STEPS)
                        split_w(0, 0)
                    act.wait_ge(half_used, c * 2 + 2)
                    nc.scalar.activation(big[:, ds(c * T, T)], ps[s % 2][:, 0:T], ACT.Gelu).then_inc(gelu_done, 1)

            def split_w(c, s):
                nc.scalar.copy(wh[:, s % 2 * T:(s % 2 + 1) * T], big[:, ds(c * T, T)]).then_inc(wh_ready, 1)

            def v_stage(it, last_=False):
                for s in range(RING):
                    c = it * RING + s
                    if last_ and s >= 2:
                        break
                    split(c + (NK + 2), (s + 2) % RING, it + (s + 2) // RING + NK // RING)
                    act.wait_ge(half_used, c * 2 + (2 * NK + 2))
                    split_w(c + 2, s)

            with act.Fori(0, 13) as it:
                u_stage(it)
            for i in range(NT):
                act.wait_ge(best_sub, i + 1)
                nc.scalar.activation(best[i], best[i], ACT.Exp).then_inc(best_exp, 1)
            with act.Fori(13, LOOPS) as it:
                u_stage(it)
            act.wait_ge(pT_done, 1)
            for s, dst in enumerate((i1T, i2T, gT)):
                last = nc.scalar.copy(dst[:, :], ps[2 + s // 2][:, (s % 2) * T:(s % 2 + 1) * T])
            last.then_inc(pT_ready, 1)
            with act.Fori(LOOPS, 2 * LOOPS - 1) as it:
                u_stage(it)
            u_stage(2 * LOOPS - 1, True)
            split_w(1, 1)
            with act.Fori(0, LOOPS - 1) as it:
                v_stage(it)
            for s in range(RING):
                c = (LOOPS - 1) * RING + s
                split(c + NK + 2, (s + 2) % RING, LOOPS - 1 + (s + 2) // RING + NK // RING)
                act.wait_ge(half_used, c * 2 + 2 * NK + 2)
                if s == 2:
                    act.wait_ge(w_done, 2 * STEPS)
                split_w(c + 2, s)
            with act.Fori(LOOPS, 2 * LOOPS - 1) as it:
                v_stage(it)
            v_stage(2 * LOOPS - 1, True)

            nc.scalar.activation(rstd[:, 6:7], iotaS[:, 0:1], ACT.Sqrt)
            act.wait_ge(half_used, 4 * NK)
            for q in range(4):
                nc.scalar.activation(sq_fin[:, q * 512:(q + 1) * 512], Y_BANKS[q][:, :], ACT.Square,
                                     accum_out=ssq[:, q:q + 1]).then_inc(f_ssq, 1)
            act.wait_ge(f_ms, 1)
            nc.scalar.activation(ssq[:, 0:NT], rstd[:, 4:4 + NT], ACT.Sqrt).then_inc(f_root, 1)

        @block.vector
        def _(dve):
            chain = [0]
            vec = nc.vector

            def link(ins):
                chain[0] += 1
                ins.then_inc(dve_chain, 1)
                dve.wait_ge(dve_chain, chain[0])

            def self_wait(ins, sem_, count):
                ins.then_inc(sem_, 1)
                dve.wait_ge(sem_, count)

            def norm_x():
                for i in range(NT):
                    dve.wait_ge(ssq_ready, i + 1)
                    vec.tensor_scalar(rstd[:, i:i + 1], ssq[:, i:i + 1], 1.0 / D, EPS, ALU.mult, ALU.add).then_inc(ms_ready, 1)
                    dve.wait_ge(root_ready, i + 1)
                    link(vec.reciprocal(rstd[:, i:i + 1], ssq[:, i:i + 1]))
                    vec.tensor_scalar(scaled[0][:, i], x3[:, i], rstd[:, i:i + 1], None, ALU.mult).then_inc(xs_ready, 1)

            def norm_h():
                for i in range(NT):
                    r, q = rstd[:, i:i + 1], 2 * i
                    dve.wait_ge(ssq_ready, NT + q + 1)
                    link(vec.tensor_scalar(r, ssq[:, q:q + 1], 1.0 / D, EPS, ALU.mult, ALU.add))
                    dve.wait_ge(ssq_ready, NT + q + 2)
                    vec.scalar_tensor_tensor(r, ssq[:, q + 1:q + 2], 1.0 / D, r, ALU.mult, ALU.add).then_inc(ms_ready, 1)
                    dve.wait_ge(root_ready, NT + i + 1)
                    link(vec.reciprocal(r, ssq[:, 4 + i:5 + i]))
                    for f in range(2):
                        vec.tensor_scalar(scaled[1][:, i, f * 512:(f + 1) * 512], Y_BANKS[q + f][:, :], r, None,
                                          ALU.mult).then_inc(xs_ready, 1)

            def gained_transposes(first, bank, gain):
                for q in (1, 3):
                    dve.wait_ge(xT_ps, first + q + 1)
                    for m in range(4):
                        k = q % 2 * 4 + m
                        last = vec.tensor_scalar(xnT3[:, k, (q // 2) * P:(q // 2 + 1) * P],
                                                 ps[bank + q][:, m * P:(m + 1) * P], gain[:, k:k + 1], None, ALU.mult)
                    last.then_inc(xnT_dve, 1)

            norm_x()
            vec.memset(kpad, 0.0)
            vec.memset(Ec, 0.0)
            dve.wait_ge(const_in, CONSTS * 16)
            gained_transposes(0, 2, gmix)
            dve.wait_ge(c_ssq, 1)
            vec.tensor_scalar(ssq[:, 2:4], rstd[:, 2:4], 1.0 / Q_RANK, EPS, ALU.mult, ALU.add)
            vec.tensor_scalar(ssq[:, 4:6], rstd[:, 4:6], 1.0 / KV_RANK, EPS, ALU.mult, ALU.add).then_inc(c_ms, 1)
            dve.wait_ge(job_done, J_CK + 1)
            for kv in range(2):
                for par in range(2):
                    for g in range(G):
                        o = kv * T + par
                        rows = slice(g * DH, (g + 1) * DH)
                        last = vec.tensor_tensor(
                            blkT[par * DH:(par + 1) * DH, kv, :, g * NC:(g + 1) * NC],
                            strided(ps[J_CK % 2][rows, o:o + 1], [[2, LP], [CMP_STRIDE, NC]]),
                            bcast(posS[rows, 2 * kv + par], NC), ALU.add)
            last.then_inc(job_dve, 1)
            dve.wait_ge(c_root, 1)
            link(vec.reciprocal(ssq[:, 2:6], rstd[:, 2:6]))
            for i in range(NT):
                vec.tensor_scalar(rest[:, i, CQ0:CKV0], rest[:, i, CQ0:CKV0], ssq[:, 2 + i:3 + i], None, ALU.mult)
                last = vec.tensor_scalar(rest[:, i, CKV0:KR0], rest[:, i, CKV0:KR0], ssq[:, 4 + i:5 + i], None, ALU.mult)
            last.then_inc(cn_ready, 1)

            def rotate(x1, x2, c, s, heads, y1, y2):
                t = [r[:, 0:heads] for r in rot]
                vec.tensor_tensor(t[0], x1, c, ALU.mult)
                vec.tensor_tensor(t[1], x2, s, ALU.mult)
                vec.tensor_tensor(t[2], x2, c, ALU.mult)
                link(vec.tensor_tensor(t[3], x1, s, ALU.mult))
                vec.tensor_tensor(y1, t[0], t[1], ALU.subtract)
                return vec.tensor_tensor(y2, t[2], t[3], ALU.add)

            HR = ROPE // 2
            last = rotate(rest[:, :, KR0:KR0 + HR], rest[:, :, KR0 + HR:KR0 + ROPE], cosS, sinS, NT,
                          kpad[:, :, NOPE:NOPE + HR], kpad[:, :, NOPE + HR:QK])
            last.then_inc(kr_ready, 1)
            for i in range(NT):
                dve.wait_ge(job_act, act_jobs_before(J_QN + 2 * i + 1) + 1)
                q = qn[:, i].rearrange("p (h c) -> p h c", c=QK)
                last = rotate(q[:, :, NOPE:NOPE + HR], q[:, :, NOPE + HR:QK], spread(cosS[:, i], H), spread(sinS[:, i], H),
                              H, q[:, :, NOPE:NOPE + HR], q[:, :, NOPE + HR:QK])
                self_wait(last, rope_ready, i + 1)
            dve.wait_ge(kc_ready, 1)
            vec.tensor_tensor(VB[0:H * NC, :].rearrange("p (h d) -> p h d", d=DH), spread(vcs[0:H * NC, :], H),
                              bcast(hmaskS[0:H * NC, :], DH), ALU.mult).then_inc(vb_ready, 1)
            dve.wait_ge(bias_in, 16)
            dve.wait_ge(gate_ready, 1)
            gates = rest[:, :, 0:3 * H]
            link(vec.tensor_scalar(gates, gates, 1.0, None, ALU.add))
            link(vec.reciprocal(gates, gates))

            def combine(gr):
                dve.wait_ge(V_done, gr + 1 if gr < 2 else 2 * gr)
                bank = ps[6 + gr % 2]
                if gr < 2:
                    i, br, hs, dst = gr, 0, slice(0, H), onat[0]
                    link(vec.reciprocal(sc[:, gr], csum[:, i]))
                    o = bank[:, :].rearrange("p (h d) -> p h d", d=DH)
                else:
                    br, i, quad = (gr - 2) // 4, gr // 2 % 2 ^ 1, gr % 2
                    hs, dst = slice(4 * quad, 4 * quad + 4), onat[br // 2]
                    link(vec.reciprocal(sc[:, gr, hs], sums[:, br * 2 + i, hs]))
                    o = (strided(bank[:, quad * DH:quad * DH + 1], [[P, 4], [1, DH]]) if br < 2 else
                         strided(bank[:, 0:1], [[2 * P, 2], [P + DH, 2], [1, DH]]))
                w = sc[:, gr, hs]
                if br < 2:
                    gate = rest[:, i, 0:3 * H].rearrange("p (h b) -> p b h", b=3)
                    link(vec.tensor_tensor(w, w, gate[:, 0 if gr < 2 else br + 1, hs], ALU.mult))
                d = dst[:, i, hs.start * DH:hs.stop * DH]
                nh = hs.stop - hs.start
                if gr < 2 or br == 2:
                    shape = (lambda z: z.rearrange("p (a b d) -> p a b d", b=2, d=DH)) if br == 2 else (
                        lambda z: z.rearrange("p (h d) -> p h d", d=DH))
                    wb_ = bcast(w.rearrange("p (a b) -> p a b", b=2) if br == 2 else w, DH)
                    self_wait(vec.tensor_tensor(shape(d), o, wb_, ALU.mult), O_free, gr + 1)
                else:
                    t = tmp[:, 0:nh * DH]
                    self_wait(vec.tensor_tensor(t.rearrange("p (h d) -> p h d", d=DH), o, bcast(w, DH), ALU.mult),
                              O_free, gr + 1)
                    self_wait(vec.tensor_tensor(d, d, t, ALU.add), onat_ready, gr - 1)

            for n in range(2):
                ncv = NC0 if n == 0 else NC
                e = Ec[:, n].rearrange("p (h c) -> p h c", c=NC)[:, :, 0:ncv]
                k0 = CMP_LEN - 1 + (P if n == 0 else 0)
                dve.wait_ge(L_done, n + 1)
                self_wait(vec.scalar_tensor_tensor(
                    e, ps[2 + n][:, 0:H * 16].rearrange("p (h c) -> p h c", c=16)[:, :, 0:ncv], DH ** -0.5,
                    strided(biasM[:, 0, k0:k0 + 1], [[T, H], [CMP_STRIDE, ncv]]), ALU.mult, ALU.add), L_free, n + 1)
                link(vec.tensor_reduce(csum[:, n], e, AX.X, ALU.max))
                vec.tensor_tensor(e, e, bcast(csum[:, n], ncv), ALU.subtract).then_inc(cmp_sub, 1)
                dve.wait_ge(cmp_exp, n + 1)
                link(vec.tensor_tensor(e, e, spread(cmaskS[:, n, 0:ncv], H), ALU.mult))
                link(vec.tensor_reduce(csum[:, n], e, AX.X, ALU.add))
                self_wait(vec.tensor_scalar(csum[:, n], csum[:, n], 1e-30, None, ALU.max), cmp_ready, n + 1)

            for n in range(2, UNITS):
                br, i, pr = unit(n)
                w = (i + 1) * P
                e = E[:, n % 2, :, 0:w]
                lg = ps[2 + n % 2][:, :].rearrange("p (a k) -> p a k", a=2)[:, :, 0:w]
                bias = biasM[:, 2 * pr:2 * pr + 2, T - w:T] if br < 2 else spread(causalS[:, T - w:T], 2)
                scale = DH ** -0.5 if br < 2 else QK ** -0.5
                dve.wait_ge(L_done, n + 1)
                dve.wait_ge(T_done, n - 1)
                self_wait(vec.scalar_tensor_tensor(e, lg, scale, bias, ALU.mult, ALU.add), L_free, n + 1)
                vec.tensor_reduce(nmx[:, n - 2], e, AX.X, ALU.max, negate=True).then_inc(max_ready, 1)
                if n in (3, 4):
                    combine(n - 3)
                if n >= 5 and n % 2:
                    combine(2 + (n - 5) // 2)
            combine(13)

            for c in range(KT):
                dve.wait_ge(br_done, c + 1)
                dve.wait_ge(sig_ready, c + 1)
                b = ps[c % 2 + 2]
                t2 = strided(tmp[:, 0:1], [[T, 2], [1, T]])
                self_wait(vec.tensor_tensor(t2, b[:, :].rearrange("p (a t) -> p a t", t=T),
                                            strided(mgT[:, c, 0:1], [[KT * T, 2], [1, T]]), ALU.mult), br_free, c + 1)
                self_wait(vec.tensor_tensor(mergedT[:, c], tmp[:, 0:T], tmp[:, T:2 * T], ALU.add), merged_ready, c + 1)
            norm_h()
            gained_transposes(4, 0, gffn)

            dve.wait_ge(xh_ready, 1)
            vec.tensor_tensor(xl[:, :], xnT[:, :], as_f32(xh[:, :]), ALU.subtract).then_inc(xl_ready, 1)

            for i in range(NT):
                dve.wait_ge(s_ready, 4 * (i + 1))
                for m in range(2 * H):
                    s = S[:, i, m]
                    link(vec.max(topv[:, m, 0:8], s))
                    vec.max_index(topi[:, m, 0:8], topv[:, m, 0:8], s)
                    link(vec.match_replace(s, topv[:, m, 0:8], s, -3e38))
                    link(vec.max(topv[:, m, 8:16], s))
                    vec.max_index(topi[:, m, 8:16], topv[:, m, 8:16], s)
                link(vec.tensor_tensor(cand.rearrange("p h (a b) -> p h a b", b=TOPK), bcast(topv[:, 0:H], TOPK),
                                       topv[:, H:2 * H].unsqueeze(2).to_broadcast([P, H, TOPK, TOPK]), ALU.add))
                link(vec.tensor_copy(topi_f, topi))
                for m in range(H):
                    c = cand[:, m]
                    link(vec.max(best[i][:, m, 0:8], c))
                    vec.max_index(pick[:, m, 0:8], best[i][:, m, 0:8], c)
                    link(vec.match_replace(c, best[i][:, m, 0:8], c, -3e38))
                    link(vec.max(best[i][:, m, 8:16], c))
                    link(vec.max_index(pick[:, m, 8:16], best[i][:, m, 8:16], c))
                link(vec.tensor_copy(gsum, best[i][:, :, 0]))
                vec.tensor_tensor(best[i], best[i], bcast(gsum, TOPK), ALU.subtract).then_inc(best_sub, 1)
                pf = pick.rearrange("p h k -> p (h k)")
                vec.tensor_scalar(pick_a, pf, 4, None, ALU.logical_shift_right)
                link(vec.tensor_scalar(pick_b, pf, TOPK - 1, None, ALU.bitwise_and))
                vec.tensor_copy(pa_f, pick_a)
                link(vec.tensor_copy(pb_f, pick_b))
                for side, pos_f in enumerate((pa_f, pb_f)):
                    link(vec.tensor_tensor(eq, bcast(pos_f, TOPK), spread(iota16S, H * TOPK), ALU.is_equal))
                    eq4 = eq.rearrange("p (h k) a -> p h k a", h=H)
                    link(vec.tensor_tensor(eq4, eq4, topi_f[:, side * H:(side + 1) * H].unsqueeze(2).to_broadcast(
                        [P, H, TOPK, TOPK]), ALU.mult))
                    link(vec.tensor_reduce(picks[side][:, i], eq, AX.X, ALU.add))
            for i in range(NT):
                dve.wait_ge(best_exp, i + 1)
                link(vec.tensor_reduce(gsum, best[i], AX.X, ALU.add))
                link(vec.reciprocal(gsum, gsum))
                self_wait(vec.tensor_tensor(picks[2][:, i].rearrange("p (h k) -> p h k", h=H), best[i], bcast(gsum, TOPK),
                                            ALU.mult), picks_ready, i + 1)

            bigT = part(big, 0, NK, T).rearrange("p c t -> p t c")
            dve.wait_ge(pT_ready, 1)
            vec.tensor_copy(iotaB[:, :], iotaS)
            link(vec.tensor_copy(gp[0][:, :], gT[:, :]))
            link(vec.tensor_tensor(g_rest[:, :], gT[:, :], gp[0][:, :], ALU.subtract))
            link(vec.tensor_copy(gp[1][:, :], g_rest[:, :]))
            link(vec.tensor_tensor(g_rest2[:, :], g_rest[:, :], gp[1][:, :], ALU.subtract))
            link(vec.tensor_copy(gp[2][:, :], g_rest2[:, :]))

            def spread_picks(it, s, half):
                n = it * UNROLL + s
                tok = ds(n * TB, TB)
                a, b = A[s % 2], part(marks, 0, TB, HALF)
                if not (half == 0 and isinstance(it, int) and it == 0 and s == 0):
                    dve.wait_ge(ab_ready, n + half * STEPS)
                vec.tensor_tensor(a, spread(iotaB[:, :], TB), bcast(i1T[:, tok], NK), ALU.is_equal)
                vec.tensor_tensor(b, spread(iotaB[:, half * HALF:(half + 1) * HALF], TB),
                                  bcast(i2T[:, tok], HALF), ALU.is_equal).then_inc(b_marked, 1)
                dve.wait_ge(b_marked, n + (half * STEPS + 1))
                for m in range(3):
                    last = vec.tensor_tensor(B[s % 2][m], b, bcast(gp[m][:, tok], HALF), ALU.mult)
                last.then_inc(ab_ready, 1)

            def weigh(it, s, half):
                n = it * UNROLL + s
                w = bigT[:, ds(n * TB, TB), half * HALF:(half + 1) * HALF]
                dve.wait_ge(g_done, n + (half * STEPS + 1))
                vec.tensor_tensor(w, ps[2 + s % 2][:, :].rearrange("p (t c) -> p t c", t=TB), w, ALU.mult).then_inc(w_done, 1)

            def rest_of_w(c, s):
                dve.wait_ge(wh_ready, c + 1)
                b = slice(s % 2 * T, (s % 2 + 1) * T)
                vec.tensor_tensor(wl[:, b], big[:, ds(c * T, T)], as_f32(wh[:, b]), ALU.subtract).then_inc(wl_ready, 1)

            dve.wait_ge(gelu_done, HALF)
            spread_picks(0, 0, 0)
            with dve.Fori(0, LOOPS - 1) as it:
                for s in range(UNROLL):
                    spread_picks(it + (s + 1) // UNROLL, (s + 1) % UNROLL, 0)
                    weigh(it, s, 0)
            for s in range(UNROLL):
                if s + 1 < UNROLL:
                    spread_picks(LOOPS - 1, s + 1, 0)
                weigh(LOOPS - 1, s, 0)
            rest_of_w(0, 0)
            rest_of_w(1, 1)
            dve.wait_ge(gelu_done, 2 * HALF)
            spread_picks(0, 0, 1)
            rest_of_w(2, 0)
            rest_of_w(3, 1)
            spread_picks(0, 1, 1)

            def second_half(it, s):
                c = (it * UNROLL + s) * 2
                weigh(it, s, 1)
                rest_of_w(c + 4, 0)
                spread_picks(it + 1, s, 1)
                rest_of_w(c + 5, 1)

            with dve.Fori(0, LOOPS - 1) as it:
                for s in range(UNROLL):
                    second_half(it, s)
            for s in range(UNROLL):
                weigh(LOOPS - 1, s, 1)
            with dve.Fori(HALF // 2, NK // 2) as it:
                for j in range(2):
                    rest_of_w(it * 2 + j, j)

            dve.wait_ge(f_ssq, 4)
            link(vec.tensor_tensor(rstd[:, 0:NT], strided(ssq[:, 0:1], [[2, NT]]), strided(ssq[:, 1:2], [[2, NT]]), ALU.add))
            vec.tensor_scalar(rstd[:, 4:6], rstd[:, 0:NT], 1.0 / D, EPS, ALU.mult, ALU.add).then_inc(f_ms, 1)
            dve.wait_ge(f_root, 1)
            link(vec.reciprocal(rstd[:, 0:NT], ssq[:, 0:NT]))
            dve.wait_ge(gfin_in, 16)
            for q in range(4):
                i, f = divmod(q, 2)
                c = slice(f * 512, (f + 1) * 512)
                vec.scalar_tensor_tensor(ynat[:, i, c], Y_BANKS[q][:, :], rstd[:, i:i + 1], gfin[:, c],
                                         ALU.mult, ALU.mult).then_inc(out_ready, 1)

        @block.tensor
        def _(pe):
            def mm(o, lhsT, rhs, start=True, stop=True, **kw):
                return nc.tensor.matmul(o, lhsT, rhs, start=start, stop=stop, **kw)

            def transpose(o, a):
                return nc.tensor.transpose(o, a, identS[0:a.shape[0], 0:a.shape[0]])

            def transpose_xs(turn, bank):
                pe.wait_ge(const_in, CONSTS * 16)
                for q in range(4):
                    i, f = divmod(q, 2)
                    pe.wait_ge(xs_ready, NT + q + 1 if turn else i + 1)
                    for m in range(4):
                        k = f * 4 + m
                        last = transpose(ps[bank + q][:, m * P:(m + 1) * P], scaled[turn][:, i, k * P:(k + 1) * P])
                    last.then_inc(xT_ps, 1)

            transpose_xs(0, 2)
            pe.wait_ge(t5_in, 32)
            mm(ps[6][0:H, 0:DIST], t5S[:, :], ohS).then_inc(rev_ps, 1)

            def project(o, weight, n=KT, rhs=xnT3, turn=None):
                for k in range(n):
                    if turn is not None and k == 0:
                        pe.wait_ge(xnT_act, 2 * turn + 2)
                    if turn is not None and k == KH:
                        pe.wait_ge(xnT_dve, 2 * turn + 2)
                    last = mm(o, weight(k), rhs[:, k], start=k == 0, stop=k == n - 1)
                return last

            def job(n, half=None):
                if n >= 2 and half != 1:
                    wait_job_evacuated(pe, n - 2)
                b = ps[n % 2]
                if n in (J_Q0, J_Q1):
                    pe.wait_ge(win_in[n], 16)
                    for j in range(2):
                        r = 2 * n + j
                        last = project(b[:, j * T:(j + 1) * T], lambda k: win[:, k, r * P:(r + 1) * P],
                                       turn=0 if r == 0 else None)
                elif n == J_K:
                    pe.wait_ge(win_in[2], 16)
                    for j in range(2):
                        c = K0 + j * P
                        last = project(b[:, j * T:(j + 1) * T], lambda k: win[:, k, c:c + P])
                elif n == J_CK:
                    for kv in range(2):
                        c = CK0 + kv * P
                        last = project(b[:, kv * T:(kv + 1) * T], lambda k: win[:, k, c:c + P])
                elif n == J_V:
                    for i in range(NT):
                        for k in range(KT):
                            last = mm(b[:, i * T:(i + 1) * T], xnT3[:, k, i * P:(i + 1) * P], win[:, k, V0:REST0],
                                      start=k == 0, stop=k == KT - 1)
                elif n in (J_R0, J_R1):
                    pe.wait_ge(win_in[3], 16)
                    i = n - J_R0
                    for k in range(KT):
                        last = mm(b[:, 0:REST], xnT3[:, k, i * P:(i + 1) * P], win[:, k, REST0:CK0],
                                  start=k == 0, stop=k == KT - 1)
                elif n == J_C:
                    pe.wait_ge(cn_ready, 1)
                    for k in range(2):
                        for i in range(NT):
                            last = transpose(b[:, k * T + i * P:k * T + (i + 1) * P],
                                             rest[:, i, CQ0 + k * P:CQ0 + (k + 1) * P])
                elif n == J_CR:
                    pe.wait_ge(kr_ready, 1)
                    for i in range(NT):
                        transpose(b[:, i * P:(i + 1) * P], rest[:, i, CKV0:KR0])
                        last = transpose(b[0:QK, T + i * P:T + (i + 1) * P], kpad[:, i])
                elif n < J_VM:
                    pe.wait_ge(wu_in, 32)
                    wait_job_evacuated(pe, J_CR)
                    for j in range(2):
                        hd = 2 * (n - J_KN) + j
                        last = mm(b[0:NOPE, j * T:(j + 1) * T], wukv[:, hd * 2 * DH:hd * 2 * DH + NOPE], cT[:, 2])
                elif n < J_QN:
                    i = n - J_VM
                    last = mm(b[:, :].rearrange("p (h d) -> p h d", d=DH), cT[:, 2, i * P:(i + 1) * P],
                              wukv.rearrange("p (h c) -> p h c", c=2 * DH)[:, :, NOPE:2 * DH])
                elif n < J_QT:
                    i, f = divmod(n - J_QN, 2)
                    for k in range(2):
                        last = mm(b[:, 0:384], cT[:, k, i * P:(i + 1) * P], wuq[:, k, f * 384:(f + 1) * 384],
                                  start=k == 0, stop=k == 1)
                elif n < J_MG:
                    pe.wait_ge(rope_ready, NT)
                    i, quad = divmod(n - J_QT, 2)
                    for j in range(4):
                        hd = quad * 4 + j
                        last = transpose(b[0:QK, j * P:(j + 1) * P], qn[:, i, hd * QK:(hd + 1) * QK])
                else:
                    c = n - J_MG
                    pe.wait_ge(merge_in[c % 2], 16 * (c // 2 + 1))
                    last = project(b[:, half * T:(half + 1) * T], lambda k: mslot[c % 2][:, k, half * P:(half + 1) * P])
                if half != 0:
                    last.then_inc(job_done, 1)

            for n in range(J_KN):
                job(n)
            pe.wait_ge(w1_in, 32)
            pe.wait_ge(job_dve, 1)
            for kv in range(2):
                for l in range(LP):
                    last = mm(ps[6][0:G * NC, kv * CMP_HID:(kv + 1) * CMP_HID], blkT[:, kv, l], w1[:, kv, l],
                              start=l == 0, stop=l == LP - 1)
            last.then_inc(hid_ps, 1)
            for n in range(J_KN, J_VM):
                job(n)
            pe.wait_ge(hid_act, 1)
            for m in range(4):
                last = transpose(ps[7][:, m * 32:m * 32 + G * NC], hidS[:, m * P:(m + 1) * P])
            last.then_inc(hT_ps, 1)
            for n in range(J_VM, J_QT):
                job(n)
            pe.wait_ge(hid_ready, 1)
            for hid in range(2):
                mm(ps[6][:, 0:G * NC], w2kS[:, hid], hTk[:, hid],
                   start=hid == 0, stop=hid == 1)
            for hid in range(2):
                last = mm(ps[6][0:H * NC, 64:64 + DH], hTv[:, hid], w2vS[:, hid], start=hid == 0, stop=hid == 1)
            last.then_inc(kc_ps, 1)
            pe.wait_ge(kc_ready, 1)

            def logits(n):
                if n >= 2:
                    pe.wait_ge(L_free, n - 1)
                b = ps[2 + n % 2]
                if n < 2:
                    for hd in range(H):
                        g, r = divmod(hd, R)
                        rows = slice(g * DH, (g + 1) * DH)
                        last = mm(b[:, hd * 16:hd * 16 + NC], qT[rows, r, n * P:(n + 1) * P], kcT[rows, :])
                        if hd == R - 1:
                            last.then_inc(half_logits, 1)
                            pe.wait_ge(half_logits, n + 1)
                else:
                    br, i, pr = unit(n)
                    w = (i + 1) * P
                    for j in range(2):
                        hd = 2 * pr + j
                        o = b[:, j * T:j * T + w]
                        if br < 2:
                            g, r = divmod(hd, R)
                            rows = slice(g * DH, (g + 1) * DH)
                            last = mm(o, qT[rows, r, i * P:(i + 1) * P], kT[rows, br, 0:w])
                        else:
                            last = mm(o, mqT[0:QK, hd, i * P:(i + 1) * P], mkT[0:QK, hd, 0:w])
                last.then_inc(L_done, 1)

            def transpose_outputs(q):
                for m in range(4):
                    last = transpose(ps[q][:, m * P:(m + 1) * P], onat[q // 2][:, q % 2, m * P:(m + 1) * P])
                last.then_inc(oT_ps, 1)

            logits(0)
            logits(1)
            for n in range(UNITS):
                if n < 2:
                    pe.wait_ge(cmp_ready, n + 1)
                    last = transpose(ps[4 + n][0:H * NC, 0:P], Ec[:, n])
                else:
                    br, i, pr = unit(n)
                    pe.wait_ge(E_ready, n - 1)
                    pe.wait_ge(eT_ready, n - 1)
                    for j in range(2):
                        for k in range(i + 1):
                            c = (j * (i + 1) + k) * P
                            last = transpose(ps[4 + n % 2][:, c:c + P], E[:, n % 2, j, k * P:(k + 1) * P])
                last.then_inc(T_done, 1)
                if n + 2 < UNITS:
                    if unit(n + 2)[0] == 2:
                        wait_job_evacuated(pe, J_QT + 3)
                    logits(n + 2)
                j, half = fill_job(n)
                if j is not None:
                    job(j, half)
                if n == 22:
                    pe.wait_ge(onat_ready, 8)
                    wait_job_evacuated(pe, JOBS - 1)
                if n in (22, 23):
                    transpose_outputs(n - 22)
                gr = group(n)
                first = n < 2 or n % 2 == 0
                if first and gr >= 2:
                    pe.wait_ge(O_free, gr - 1)
                pe.wait_ge(eT_ready, n + 1)
                b = ps[6 + gr % 2]
                if n < 2:
                    pe.wait_ge(vb_ready, 1)
                    last = mm(b[:, :], eT[n % 2][0:H * NC, 0:P], VB[0:H * NC, :])
                else:
                    for j in range(2):
                        hd = 2 * pr + j
                        for k in range(i + 1):
                            c = (j * (i + 1) + k) * P
                            val = Vn[:, k, br * P:(br + 1) * P] if br < 2 else Vm[:, k, hd // 2 * P:(hd // 2 + 1) * P]
                            last = mm(b[:, hd % 4 * P:(hd % 4 + 1) * P], eT[n % 2][:, c:c + P], val, start=k == 0, stop=k == i)
                last.then_inc(V_done, 1)

            for q in (2, 3):
                pe.wait_ge(O_free, 12 if q == 2 else 14)
                transpose_outputs(q)
            for q in range(4):
                i, f = divmod(q, 2)
                mm(Y_BANKS[q][:, :], identS, x3[:, i, f * 512:(f + 1) * 512], stop=False, skip_group_check=True)
            pe.wait_ge(oT_ready, 4)
            pe.wait_ge(wb_in, 32)
            for c in range(KT):
                if c >= 2:
                    pe.wait_ge(br_free, c - 1)
                for m in range(2):
                    last = project(ps[c % 2 + 2][:, m * T:(m + 1) * T], lambda k: wb[:, m, k, c * P:(c + 1) * P], 4,
                                   oT[:, 4 * m:4 * m + 4])
                last.then_inc(br_done, 1)
            pe.wait_ge(wo_in, 16)
            for q in range(4):
                i, f = divmod(q, 2)
                for k in range(KT):
                    if q == 0:
                        pe.wait_ge(merged_ready, k + 1)
                    last = mm(Y_BANKS[q][:, :], mergedT[:, k, i * P:(i + 1) * P], wo[:, k, f * 512:(f + 1) * 512],
                              start=False, stop=False, skip_group_check=True)
                last.then_inc(h_ps, 1)

            transpose_xs(1, 0)
            pe.wait_ge(wq_in, 16)
            for j in range(4):
                for m in range(2):
                    hd = 2 * j + m
                    last = project(ps[j][:, m * T:(m + 1) * T], lambda k: wq[:, k, hd * P:(hd + 1) * P],
                                   turn=1 if hd == 0 else None)
                last.then_inc(qp_done, 1)
            pe.wait_ge(keys_in, 16)
            for q in range(2 * 4):
                i, f = divmod(q, 4)
                if q == 0:
                    pe.wait_ge(qp_ready, 4)
                if q >= 4:
                    pe.wait_ge(s_ready, q - 3)
                for m in range(4):
                    side, hd = divmod(4 * f + m, H)
                    rows = slice(side * DH, (side + 1) * DH)
                    last = mm(ps[q % 4][:, m * NK:(m + 1) * NK], qpT[rows, hd, i * P:(i + 1) * P], keysT[rows, hd])
                last.then_inc(s_done, 1)

            def expert_inputs(it, s):
                c = it * RING + s
                if not (isinstance(it, int) and it == 0 and s < 2):
                    pe.wait_ge(gelu_done, c - 1)
                for k in range(KT):
                    if k % KH == 0:
                        pe.wait_ge(lo_ready, c * 2 + (k // KH + 1))
                    w, m = s % 2 * D + k * P, slice(k * T, (k + 1) * T)
                    o = ps[s % 2][:, 0:T]
                    mm(o, hi[:, w:w + P], xh[:, m], start=k == 0, stop=False)
                    mm(o, hi[:, w:w + P], xl[:, m], start=False, stop=False)
                    last = mm(o, lo[:, w:w + P], xh[:, m], start=False, stop=k == KT - 1)
                    if k % KH == KH - 1:
                        last.then_inc(half_used, 1)

            def pick_weights(it, s, half):
                n = it * UNROLL + s
                pe.wait_ge(ab_ready, n + (half * STEPS + 1))
                if not (half == 0 and isinstance(it, int) and it == 0):
                    pe.wait_ge(w_done, n + (half * STEPS - 1))
                for t in range(TB):
                    o = ps[2 + s % 2][:, t * HALF:(t + 1) * HALF]
                    for m in range(3):
                        last = mm(o, A[s % 2][:, t], B[s % 2][m][:, t], start=m == 0, stop=m == 2)
                last.then_inc(g_done, 1)

            def expert_outputs(it, s):
                c = it * RING + s
                pe.wait_ge(wl_ready, c + 1)
                for f in range(2):
                    pe.wait_ge(lo_ready, c * 2 + (2 * NK + f + 1))
                    vs = slice(s % 2 * D + f * 512, s % 2 * D + (f + 1) * 512)
                    for i in range(NT):
                        o = Y_BANKS[2 * i + f][:, :]
                        tok = slice(s % 2 * T + i * P, s % 2 * T + (i + 1) * P)
                        for w, val in ((wh, hi), (wh, lo), (wl, hi)):
                            last = mm(o, w[:, tok], val[:, vs], start=False, stop=False, skip_group_check=True)
                    last.then_inc(half_used, 1)

            pe.wait_ge(s_ready, 8)
            pe.wait_ge(xl_ready, 1)
            for s in range(RING):
                expert_inputs(0, s)
            with pe.Fori(1, LOOPS) as it:
                for s in range(RING):
                    expert_inputs(it, s)
            pe.wait_ge(picks_ready, NT)
            for s in range(3):
                for i in range(NT):
                    c = (s % 2) * T + i * P
                    last = transpose(ps[2 + s // 2][:, c:c + P], picks[s][:, i])
            last.then_inc(pT_done, 1)
            for s in range(RING):
                expert_inputs(LOOPS, s)
                if s == 0:
                    pe.wait_ge(pT_ready, 1)
                if s >= 2:
                    pick_weights(0, s - 2, 0)
            with pe.Fori(1, LOOPS - 1) as it:
                for s in range(RING):
                    expert_inputs(it + LOOPS, s)
                    if s % 2:
                        pick_weights(it, s // 2, 0)
            for s in range(RING):
                expert_inputs(2 * LOOPS - 1, s)
                if s in (1, 2):
                    pick_weights(LOOPS - 1, s - 1, 0)
            with pe.Fori(0, LOOPS - 1) as it:
                for s in range(RING):
                    expert_outputs(it, s)
                    if s % 2:
                        pick_weights(it, s // 2, 1)
            for s in range(RING):
                expert_outputs(LOOPS - 1, s)
                if s in (1, 2):
                    pick_weights(LOOPS - 1, s - 1, 1)
            with pe.Fori(LOOPS, 2 * LOOPS) as it:
                for s in range(RING):
                    expert_outputs(it, s)


def constants():
    f = np.float32
    dist = (T - 1) - np.arange(DIST)
    n = np.maximum(dist, 0)
    half = BUCKETS // 2
    ratio = np.maximum(n, half).astype(f) / f(half)
    large = half + (np.log(ratio) / f(math.log(MAX_DIST / half)) * f(BUCKETS - half)).astype(np.int32)
    bucket = np.where(n < half, n, np.minimum(large, BUCKETS - 1))
    bucket = np.where(dist < 0, BUCKETS, bucket)
    one_hot = (np.arange(BUCKETS + 1)[:, None] == bucket[None, :]).astype(f)
    inv = f(10000.0) ** (-np.arange(0, ROPE, 2, dtype=f) / f(ROPE))
    ang = (np.arange(T, dtype=f)[:, None] * inv[None, :]).astype(f)
    tiles = lambda a: np.ascontiguousarray(a.reshape(NT, P, -1).transpose(1, 0, 2)).astype(f)
    keys, p = np.arange(T), np.arange(P)[:, None]
    causal = np.where(P + p - keys[None, :] >= 0, f(0), f(MASKED)).astype(f)
    ends = np.arange(NC) * CMP_STRIDE + CMP_LEN - 1
    return {
        "ident": np.eye(P, dtype=f),
        "one_hot": one_hot,
        "cos": tiles(np.cos(ang)), "sin": tiles(np.sin(ang)),
        "causal": causal,
        "cmp_mask": tiles((np.arange(T)[:, None] >= ends[None, :]).astype(f)),
        "head_mask": np.concatenate([np.repeat(np.eye(H, dtype=f), NC, axis=0), np.zeros((P - H * NC, H), f)]),
        "iota": np.tile(np.arange(NK, dtype=f), (P, 1)),
        "iota16": np.tile(np.arange(TOPK, dtype=f), (P, 1)),
    }


def kernel(**inputs):
    import concourse.bacc as bacc
    from concourse.bass_utils import run_bass_kernel_spmd

    a = {k: np.asarray(val) for k, val in inputs.items()}
    cols = lambda g: g.reshape(-1, P).T
    pos = lambda g: np.concatenate([g.reshape(LP, 2, DH).transpose(2, 1, 0)] * G)
    w = a["w_in"][0]
    kv = w[:, Q_COLS:Q_COLS + 6 * P].reshape(D, 6, G, DH)
    end = Q_COLS + 6 * P
    w_in = np.concatenate([
        w[:, :Q_COLS].reshape(D, G, R, DH).transpose(0, 2, 1, 3).reshape(D, Q_COLS),
        kv[:, 2].reshape(D, P), kv[:, 4].reshape(D, P), kv[:, 3].reshape(D, P), kv[:, 5].reshape(D, P),
        w[:, end:end + REST], kv[:, 0].reshape(D, P), kv[:, 1].reshape(D, P), w[:, end + REST:]], axis=1)
    w2k = a["nsa_cmp_k_w2"][0]
    c = constants()
    rows = lambda z: z.reshape(2, P, -1).transpose(1, 0, 2)
    pack = lambda *z: np.concatenate([t.reshape(P, -1) for t in z], axis=1)
    arrays = {
        "x": a["x"].reshape(T, D),
        "g_fin": a["ln_final_g"],
        "w_in": w_in,
        "w1k": a["nsa_cmp_k_w1"][0], "w1v": a["nsa_cmp_v_w1"][0],
        "w_uq": a["mla_w_uq"][0], "w_ukv": a["mla_w_ukv"][0],
        "w_bn": a["w_branch_nsa"][0], "w_bm": a["w_branch_mla"][0], "w_out": a["w_out"][0],
        "w_query": a["peer_w_query"][0],
        "keys_t": a["peer_sub_keys"][0].transpose(1, 3, 0, 2).reshape(P, H, NK),
        "u_t": a["peer_u"][0].reshape(NK, NK, KT, P).transpose(1, 3, 2, 0).reshape(NK, P, KT * NK),
        "v_t": a["peer_v"][0].reshape(NK, NK, D).transpose(1, 0, 2),
        "t5": np.concatenate([a["t5_bias"], np.full((1, H), MASKED, np.float32)]),
        "one_hot": c["one_hot"],
        "keep_pack": pack(c["ident"], c["iota"], c["iota16"], cols(a["ln_mix_g"][0]), cols(a["ln_ffn_g"][0])),
        "early_pack": pack(pos(a["nsa_cmp_pos_k"][0]), pos(a["nsa_cmp_pos_v"][0]), cols(a["mla_q_norm_g"][0]),
                           cols(a["mla_kv_norm_g"][0]), c["cos"], c["sin"], c["cmp_mask"], c["head_mask"],
                           rows(np.concatenate([w2k, w2k], axis=1)), rows(a["nsa_cmp_v_w2"][0]), c["causal"]),
    }
    arrays = {k: np.ascontiguousarray(val) for k, val in arrays.items()}
    nc = bacc.Bacc("TRN2", target_bir_lowering=False, num_devices=1)
    aps = {k: nc.dram_tensor(k, val.shape, mybir.dt.from_np(val.dtype), kind="ExternalInput").ap()
           for k, val in arrays.items()}
    out = nc.dram_tensor("out", (T, D), mybir.dt.float32, kind="ExternalOutput").ap()
    build(nc, out=out, **aps)
    r = run_bass_kernel_spmd(nc, [arrays], core_ids=[0])
    return r.results[0]["out"].reshape(1, T, D)
```
